# Optimizing a Trainium2 kernel written in Bass

```python
import math
import jax
import jax.numpy as jnp
from jax import lax
import numpy as np

D_MODEL = 1024
BATCH = 1
SEQ = 1024
DEPTH = 1
DEC_BATCH = 8
DEC_SEQ = 1
PAST_LEN = 4096
PAGE_SIZE = 128

N_GROUPS = 4
W_GRP = D_MODEL // N_GROUPS
HEAD_DIM = 64
H_A = W_GRP // HEAD_DIM
H_C = W_GRP // HEAD_DIM
H_M = 4
HEAD_DIM_M = W_GRP // H_M
G_B = 4
GB_DIM = W_GRP // G_B
CHUNK = 128
QBLK = 128
C_PAIRS = ((128, 1), (512, 4), (2048, 16))
C_WIN = 2048
N_MEM = 256
N_BUCKETS = 32
MAX_DIST = 2048
CONV_W = 3
D_FF = ((8 * D_MODEL // 3 + 127) // 128) * 128
FORGET_BIAS_MEAN = 2.0
EPS = 1e-6
NEG = -1e30
PROJ_WIDTHS = (W_GRP, W_GRP, W_GRP, H_A, W_GRP, W_GRP, W_GRP, W_GRP, W_GRP, W_GRP)
D_IN = sum(PROJ_WIDTHS)

kernel_name = 'hybrid_fox_sgu_dilated_mem_decoder_step'

def rmsnorm(x, g):
    xf = x.astype(jnp.float32)
    y = xf * lax.rsqrt(jnp.mean(xf * xf, axis=-1, keepdims=True) + EPS)
    return (y * g.astype(jnp.float32)).astype(x.dtype)

def split_heads(t, n_heads):
    return t.reshape(t.shape[:-1] + (n_heads, t.shape[-1] // n_heads))

def rel_bucket(dist):
    max_exact = N_BUCKETS // 2
    df = jnp.maximum(dist, 1).astype(jnp.float32)
    large = max_exact + (jnp.log(df / max_exact) / math.log(MAX_DIST / max_exact)
                         * (N_BUCKETS - max_exact)).astype(jnp.int32)
    large = jnp.minimum(large, N_BUCKETS - 1)
    return jnp.where(dist < max_exact, dist, large)

def branch_bias(rel_bias, window, dil):
    dist = jnp.arange(window // dil + 1, dtype=jnp.int32) * dil
    return rel_bias[rel_bucket(dist)].astype(jnp.float32).T

def project(x, g, w_in, b_f, qk_g):
    z = rmsnorm(x, g) @ w_in
    offs = np.cumsum(PROJ_WIDTHS)[:-1].tolist()
    qa, ka, va, fa, bu, bv, qc, kc, vc, qm = jnp.split(z, offs, axis=-1)
    qa = rmsnorm(split_heads(qa, H_A), qk_g[0])
    ka = rmsnorm(split_heads(ka, H_A), qk_g[1])
    va = split_heads(va, H_A)
    logf = jax.nn.log_sigmoid(fa.astype(jnp.float32) + b_f.astype(jnp.float32))
    bu = jax.nn.gelu(bu)
    bv = jax.nn.gelu(bv)
    qc = rmsnorm(split_heads(qc, H_C), qk_g[2])
    kc = rmsnorm(split_heads(kc, H_C), qk_g[3])
    vc = split_heads(vc, H_C)
    qm = rmsnorm(split_heads(qm, H_M), qk_g[4])
    return qa, ka, va, logf, bu, bv, qc, kc, vc, qm

def memory_kv(mem, g, w, qk_gk):
    z = rmsnorm(mem, g) @ w
    mk, mv = jnp.split(z, 2, axis=-1)
    return rmsnorm(split_heads(mk, H_M), qk_gk), split_heads(mv, H_M)

def fox_prompt(q, k, v, logf):
    b, s, h, e = q.shape
    nb = s // QBLK
    scale = 1.0 / math.sqrt(e)
    c = jnp.cumsum(logf, axis=1)
    ct = jnp.transpose(c, (0, 2, 1))[:, :, None, :]
    kpos = jnp.arange(s)

    def block(args):
        qb, cb, start = args
        sc = jnp.einsum('bqhe,bkhe->bhqk', qb, k).astype(jnp.float32) * scale
        sc = sc + jnp.transpose(cb, (0, 2, 1))[..., None] - ct
        qpos = start + jnp.arange(QBLK)
        sc = jnp.where(kpos[None, :] <= qpos[:, None], sc, NEG)
        p = jax.nn.softmax(sc, axis=-1)
        return jnp.einsum('bhqk,bkhe->bqhe', p.astype(v.dtype), v)

    qs = jnp.moveaxis(q.reshape(b, nb, QBLK, h, e), 1, 0)
    cs = jnp.moveaxis(c.reshape(b, nb, QBLK, h), 1, 0)
    starts = jnp.arange(nb, dtype=jnp.int32) * QBLK
    o = lax.map(block, (qs, cs, starts))
    return jnp.moveaxis(o, 0, 1).reshape(b, s, h * e)

def fox_sample(q, k_new, v_new, logf_new, pool_k, pool_v, pool_logf, page_table):
    b, t, h, e = q.shape
    past = page_table.shape[1] * PAGE_SIZE
    scale = 1.0 / math.sqrt(e)
    k_all = jnp.concatenate([pool_k[page_table].reshape(b, past, h, e).astype(k_new.dtype), k_new], axis=1)
    v_all = jnp.concatenate([pool_v[page_table].reshape(b, past, h, e).astype(v_new.dtype), v_new], axis=1)
    lf_all = jnp.concatenate([pool_logf[page_table].reshape(b, past, h).astype(jnp.float32), logf_new], axis=1)
    c = jnp.cumsum(lf_all, axis=1)
    cq = jnp.transpose(c[:, past:], (0, 2, 1))[..., None]
    ck = jnp.transpose(c, (0, 2, 1))[:, :, None, :]
    sc = jnp.einsum('bthe,bshe->bhts', q, k_all).astype(jnp.float32) * scale + cq - ck
    qpos = past + jnp.arange(t)
    kpos = jnp.arange(past + t)
    sc = jnp.where(kpos[None, :] <= qpos[:, None], sc, NEG)
    p = jax.nn.softmax(sc, axis=-1)
    return jnp.einsum('bhts,bshe->bthe', p.astype(v_all.dtype), v_all).reshape(b, t, h * e)

def sgu_prompt(u, v, w_s, b_s):
    b, s, _ = u.shape
    n = s // CHUNK
    w = jnp.where(jnp.tril(jnp.ones((CHUNK, CHUNK), dtype=bool)), w_s, 0.0)
    vg = v.reshape(b, n, CHUNK, G_B, GB_DIM)
    sv = jnp.einsum('gqk,bnkgc->bnqgc', w, vg) + b_s.T[None, None, :, :, None]
    return u * sv.reshape(b, s, W_GRP)

def sgu_sample(u, v, w_s, b_s):
    b, t, _ = u.shape
    w = jnp.where(jnp.tril(jnp.ones((CHUNK, CHUNK), dtype=bool)), w_s, 0.0)[:, :t, :t]
    vg = v.reshape(b, t, G_B, GB_DIM)
    sv = jnp.einsum('gqk,bkgc->bqgc', w, vg) + b_s[:, :t].T[None, :, :, None]
    return u * sv.reshape(b, t, W_GRP)

def dilated_branch_prompt(q, k, v, bias_j, dil):
    b, s, h, e = q.shape
    n_keys = bias_j.shape[1]
    sub_len = s // dil
    nb = -(-sub_len // QBLK)
    lp = nb * QBLK
    scale = 1.0 / math.sqrt(e)

    def to_sub(t):
        t = jnp.swapaxes(t.reshape(b, sub_len, dil, h, e), 1, 2)
        t = jnp.pad(t, ((0, 0), (0, 0), (0, lp - sub_len), (0, 0), (0, 0)))
        return t.reshape(b, dil, nb, QBLK, h, e)

    def with_prev(t):
        prev = jnp.pad(t[:, :, :-1], ((0, 0), (0, 0), (1, 0), (0, 0), (0, 0), (0, 0)))
        return jnp.concatenate([prev, t], axis=3)

    qb = to_sub(q)
    kk = with_prev(to_sub(k))
    vv = with_prev(to_sub(v))
    sc = jnp.einsum('bdnqhe,bdnkhe->bdnhqk', qb, kk).astype(jnp.float32) * scale
    rel = jnp.arange(QBLK)[:, None] + QBLK - jnp.arange(2 * QBLK)[None, :]
    band = (rel >= 0) & (rel < n_keys)
    in_cur = jnp.arange(2 * QBLK) >= QBLK
    valid = band[None] & ((jnp.arange(nb)[:, None, None] > 0) | in_cur[None, None, :])
    sc = sc + bias_j[:, jnp.clip(rel, 0, n_keys - 1)][None, None, None]
    sc = jnp.where(valid[None, None, :, None], sc, NEG)
    m = jnp.max(sc, axis=-1)
    p = jnp.exp(sc - m[..., None])
    den = jnp.sum(p, axis=-1)
    o = jnp.einsum('bdnhqk,bdnkhe->bdnqhe', p.astype(v.dtype), vv)

    def back(t):
        t = t.reshape((b, dil, lp) + t.shape[4:])[:, :, :sub_len]
        t = jnp.swapaxes(t, 1, 2)
        return t.reshape((b, s) + t.shape[3:])

    return back(jnp.swapaxes(m, 3, 4)), back(jnp.swapaxes(den, 3, 4)), back(o)

def dilated_branch_sample(q, ext_k, ext_v, bias_j, dil, cw):
    b, t, h, e = q.shape
    n_keys = bias_j.shape[1]
    scale = 1.0 / math.sqrt(e)
    rows = cw + jnp.arange(t)[:, None] - jnp.arange(n_keys)[None, :] * dil
    valid = rows >= 0
    rc = jnp.maximum(rows, 0)
    kg = ext_k[:, rc]
    vg = ext_v[:, rc]
    sc = jnp.einsum('bthe,btjhe->bhtj', q, kg).astype(jnp.float32) * scale + bias_j[None, :, None, :]
    sc = jnp.where(valid[None, None], sc, NEG)
    m = jnp.max(sc, axis=-1)
    p = jnp.exp(sc - m[..., None])
    den = jnp.sum(p, axis=-1)
    o = jnp.einsum('bhtj,btjhe->bthe', p.astype(vg.dtype), vg)
    return jnp.swapaxes(m, 1, 2), jnp.swapaxes(den, 1, 2), o

def combine_branches(parts, dtype):
    ms = jnp.stack([p[0] for p in parts])
    dens = jnp.stack([p[1] for p in parts])
    outs = jnp.stack([p[2].astype(jnp.float32) for p in parts])
    wts = jnp.exp(ms - jnp.max(ms, axis=0))
    num = jnp.sum(wts[..., None] * outs, axis=0)
    out = num / jnp.sum(wts * dens, axis=0)[..., None]
    return out.reshape(out.shape[:2] + (-1,)).astype(dtype)

def dilated_prompt(q, k, v, rel_bias):
    parts = [dilated_branch_prompt(q, k, v, branch_bias(rel_bias, w, d), d) for (w, d) in C_PAIRS]
    return combine_branches(parts, q.dtype)

def dilated_sample(q, ext_k, ext_v, rel_bias, cw):
    parts = [dilated_branch_sample(q, ext_k, ext_v, branch_bias(rel_bias, w, d), d, cw) for (w, d) in C_PAIRS]
    return combine_branches(parts, q.dtype)

def mem_attend(q, mk, mv):
    b, t, h, e = q.shape
    sc = jnp.einsum('bthe,bmhe->bhtm', q, mk).astype(jnp.float32) * (1.0 / math.sqrt(e))
    p = jax.nn.softmax(sc, axis=-1)
    return jnp.einsum('bhtm,bmhe->bthe', p.astype(mv.dtype), mv).reshape(b, t, h * e)

def merge_groups(outs, g, w_out):
    o = jnp.concatenate([t.reshape(t.shape[:2] + (W_GRP,)) for t in outs], axis=-1)
    o = rmsnorm(split_heads(o, N_GROUPS), g.reshape(N_GROUPS, W_GRP))
    return o.reshape(o.shape[:2] + (N_GROUPS * W_GRP,)) @ w_out

def conv_ffn(x, g, w_up, conv_w, conv_b, w_down, buf):
    t = x.shape[1]
    up = rmsnorm(x, g) @ w_up
    ext = jnp.concatenate([buf.astype(up.dtype), up], axis=1)
    conv = conv_b + sum(ext[:, i:i + t] * conv_w[i] for i in range(CONV_W))
    a, gate = jnp.split(conv, 2, axis=-1)
    y = (jax.nn.silu(gate) * a) @ w_down
    return y, ext[:, t:]

def setup_inputs(seed: int = 0) -> dict:
    key = jax.random.key(seed)
    ks = iter(jax.random.split(key, 40))

    def nrm(shape, scale=1.0):
        return scale * jax.random.normal(next(ks), shape, jnp.float32)

    n_pages = PAST_LEN // PAGE_SIZE
    n_used = DEC_BATCH * n_pages
    n_pool = n_used + (n_used + 3) // 4
    cw = min(C_WIN, PAST_LEN)
    page_table = jax.random.permutation(next(ks), n_pool)[:n_used].reshape(DEC_BATCH, n_pages).astype(jnp.int32)
    return {
        'x_prompt': nrm((BATCH, SEQ, D_MODEL)),
        'x_sample': nrm((DEC_BATCH, DEC_SEQ, D_MODEL)),
        'mem_prompt': nrm((BATCH, N_MEM, D_MODEL)),
        'cache_a_k': nrm((DEPTH, n_pool, PAGE_SIZE, H_A, HEAD_DIM)),
        'cache_a_v': nrm((DEPTH, n_pool, PAGE_SIZE, H_A, HEAD_DIM)),
        'cache_a_logf': jax.nn.log_sigmoid(FORGET_BIAS_MEAN + nrm((DEPTH, n_pool, PAGE_SIZE, H_A))),
        'cache_c_k': nrm((DEPTH, DEC_BATCH, cw, H_C, HEAD_DIM)),
        'cache_c_v': nrm((DEPTH, DEC_BATCH, cw, H_C, HEAD_DIM)),
        'cache_mem_k': nrm((DEPTH, DEC_BATCH, N_MEM, H_M, HEAD_DIM_M)),
        'cache_mem_v': nrm((DEPTH, DEC_BATCH, N_MEM, H_M, HEAD_DIM_M)),
        'state_ffn_conv': nrm((DEPTH, DEC_BATCH, CONV_W - 1, 2 * D_FF)),
        'page_table': page_table,
        'norm_mix': 1.0 + nrm((DEPTH, D_MODEL), 0.02),
        'w_in': nrm((DEPTH, D_MODEL, D_IN), D_MODEL ** -0.5),
        'b_forget': FORGET_BIAS_MEAN + nrm((DEPTH, H_A), 0.5),
        'qk_gain': 1.0 + nrm((DEPTH, 6, HEAD_DIM), 0.02),
        'w_spatial': nrm((DEPTH, G_B, CHUNK, CHUNK), CHUNK ** -0.5),
        'b_spatial': 1.0 + nrm((DEPTH, G_B, CHUNK), 0.1),
        'rel_bias': nrm((N_BUCKETS, H_C), 0.1),
        'norm_mem': 1.0 + nrm((DEPTH, D_MODEL), 0.02),
        'w_mem_kv': nrm((DEPTH, D_MODEL, 2 * W_GRP), D_MODEL ** -0.5),
        'norm_out': 1.0 + nrm((DEPTH, D_MODEL), 0.02),
        'w_out': nrm((DEPTH, D_MODEL, D_MODEL), D_MODEL ** -0.5),
        'norm_ffn': 1.0 + nrm((DEPTH, D_MODEL), 0.02),
        'w_up': nrm((DEPTH, D_MODEL, 2 * D_FF), D_MODEL ** -0.5),
        'conv_w': nrm((DEPTH, CONV_W, 2 * D_FF), CONV_W ** -0.5),
        'conv_b': nrm((DEPTH, 2 * D_FF), 0.02),
        'w_down': nrm((DEPTH, D_FF, D_MODEL), D_FF ** -0.5),
    }

def reference(x_prompt, x_sample, mem_prompt, cache_a_k, cache_a_v, cache_a_logf, cache_c_k, cache_c_v,
              cache_mem_k, cache_mem_v, state_ffn_conv, page_table, norm_mix, w_in, b_forget, qk_gain,
              w_spatial, b_spatial, rel_bias, norm_mem, w_mem_kv, norm_out, w_out, norm_ffn, w_up,
              conv_w, conv_b, w_down):
    cw_p = min(C_WIN, x_prompt.shape[1])
    cw_s = cache_c_k.shape[2]
    pa_k, pa_v, pa_lf, pc_k, pc_v, pm_k, pm_v, pf = [], [], [], [], [], [], [], []
    sa_k, sa_v, sa_lf, sc_k, sc_v, sb_v, sf = [], [], [], [], [], [], []
    xp = x_prompt
    xs = x_sample
    for l in range(DEPTH):
        qa, ka, va, lfa, bu, bv, qc, kc, vc, qm = project(xp, norm_mix[l], w_in[l], b_forget[l], qk_gain[l])
        mk, mv = memory_kv(mem_prompt, norm_mem[l], w_mem_kv[l], qk_gain[l, 5])
        outs = (fox_prompt(qa, ka, va, lfa),
                sgu_prompt(bu, bv, w_spatial[l], b_spatial[l]),
                dilated_prompt(qc, kc, vc, rel_bias),
                mem_attend(qm, mk, mv))
        xp = xp + merge_groups(outs, norm_out[l], w_out[l]).astype(xp.dtype)
        f, conv_state = conv_ffn(xp, norm_ffn[l], w_up[l], conv_w[l], conv_b[l], w_down[l],
                                 jnp.zeros((xp.shape[0], CONV_W - 1, 2 * D_FF), xp.dtype))
        xp = xp + f.astype(xp.dtype)
        pa_k.append(ka)
        pa_v.append(va)
        pa_lf.append(lfa)
        pc_k.append(kc[:, -cw_p:])
        pc_v.append(vc[:, -cw_p:])
        pm_k.append(mk)
        pm_v.append(mv)
        pf.append(conv_state)
        qa, ka, va, lfa, bu, bv, qc, kc, vc, qm = project(xs, norm_mix[l], w_in[l], b_forget[l], qk_gain[l])
        ext_k = jnp.concatenate([cache_c_k[l].astype(kc.dtype), kc], axis=1)
        ext_v = jnp.concatenate([cache_c_v[l].astype(vc.dtype), vc], axis=1)
        outs = (fox_sample(qa, ka, va, lfa, cache_a_k[l], cache_a_v[l], cache_a_logf[l], page_table),
                sgu_sample(bu, bv, w_spatial[l], b_spatial[l]),
                dilated_sample(qc, ext_k, ext_v, rel_bias, cw_s),
                mem_attend(qm, cache_mem_k[l].astype(qm.dtype), cache_mem_v[l].astype(qm.dtype)))
        xs = xs + merge_groups(outs, norm_out[l], w_out[l]).astype(xs.dtype)
        f, conv_state = conv_ffn(xs, norm_ffn[l], w_up[l], conv_w[l], conv_b[l], w_down[l], state_ffn_conv[l])
        xs = xs + f.astype(xs.dtype)
        sa_k.append(ka)
        sa_v.append(va)
        sa_lf.append(lfa)
        sc_k.append(kc)
        sc_v.append(vc)
        sb_v.append(bv)
        sf.append(conv_state)
    y_prompt = xp
    y_sample = xs
    prompt_a_k = jnp.stack(pa_k)
    prompt_a_v = jnp.stack(pa_v)
    prompt_a_logf = jnp.stack(pa_lf)
    prompt_c_k = jnp.stack(pc_k)
    prompt_c_v = jnp.stack(pc_v)
    prompt_mem_k = jnp.stack(pm_k)
    prompt_mem_v = jnp.stack(pm_v)
    prompt_ffn_conv = jnp.stack(pf)
    sample_a_k = jnp.stack(sa_k)
    sample_a_v = jnp.stack(sa_v)
    sample_a_logf = jnp.stack(sa_lf)
    sample_c_k = jnp.stack(sc_k)
    sample_c_v = jnp.stack(sc_v)
    sample_b_v = jnp.stack(sb_v)
    sample_ffn_conv = jnp.stack(sf)
    return (y_prompt, y_sample, prompt_a_k, prompt_a_v, prompt_a_logf, prompt_c_k, prompt_c_v,
            prompt_mem_k, prompt_mem_v, prompt_ffn_conv, sample_a_k, sample_a_v, sample_a_logf,
            sample_c_k, sample_c_v, sample_b_v, sample_ffn_conv)


_drawn_inputs = setup_inputs


def setup_inputs(seed=0):
    import zlib

    import numpy as np

    out = dict(_drawn_inputs(seed))
    spreads = {}
    factors = {'norm_mix': 2.825,
     'norm_mem': 2.837,
     'norm_out': 3.573,
     'norm_ffn': 2.936,
     'conv_b': 5.106}
    for name, (base, spread) in spreads.items():
        noise = np.random.default_rng([zlib.crc32(name.encode()), seed]).standard_normal(out[name].shape)
        drawn = base * np.exp(spread * noise) if base else spread * noise
        out[name] = jnp.asarray(drawn.astype(out[name].dtype))
    for name, factor in factors.items():
        out[name] = (out[name] * factor).astype(out[name].dtype)
    return out
```

```python
import math
import numpy as np
import concourse.bass as bass
from concourse import mybir
from concourse.alu_op_type import AluOpType as ALU
from contextlib import ExitStack

P = 128
DM, SEQ, NSAMP, NMEM = 1024, 1024, 8, 256
COLS = NSAMP + SEQ
KC = DM // P
NT = SEQ // P
WG, HD, NH = 256, 64, 4
DFF = 2816
FT = DFF // P
NGRP = FT // 2
PAGES, PSZ, NPOOL = 32, 128, 320
EPS, NEG = 1e-6, -1e30
QSCALE = 1.0 / math.sqrt(HD)
BR = ((128, 1), (512, 4), (2048, 16))
CH = 344
NR = 2 * SEQ - 1 + P - SEQ
BLK = [(0, 512), (512, 260), (772, 512), (1284, 512), (1796, 512)]
ATT, DIL, MEMG = 0, 1, 2


def bucket(d):
    d = np.asarray(d)
    df = np.maximum(d, 1).astype(np.float32)
    large = 16 + (np.log(df / np.float32(16)) / np.float32(math.log(128.0)) * np.float32(16)).astype(np.int32)
    return np.where(d < 16, d, np.minimum(large, 31))


def branches_at(d):
    return sum(((d % dil) == 0) & (d <= win) for win, dil in BR)


def samp_dist():
    return [np.arange(128, 0, -1), 4 * np.arange(128, 32, -1), 16 * np.arange(128, 32, -1)]


def host_constants():
    c = {}
    r = np.arange(P)
    parts = [np.eye(P), np.ones((P, P)), (r[:, None] > r[None, :])]
    m4 = np.zeros((P, WG)); m4[:4] = (np.arange(WG)[None] // HD == np.arange(4)[:, None])
    sel = np.zeros((P, 8, 8)); sel[:4, np.arange(8), np.arange(8)] = 1.0
    lm = np.full((P, 3), 0.0)
    for j, d in enumerate(samp_dist()):
        lm[:len(d), j] = np.log(branches_at(d))
    dm = np.full((P, 8, 4), NEG); e8 = np.zeros((P, 8, 4))
    for b in range(8):
        dm[b, b] = 0.0; e8[b, b] = 1.0
    rs = np.ones((P, 4, NT)); rs[:, :, 0] = 0.0
    parts += [m4, sel.reshape(P, 64), lm, dm.reshape(P, 32), e8.reshape(P, 32), rs.reshape(P, 32)]
    c["ca"] = np.concatenate([np.asarray(p, np.float32) for p in parts], 1)
    d = SEQ - 1 - np.arange(NR)
    oh = np.zeros((32, NR + 320), np.float32)
    ok = d >= 0
    oh[bucket(d[ok]), np.nonzero(ok)[0]] = 1.0
    sd = np.concatenate(samp_dist())
    oh[bucket(sd), NR + np.arange(320)] = 1.0
    n = np.where(ok, branches_at(np.maximum(d, 0)), 0)
    row = np.where(n > 0, np.log(np.maximum(n, 1)), NEG).astype(np.float32)
    c["coh"] = oh
    c["clm"] = np.tile(row[None], (4, 1)).astype(np.float32)
    c["cmask"] = np.tile(np.where(ok, 0.0, NEG).astype(np.float32)[None], (4, 1))
    c["czero"] = np.zeros((1, 4096), np.float32)
    return c


CA = {}
_o = 0
for _n, _w in (("id", P), ("one", P), ("u", P), ("m4", WG), ("sel", 64), ("lm", 3), ("dm", 32), ("e8", 32), ("rs", 32)):
    CA[_n] = (_o, _o + _w)
    _o += _w
CA_W = _o
PR = {}
_o = 0
for _n, _w in (("conv", 4 * 2 * FT), ("gain", 4 * KC), ("g", 6 * HD), ("bs", 4), ("bf", 4),
               ("w00", 4), ("b0", 4), ("rb0", 4)):
    PR[_n] = (_o, _o + _w)
    _o += _w
PR_W = _o


def build(nc, t):
    f32, f32r, i32 = mybir.dt.float32, mybir.dt.float32r, mybir.dt.int32
    ACT = mybir.ActivationFunctionType
    AX = mybir.AxisListType
    RMAX = bass.bass_isa.ReduceOp.max
    ctx = ExitStack()
    with ctx:
        base = (nc.sbuf_base + 31) // 32 * 32
        end = 229344
        cur = [base]

        def at(name, shape, dt=f32, off=None):
            size = int(np.prod(shape[1:])) * 4
            size = (size + 31) // 32 * 32
            o = cur[0] if off is None else off
            if off is None:
                cur[0] += size
            assert o + size <= end, (name, o + size - end)
            return nc.alloc_sbuf_tensor_at(name, list(shape), dt, offset=o), o + size

        def keep(name, shape, dt=f32):
            return at(name, shape, dt)[0]

        prm_a = keep("prm_a", [P, PR["gain"][1]])
        u10 = keep("u10", [P, 2 * FT, 18])
        rstd_bc = keep("rstd_bc", [P, COLS])
        epsc = keep("epsc", [P, 1])
        cfree = cur[0]
        ca = keep("ca", [P, CA_W])
        prm_b = keep("prm_b", [P, PR_W - PR["gain"][1]])
        ssx = keep("ssx", [P, 11]); rsx = keep("rsx", [P, 11])
        ssn = keep("ssn", [P, 2, 8]); rsn = keep("rsn", [P, 2, 8])
        nhalf = keep("nhalf", [P, 32])
        fa = keep("fa", [P, 36]); fb = keep("fb", [P, 36]); lf = keep("lf", [P, 36]); npre = keep("npre", [P, 32])
        ptab = keep("ptab", [1, NSAMP * PAGES], i32)
        bsamp = keep("bsamp", [P, 3, NH])
        cend = cur[0]
        convA = at("convA", [P, COLS], off=cfree)[0]
        sbase, o = at("sbase", [P, 2 * FT, NSAMP], f32, cfree + 4128)
        assert o <= cend, (o, cend)
        hhi = keep("hhi", [P, KC, COLS], f32r)
        hlo = keep("hlo", [P, KC, COLS], f32r)
        R = cur[0]
        o = R
        NW = 12
        whi, o = at("whi", [P, NW, 512], f32r, o); wlo, o = at("wlo", [P, NW, 512], f32r, o)
        wst, o = at("wst", [P, 4, 512], f32, o)
        zo, o = at("zo", [P, 4, 512], f32, o)
        zn, o = at("zn", [P, 2, 512], f32, o)
        sq, o = at("sq", [P, 2, 512], f32, o)
        xst, o = at("xst", [P, 2, NMEM], f32, o)
        ob, o = at("ob", [P, 2, WG], f32, o)
        wsT, o = at("wsT", [P, NH, P], f32, o)
        crow, o = at("crow", [4 * NT, P], f32, o)
        pidx, o = at("pidx", [P, 2], i32, o)
        prep = R + 2 * NW * 2048 + 4 * 2048
        lfp = at("lfp", [P, 2, PSZ * NH], f32, prep)[0]
        lft = at("lft", [P, 2, NH, P], f32, prep + 4096)[0]
        lmask = at("lmask", [P, 2 * NH * P], f32, prep + 8192)[0]
        lscan = at("lscan", [P, 2 * NH * P], f32, prep + 12288)[0]
        clm = at("clm", [4, NR], f32, R + 8 * 2048)[0]
        rtab = at("rtab", [4, NR], f32, R + (NW + 8) * 2048)[0]
        relb = at("relb", [32, NH], f32, R + (NW + 8) * 2048 + 4608)[0]
        o2 = R
        oN, o2 = at("oN", [P, NT, DM], f32, o2)
        att0 = o2
        qst, o2 = at("qst", [P, 2, NT, HD], f32, o2); kst, o2 = at("kst", [P, 2, NT, HD], f32, o2)
        vst, o2 = at("vst", [P, 2, NT, HD + 1], f32, o2)
        qT, o2 = at("qT", [HD + 1, 2, SEQ], f32, o2); kT, o2 = at("kT", [HD + 1, 2, SEQ], f32, o2)
        toe0 = o2
        toe, o2 = at("toe", [P, 2, SEQ], f32, o2)
        lg0 = o2
        lg, o2 = at("lg", [P, 2, SEQ], f32, o2)
        pts, o2 = at("pts", [P, 2, NT, P], f32, o2)
        nm, o2 = at("nm", [P, 2, 2], f32, o2)
        rc, o2 = at("rc", [P, 2], f32, o2)
        o = max(o, o2)
        zs, o = at("zs", [NSAMP, 2308], f32, o)
        sA, o = at("sA", [P, 8, PAGES, NH], f32, o); biasA, o = at("biasA", [P, 8, PAGES, NH], f32, o)
        qb, o = at("qb", [P, 8, WG], f32, o)
        ring, o = at("ring", [P, 4, 4, WG], f32, o)
        x7 = at("x7", [P, 7, 516], f32, o - 16384)[0]
        coh = at("coh", [32, NR + 320], f32, o - 16384 - 8192)[0]
        o3 = att0
        mkd, o3 = at("mkd", [4, 3, 8, WG], f32, o3)
        oS, o3 = at("oS", [NSAMP, 4, WG], f32, o3)
        assert o3 <= toe0
        o3 = toe0
        sC, o3 = at("sC", [P, 3, 8, NH], f32, o3); sM, o3 = at("sM", [P, 2, 8, NH], f32, o3)
        est, o3 = at("est", [P, 4, 16], f32, o3)
        small, o3 = at("small", [P, 3, 32 * 5], f32, o3)
        sso, o3 = at("sso", [P, 36], f32, o3); rso, o3 = at("rso", [P, 36], f32, o3)
        prod8, o3 = at("prod8", [NSAMP, 2, WG], f32, o3)
        assert o3 <= lg0
        osq, o3 = at("osq", [P, 2, DM], f32, lg0)
        assert o3 <= o2
        x2off = R + 49152 + 8192 + 33024
        x2, o4 = at("x2", [P, KC, COLS], f32, x2off)
        stT = at("stT", [P, 2 * FT, 2, NSAMP], f32, o4)[0]
        uu, o4 = at("uu", [P, COLS], f32, o4)
        convG, o4 = at("convG", [P, COLS], f32, o4)
        o5 = att0
        wohi, o5 = at("wohi", [P, 2, KC, P], f32r, o5); wolo, o5 = at("wolo", [P, 2, KC, P], f32r, o5)
        wost, o5 = at("wost", [P, 2, KC, P], f32, o5)
        sqx, o5 = at("sqx", [P, COLS], f32, o5); sacc, o5 = at("sacc", [P, COLS], f32, o5)
        assert o5 <= x2off
        o6 = R
        uhi, o6 = at("uhi", [P, 2, KC, 256], f32r, o6); ulo, o6 = at("ulo", [P, 2, KC, 256], f32r, o6)
        dhi, o6 = at("dhi", [P, 2, DM], f32r, o6); dlo, o6 = at("dlo", [P, 2, DM], f32r, o6)
        fst, o6 = at("fst", [P, 2, DM], f32, o6)
        ahi, o6 = at("ahi", [P, 2, 2, COLS], f32r, o6); alo, o6 = at("alo", [P, 2, 2, COLS], f32r, o6)
        assert o6 <= x2off, (o6, x2off)
        ps = ctx.enter_context(nc.psum_tensor("ps", [P, 8, 512], f32))

        def cv(name, rows=P):
            a, b = CA[name]
            return ca[0:rows, a:b]

        def pv(name, rows=P):
            a, b = PR[name]
            if b <= PR["gain"][1]:
                return prm_a[0:rows, a:b]
            return prm_b[0:rows, a - PR["gain"][1]:b - PR["gain"][1]]

        ident, ones, ustr = cv("id"), cv("one"), cv("u")
        gain = pv("gain").rearrange("p (s k) -> p s k", s=4)
        conv = pv("conv").rearrange("p (s f) -> p s f", s=4)
        gq = pv("g").rearrange("p (s e) -> p s e", s=6)

        def dram(name, shape):
            return nc.dram_tensor(name, shape, f32, kind="Internal").ap()
        scr_q = dram("scr_q", (3, SEQ, WG))
        scr_b = dram("scr_b", (SEQ, WG))
        scr_qs = dram("scr_qs", (3, NSAMP, WG))
        scr_r = dram("scr_r", (8, NR))
        scr_t = dram("scr_t", (8, P, NR))
        scr_c = dram("scr_c", (8, SEQ))

        sems = {}

        def S(name):
            if name not in sems:
                sems[name] = ctx.enter_context(nc.semaphore(name))
            return sems[name]

        units = [(b, tt) for b in range(5) for tt in ["S"] + list(range(NT))] + [(5, 0), (5, 1)]
        UI = {k: i for i, k in enumerate(units)}
        NU = len(units)
        prompt_no = {}
        for k in units:
            if k[1] != "S":
                prompt_no[k] = len(prompt_no)
        bank = {k: (6 if k[1] == "S" else prompt_no[k] % 4) for k in units}
        WID = [w for _, w in BLK] + [512]
        NORM = {0: (0, 8, 0), 3: (0, 8, 2), 4: (256, 4, 4), 5: (0, 4, 5)}
        COPY = {1: (0, 256), 4: (0, 256), 5: (256, 256)}
        norm_units = [k for k in units if k[0] in NORM]
        NI = {k: i for i, k in enumerate(norm_units)}
        dve_units = [k for k in units if k[0] in NORM or k[0] == 1]
        DI = {k: i for i, k in enumerate(dve_units)}
        first_kg = UI[(1, 0)]

        def xi(k):
            return 9 + k[1] if k[0] == 5 else (0 if k[1] == "S" else 1 + k[1])

        def rows(k):
            return NSAMP if k[1] == "S" else P

        def xslot(i):
            return x7[:, i % 7, :] if i < 16 else xst[:, i % 2, :]

        def xsem(i):
            return S(f"x_ld{i % 7}") if i < 16 else S(f"m_ld{i % 2}")

        def xtotal(i):
            return 16 * (i // 7 + 1) if i < 16 else 16 * (i // 2 - 7)

        def xrow(x, n):
            if x % 3 == 0:
                return sA[0:n].rearrange("p b g h -> p (b g h)")
            return qb[0:n, 4 * (x % 3) - 4:4 * (x % 3), :].rearrange("p b c -> p (b c)")

        def prev_in_bank(k):
            same = [m for m in units[:UI[k]] if bank[m] == bank[k]]
            return same[-1] if same else None

        def dve_last(k):
            return max([DI[m] + 1 for m in dve_units if UI[m] <= UI[k]], default=0)

        def zdst(k):
            if k[1] == "S":
                a, w = BLK[k[0]]
                return zs[:, a:a + min(w, 512)]
            return zo[:, prompt_no[k] % 4, :]

        def chunk_turns():
            turns = {u: [] for u in range(-1, NU)}
            for b in range(6):
                for kc in range(KC):
                    if b == 0:
                        turns[-1].append((b, kc))
                    else:
                        u = UI[(b - 1, kc if kc < 4 else 7)]
                        turns[u if kc < 6 else UI[(b, "S")] if b < 5 else UI[(5, 0)]].append((b, kc))
            return turns
        CT = chunk_turns()
        CT_load = {u: [b * KC + kc for b, kc in CT.get(u + 2, []) if b > 0] for u in range(-1, NU)}
        CT_load[0] = sorted([b * KC + kc for v in (0, 1, 2) for b, kc in CT.get(v, []) if b > 0])
        n_out = {0: 2, 1: 1, 2: 1, 3: 2, 4: 2, 5: 2}
        kgran = {}
        for b in range(1, 5):
            for tt in range(NT):
                kgran[(b, tt)] = len(kgran)
        NKP = len(kgran)
        NKA = NSAMP * PAGES // 4

        kpool = t["cache_a_k"].rearrange("o n p h e -> (o n) p (h e)")
        vpool = t["cache_a_v"].rearrange("o n p h e -> (o n) p (h e)")
        lfpool = t["cache_a_logf"].rearrange("o n p h -> (o n) (p h)")
        o_ka = t["o_ka"]; o_va = t["o_va"]; o_kc = t["o_kc"]; o_vc = t["o_vc"]; o_mk = t["o_mk"]; o_mv = t["o_mv"]

        def load_pages(sp, pool, seq, group, slot, pages=range(4)):
            for j in pages:
                page = sp.value_load(ptab[0:1, bass.ds(seq * PAGES + (group * 4 + j), 1)], min_val=0, max_val=NPOOL - 1)
                sp.dma_start(ring[:, slot, j, :], pool[bass.ds(page, 1)].rearrange("o p c -> p (o c)"))\
                    .then_inc(S(f"ring_ld{slot}"), 16)

        def ck_rows(cache, c, b0):
            if c == 0:
                v = cache[0, b0:b0 + 4, 1920:2048]
            elif c == 1:
                v = cache[0, b0:b0 + 4, 1536:1917:4]
            else:
                v = cache[0, b0:b0 + 4, 0:1521:16]
            return v.rearrange("b r h e -> r b (h e)")
        CROWS = [128, 96, 96]
        cm = [(DIL, c, b0) for b0 in (0, 4) for c in range(3)] + [(MEMG, c, b0) for b0 in (0, 4) for c in range(2)]
        NCM = len(cm)

        def ring_total(n):
            paged = lambda m: m < NKA or NKA + NCM <= m < 2 * NKA + NCM
            return sum(64 if paged(m) else 16 for m in range(n % 4, n + 1, 4))
        V0 = [ring_total(max(m for m in range(NKA + NCM) if m % 4 == s4)) for s4 in range(4)]

        def cm_load(sp, caches, i, slot, key):
            g, c, b0 = cm[i]
            if g == DIL:
                src = ck_rows(t["cache_c_" + key], c, b0)
                n = CROWS[c]
            else:
                src = t["cache_mem_" + key][0, b0:b0 + 4, c * P:(c + 1) * P].rearrange("b r h e -> r b (h e)")
                n = P
            sp.dma_start(ring[0:n, slot, :, :], src).then_inc(S(f"ring_ld{slot}"), 16)

        AC = dict(n="ac", iters=4, blocks=[NT - s for s in range(NT)], tile=[NT - 1 - s for s in range(NT)], bias=True)
        MM = dict(n="mm", iters=2, blocks=[2] * NT, tile=list(range(NT)), bias=False)

        block = ctx.enter_context(nc.Block())

        @block.sync
        def _(sp):
            sp.dma_start(ca[:, :], t["ca"]).then_inc(S("const_ld"), 16)
            sp.dma_start(prm_a[:, :], t["prm"][:, 0:PR["gain"][1]]).then_inc(S("const_ld"), 16)
            sp.dma_start(prm_b[:, :], t["prm"][:, PR["gain"][1]:PR_W]).then_inc(S("const_ld"), 16)
            sp.dma_start(ptab[:, :], t["ptab"]).then_inc(S("const_ld"), 16)
            sp.dma_start(pidx[:, :], t["pidx"]).then_inc(S("const_ld"), 16)
            sp.dma_start(coh[:, :], t["coh"]).then_inc(S("tab_ld"), 16)
            sp.dma_start(clm[:, :], t["clm"]).then_inc(S("tab_ld"), 16)
            sp.dma_start(relb[:, :], t["rel_bias"]).then_inc(S("tab_ld"), 16)
            sp.dma_start(wsT[:, :, :], t["wsT"]).then_inc(S("const_ld"), 16)
            def stat_load(x):
                src, n = (t["x_sample"], NSAMP) if x == 0 else \
                    ((t["x_prompt"][(x - 1) * P:x * P], P) if x < 9 else (t["mem"][(x - 9) * P:(x - 8) * P], P))
                if x >= 3:
                    sp.wait_ge(S("x_stat"), x - 2)
                elif x == 1:
                    sp.wait_ge(S("rt_pe"), 6)
                sp.dma_start(xrow(x, n), src).then_inc(S(f"xrow_ld{x % 3}"), 16)
            def w_load(q):
                b, kc = divmod(q, KC)
                src = t["w_in"][0, kc * P:(kc + 1) * P, BLK[b][0]:BLK[b][0] + WID[b]] if b < 5 else \
                    t["w_mem"][0, kc * P:(kc + 1) * P, :]
                if q >= 4:
                    sp.wait_ge(S("w_split"), q - 3)
                sp.dma_start(wst[:, q % 4, 0:WID[b]], src).then_inc(S(f"w_ld{q % 4}"), 16)

            def x_load(i):
                if i < 16:
                    src, w = t["xT"][:, i % 8, (i // 8) * 516:(i // 8) * 516 + 516], 516
                else:
                    src, w = t["memT"][:, i - 16, :], NMEM
                if 7 <= i < 16:
                    sp.wait_ge(S("x_split"), i - 6)
                elif i >= 18:
                    sp.wait_ge(S("x_split"), i - 1)
                sp.dma_start(xslot(i)[:, 0:w], src).then_inc(xsem(i), 16)

            for kc in range(KC):
                x_load(kc)
                w_load(kc)
            sp.wait_ge(S("rtab"), 3)
            sp.dma_start(scr_r[4:8, :], rtab[:, :]).then_inc(S("rdram"), 16)
            sp.dma_start(scr_r[0:4, :], t["cmask"]).then_inc(S("rdram"), 16)
            sp.dma_start(scr_c[4:8, :], t["czero"].rearrange("o (a c) -> (o a) c", a=4)).then_inc(S("crow_dram"), 16)
            for i in range(8, 16):
                x_load(i)
            for x in range(11):
                stat_load(x)
                if x >= 7:
                    w_load(KC + x - 7)

            def outputs(k):
                b, tt = k
                n = prompt_no[k]
                z = zo[:, n % 4, :]
                r = slice(tt * P, (tt + 1) * P)
                so = S(f"zo_out{n % 4}")
                if b == 2:
                    sp.wait_ge(S("ob_ready"), tt + 1)
                    sp.dma_start(scr_b[r, :], ob[:, tt % 2, :]).then_inc(S(f"ob_out{tt % 2}"), 16)
                    return
                if b in NORM:
                    sp.wait_ge(S("zo_dve"), NI[k] + 1)
                if b in COPY:
                    sp.wait_ge(S("act_z"), UI[k] + 1)
                dst = {0: (scr_q[0], o_ka), 1: (o_va,), 3: (scr_q[1], o_kc), 4: (o_vc, scr_q[2]), 5: (o_mk, o_mv)}[b]
                for i, d in enumerate(dst):
                    sp.dma_start(d[r, :], z[:, i * WG:(i + 1) * WG]).then_inc(so, 16)

            lag = []
            for u, k in enumerate(units):
                b, tt = k
                for q in CT_load[u]:
                    if q >= KC + 4:
                        w_load(q)
                if k == (0, 4):
                    sp.wait_ge(S("const_ld"), 96)
                    sp.wait_ge(S("x_split"), 16)
                    for s4 in range(4):
                        load_pages(sp, kpool, 0, s4, s4)
                if k == (1, 0):
                    sp.wait_ge(S("rdram"), 32)
                if b == 1 and tt != "S":
                    src = scr_r[tt:tt + 1, :]
                    sp.dma_start(scr_t[tt], bass.AP(src.tensor, src.offset, [[0, P], [1, NR]])).then_inc(S("toe_dram"), 16)
                if b == 4 and tt != "S" and tt >= 2 and tt < 6:
                    for i in (2 * (tt - 2), 2 * (tt - 2) + 1):
                        x_load(16 + i)
                if k in kgran:
                    n = kgran[k] + 3
                    if 4 <= n < NKP:
                        sp.wait_ge(S("k_used"), n - 3)
                        load_pages(sp, kpool, n // 8, n % 8, n % 4, (0, 1))
                if u >= 2 and units[u - 2][1] != "S":
                    outputs(units[u - 2])
                if k == (0, 2):
                    sp.wait_ge(S("zs_norm"), 1)
                    sp.dma_start(scr_qs[0], zs[:, 0:WG]).then_inc(S("qs_dram"), 16)
                    sp.wait_ge(S("qs_dram"), 16)
                    sp.dma_start(qb[:, :, :], bass.AP(scr_qs.tensor, scr_qs[0].offset, [[0, P], [1, 8 * WG]]))\
                        .then_inc(S("qb_ld"), 16)
                if k == (3, 0):
                    sp.wait_ge(S("crow"), 1)
                    sp.dma_start(scr_c[0:4].rearrange("h (t p) -> (h t) p", p=P), crow[:, :]).then_inc(S("crow_dram"), 16)
                    sp.dma_start(t["o_lf"], lf[:, :]).then_inc(S("out"), 16)
            for u in (NU - 2, NU - 1):
                outputs(units[u])
            for s4 in range(4):
                uses = [k for k in prompt_no if prompt_no[k] % 4 == s4]
                sp.wait_ge(S(f"zo_out{s4}"), 16 * sum(0 if k[0] == 2 else n_out[k[0]] for k in uses))
            for s2 in range(2):
                sp.wait_ge(S(f"ob_out{s2}"), 64)
            sp.wait_ge(S("crow_dram"), 32)
            sp.wait_ge(S("toe_dram"), 128)
            sp.wait_ge(S("zo_dve"), len(norm_units))
            sp.wait_ge(S("z_done"), NU)
            sp.dma_start(oN[:, :, 2 * WG:3 * WG], scr_b.rearrange("(t p) c -> p t c", p=P)).then_inc(S("ob_ld"), 16)

            def head_load(par, h, group, hh):
                qs = scr_q[group][:, bass.ds(hh * HD, HD)].rearrange("(t p) e -> p t e", p=P)
                ks = (o_ka, o_kc, o_mk)[group][:, bass.ds(hh * HD, HD)].rearrange("(t p) e -> p t e", p=P)
                vs = (o_va, o_vc, o_mv)[group][:, bass.ds(hh * HD, HD)].rearrange("(t p) e -> p t e", p=P)
                nk = 2 if group == MEMG else NT
                ld = S(f"head_ld{par}")
                sp.dma_start(qst[:, par], qs).then_inc(ld, 16)
                sp.dma_start(kst[:, par, 0:nk], ks).then_inc(ld, 16)
                sp.dma_start(vst[:, par, 0:nk, 0:HD], vs).then_inc(ld, 16)
                if group != MEMG:
                    src = scr_t[bass.ds(h, 1), :, :]
                    off = scr_t.rearrange("h p r -> h (p r)")[bass.ds(h, 1), P - 1:P - 1 + P * (NR - 1)]
                    sp.dma_start(toe[:, par, :], off.rearrange("o (p r) -> (o p) r", r=NR - 1)[:, 0:SEQ]).then_inc(ld, 16)
                    sp.dma_start(kT[HD:HD + 1, par, :], scr_c[bass.ds(h, 1), :]).then_inc(ld, 16)

            def k_granules(h):
                for n in range(NKP + 4 * h, NKP + 4 * h + 4):
                    sp.wait_ge(S("k_used"), n - 3)
                    load_pages(sp, kpool, n // 8, n % 8, n % 4)
            head_load(0, 0, ATT, 0)
            head_load(1, 1, ATT, 1)
            k_granules(0)
            for h in range(8):
                if h + 1 < 8:
                    k_granules(h + 1)
                sp.wait_ge(S("ac_pv"), 2 + 8 * (h + 1))
                sp.wait_ge(S("ac_lg"), 2 + 8 * (h + 1))
                if h + 2 < 8:
                    head_load(h % 2, h + 2, (h + 2) // 4, (h + 2) % 4)
                else:
                    head_load(h % 2, h - 6, MEMG, h - 6)
            for h in (2, 3):
                sp.wait_ge(S("mm_pv"), 2 + 8 * (h - 1))
                head_load(h % 2, h, MEMG, h)
            for i in range(NCM):
                n = NKA + i
                sp.wait_ge(S("k_used"), n - 3)
                cm_load(sp, None, i, n % 4, "k")
                if i == 0:
                    sp.wait_ge(S("k_used"), NKA)
                    sp.wait_ge(S("zs_norm"), 3)
                    sp.dma_start(scr_qs[1], zs[:, BLK[3][0]:BLK[3][0] + WG]).then_inc(S("qs_dram"), 16)
                    sp.dma_start(scr_qs[2], zs[:, BLK[4][0] + WG:BLK[4][0] + 2 * WG]).then_inc(S("qs_dram"), 16)
                    sp.wait_ge(S("qs_dram"), 48)
                    sp.dma_start(qb[:, :, :], bass.AP(scr_qs.tensor, scr_qs[1].offset, [[0, P], [1, 8 * WG]]))\
                        .then_inc(S("qb_ld"), 16)
                if i == 6:
                    sp.wait_ge(S("k_used"), NKA + 6)
                    sp.dma_start(qb[:, :, :], bass.AP(scr_qs.tensor, scr_qs[2].offset, [[0, P], [1, 8 * WG]]))\
                        .then_inc(S("qb_ld"), 16)
            slot0 = (NKA + NCM) % 4
            for j in range(0, 8, 2):
                if j < 4:
                    sp.wait_ge(S("k_used"), NKA + NCM - 3 + j)
                else:
                    sp.wait_ge(S("v_used"), 8 + j - 3)
                load_pages(sp, vpool, 0, j, (slot0 + j) % 4)
            with sp.Fori(1, 8) as b:
                for j in range(0, 8, 2):
                    sp.wait_ge(S("v_used"), b * 8 + (8 + j - 3))
                    load_pages(sp, vpool, b, j, (slot0 + j) % 4)
            for i in range(NCM):
                sp.wait_ge(S("v_used"), 8 + NKA + i - 3)
                cm_load(sp, None, i, (NKA + NCM + NKA + i) % 4, "v")
            sp.wait_ge(S("zs_norm"), 3)
            sp.dma_start(t["o_zs"], zs[:, :]).then_inc(S("out"), 16)
            sp.wait_ge(S("o_scaled"), 9)
            sp.wait_ge(S("ot_pe"), 9)
            sp.wait_ge(S("out"), 32)
            for kc in range(KC):
                sp.dma_start(x2[:, kc, :], t["xT"][:, kc, :]).then_inc(S("x2_ld"), 16)
            sp.dma_start(stT[:, :, :, :], t["stT"]).then_inc(S("x2_ld"), 16)
            for d in range(KC):
                if d >= 2:
                    sp.wait_ge(S("wo_split"), d - 1)
                sp.dma_start(wost[:, d % 2], t["w_outL"][d]).then_inc(S(f"wo_ld{d % 2}"), 16)
            sp.wait_ge(S("out_pe"), 8)

            upL, dnL = t["w_upL"], t["w_down"]

            def f_piece(i, src):
                sp.dma_start(fst[:, i % 2], src).then_inc(S(f"f_ld{i % 2}"), 16)
            for p in range(8):
                if p >= 2:
                    sp.wait_ge(S("f_split"), p - 1)
                f_piece(p, upL[p // 4, (p % 4) // 2, p % 2])
            with sp.Fori(1, NGRP - 1) as G:
                for i in range(6):
                    sp.wait_ge(S("f_split"), G * 6 + (i + 1))
                    if i < 2:
                        f_piece(i, dnL[bass.ds(G * 2 + (i - 2), 1)].rearrange("o p c -> (o p) c"))
                    else:
                        f_piece(i, upL[bass.ds(G + 1, 1), (i - 2) // 2, i % 2].rearrange("o p c -> (o p) c"))
            for i in range(4):
                p = 8 + 6 * (NGRP - 2) + i
                sp.wait_ge(S("f_split"), p - 1)
                f_piece(p, dnL[2 * (NGRP - 2) + i])
            for d in range(KC):
                sp.wait_ge(S("f_free"), 4 + 12 * (NGRP - 1) + d + 1)
                sp.dma_start(t["o_yT"][:, d, :], x2[:, d, :]).then_inc(S("out"), 16)
            sp.dma_start(t["o_u10"], u10[:, :, :]).then_inc(S("out"), 16)
            sp.wait_ge(S("out"), 16 * (1 + 1 + KC + 1))

        targets = []

        class LoopTargets:

            def __init__(self, eng, last):
                self.eng, self.reg, self.cur = eng, {}, {}
                self.last = {name: (per, max(per, c)) for name, (per, c) in last.items()}
                for name, (per, c) in self.last.items():
                    self.reg[name] = eng.alloc_register(f"{name}_{len(targets)}")
                    targets.append(name)
                    eng.reg_mov(self.reg[name], c - per)
                    self.cur[name] = c - per

            def wait(self, name, c):
                if c <= self.cur[name]:
                    return
                self.eng.reg_add(self.reg[name], self.reg[name], c - self.cur[name])
                self.cur[name] = c
                self.eng.wait_ge(S("const_ld"), 96)
                self.eng.wait_ge(S(name), self.reg[name])

            def end(self):
                for name, (per, c) in self.last.items():
                    assert self.cur[name] <= c, (name, self.cur[name], c)
                    if self.cur[name] < c:
                        self.eng.reg_add(self.reg[name], self.reg[name], c - self.cur[name])
                    self.cur[name] = c - per

        def zview(k):
            return ps[0:rows(k), bank[k], :]

        def wait_zo_free(e, k):
            n = prompt_no[k]
            if n >= 4:
                m = [x for x in prompt_no if prompt_no[x] == n - 4][0]
                if m[0] == 2:
                    e.wait_ge(S("ob_ready"), m[1] + 1)
                done = sum(n_out[x[0]] for x in prompt_no if prompt_no[x] % 4 == n % 4 and prompt_no[x] < n and x[0] != 2)
                if done:
                    e.wait_ge(S(f"zo_out{n % 4}"), 16 * done)

        SBANK = lambda a: ps[:, 2 * a:2 * a + 2, :].rearrange("p b c -> p (b c)")

        def U3(par):
            return ps[:, 3 * par:3 * par + 3, 0:CH]

        def c3(ap):
            return ap.rearrange("p (b c) -> p b c", b=3)

        @block.tensor
        def _(pe):
            pe.wait_ge(S("const_ld"), 96)
            pe.wait_ge(S("tab_ld"), 48)
            for j in range(3):
                w = min(512, NR - 512 * j)
                pe.matmul(ps[0:NH, j, 0:w], relb[:, :], coh[:, 512 * j:512 * j + w], start=True, stop=True)\
                    .then_inc(S("rt_pe"), 1)
            for c in range(3):
                n = CROWS[c]
                o_ = NR + sum(CROWS[:c])
                pe.matmul(ps[0:n, 3, NH * c:NH * c + NH], coh[:, o_:o_ + n], relb[:, :], start=True, stop=True)\
                    .then_inc(S("rt_pe"), 1)
            pe.wait_ge(S("lfp_ld"), 32)
            for i in range(2):
                for h in range(NH):
                    pe.transpose(ps[:, 4 + i, h * P:(h + 1) * P], lfp[:, i, h::NH], ident).then_inc(S("lft_pe"), 1)
            pe.wait_ge(S("lsuf"), 1)
            for i in range(2):
                v = slice(i * 512, (i + 1) * 512)
                pe.matmul(ps[:, 6 + i, :], ustr, lft[:, i].rearrange("p h c -> p (h c)"), start=True, stop=False)
                pe.matmul(ps[:, 6 + i, :], ones, lmask[:, v], start=False, stop=True).then_inc(S("lft_pe"), 1)

            def sgu(tt):
                k = (2, tt)
                if tt == 0:
                    pe.wait_ge(S("crow"), 1)
                    pe.wait_ge(S("ws_mask"), 2)
                pe.wait_ge(S("act_z"), UI[k] + 1)
                if tt >= 1:
                    pe.wait_ge(S("ob_ready"), tt)
                v = zo[:, prompt_no[k] % 4, WG:2 * WG]
                for g in range(NH):
                    i = pe.matmul(ps[:, 7, WG + g * HD:WG + (g + 1) * HD], wsT[:, g, :], v[:, g * HD:(g + 1) * HD],
                                  start=True, stop=True)
                i.then_inc(S("sgu_pe"), 1)

            for u, k in enumerate(units):
                b, tt = k
                pk = prev_in_bank(k)
                if pk is not None:
                    pe.wait_ge(S("act_z"), UI[pk] + 1)
                    if dve_last(pk):
                        pe.wait_ge(S("dve_z"), dve_last(pk))
                elif bank[k] == 6:
                    pe.wait_ge(S("lft_cp"), 4)
                else:
                    pe.wait_ge(S("rtab"), 4)
                c0 = 0 if tt == "S" else (tt * P if b == 5 else NSAMP + tt * P)
                for kc in range(KC):
                    if tt == "S" or (b == 5 and tt == 0):
                        pe.wait_ge(S("w_split"), b * KC + kc + 1)
                    if b == 0:
                        pe.wait_ge(S("x_split"), (kc + 1) if tt in ("S", 0, 1, 2) else 9 + kc)
                    if b == 5:
                        pe.wait_ge(S("x_split"), 17 + kc)
                    sl = (b * KC + kc) % NW
                    w = WID[b]
                    lh, ll = hhi[:, kc, c0:c0 + P], hlo[:, kc, c0:c0 + P]
                    out = ps[:, bank[k], 0:w]
                    pe.matmul(out, lh, whi[:, sl, 0:w], start=(kc == 0), stop=False)
                    pe.matmul(out, lh, wlo[:, sl, 0:w], start=False, stop=False)
                    i = pe.matmul(out, ll, whi[:, sl, 0:w], start=False, stop=(kc == KC - 1))
                    if tt == NT - 1 or (b == 5 and tt == 1):
                        i.then_inc(S("w_used"), 1)
                    elif kc == KC - 1:
                        i.then_inc(S("z_done"), 1)
                if tt == NT - 1 or (b == 5 and tt == 1):
                    pe.wait_ge(S("w_used"), (b + 1) * KC)
                    pe.sem_inc(S("z_done"), 1)
                if k == (2, 0):
                    pe.wait_ge(S("forget"), 3)
                    pe.wait_ge(S("lft_cp"), 4)
                    pe.matmul(ps[:, 7, 0:32], ustr, lf[:, 0:32], start=True, stop=False)
                    pe.matmul(ps[:, 7, 0:32], ones, npre[:, :], start=False, stop=True).then_inc(S("csum_pe"), 1)
                if k == (2, 1):
                    pe.wait_ge(S("forget"), 4)
                    pe.transpose(ps[0:32, 7, 64:64 + P], fb[:, 0:32], ident).then_inc(S("csum_pe"), 1)
                if b == 2 and tt not in ("S", 0, 1):
                    sgu(tt - 2)
                if k == (3, "S"):
                    sgu(6)
                if k == (3, 0):
                    sgu(7)

            def attention(A):
                n, two = A["n"], A["bias"]
                K1 = HD + 1 if two else HD
                free = "_lg" if two else "_exp"
                exp_seed = 0 if two else 2
                last = {"head_ld0": (A["ld"], A["ld0"] + A["ld"]), "head_ld1": (A["ld"], A["ld0"] + A["ld"]),
                        n + free: (16, 16), n + "_qT": (2, 2), n + "_kT": (2, 2), n + "_eva": (16, 17),
                        n + "_o": (16, 16)}
                if two:
                    last[n + "_exp"] = (16, 16)
                    last[n + "_evb"] = (8, 9)
                else:
                    last[n + "_exp"] = (16, 18)
                T_ = LoopTargets(pe, last)
                pe.sem_inc(S(n + "_tpa"), 2)
                pe.sem_inc(S(n + "_pv"), 2)
                if two:
                    pe.sem_inc(S(n + "_tpb"), 1)
                with pe.Fori(0, A["iters"]):
                    for par in range(2):
                        T_.wait(f"head_ld{par}", A["ld0"] + A["ld"])
                        T_.wait(n + free, 8 * par + 2)
                        for j in range(NT):
                            pe.transpose(ps[0:HD, j // 4, (j % 4) * P:(j % 4 + 1) * P], qst[:, par, j, :], ident)
                        for j in range(A["nk"]):
                            i = pe.transpose(ps[0:HD, 2 + j // 4, (j % 4) * P:(j % 4 + 1) * P], kst[:, par, j, :], ident)
                        i.then_inc(S(n + "_prep"), 1)
                        T_.wait(n + "_qT", par + 1)
                        T_.wait(n + "_kT", par + 1)

                        def qk(s):
                            g, W = 8 * par + s, P * A["blocks"][s]
                            T_.wait(n + free, g + 1)
                            q0 = A["tile"][s] * P
                            for c in range(0, W, 512):
                                w = min(512, W - c)
                                i = pe.matmul(ps[:, 2 * (s % 2) + c // 512, 0:w], qT[0:K1, par, q0:q0 + P],
                                              kT[0:K1, par, c:c + w], start=True, stop=True)
                            i.then_inc(S(n + "_qk"), 1)

                        def tp(s):
                            g, nb = 8 * par + s, A["blocks"][s]
                            T_.wait(n + "_exp", g + 1 + exp_seed)
                            T_.wait(n + "_eva", g + 1)
                            for j in range(min(nb, 4)):
                                i = pe.transpose(ps[:, 4, j * P:(j + 1) * P], lg[:, s % 2, j * P:(j + 1) * P], ident)
                            i.then_inc(S(n + "_tpa"), 1)
                            if nb > 4:
                                T_.wait(n + "_evb", 4 * par + s + 1)
                                for j in range(4, nb):
                                    i = pe.transpose(ps[:, 5, (j - 4) * P:(j - 3) * P],
                                                     lg[:, s % 2, j * P:(j + 1) * P], ident)
                                i.then_inc(S(n + "_tpb"), 1)

                        def pv_(s):
                            g, nb = 8 * par + s, A["blocks"][s]
                            T_.wait(n + "_eva", g + 2)
                            if nb > 4:
                                T_.wait(n + "_evb", 4 * par + s + 2)
                            T_.wait(n + "_o", g + 1)
                            for j in range(nb):
                                i = pe.matmul(ps[:, 6 + s % 2, 0:HD + 1], pts[:, s % 2, j, :], vst[:, par, j, :],
                                              start=(j == 0), stop=(j == nb - 1))
                            i.then_inc(S(n + "_pv"), 1)

                        qk(0)
                        qk(1)
                        tp(0)
                        for s in range(2, NT):
                            qk(s)
                            tp(s - 1)
                            pv_(s - 2)
                        tp(NT - 1)
                        pv_(NT - 2)
                        pv_(NT - 1)
                    T_.end()
            AC.update(ld=80, ld0=0, nk=NT)
            MM.update(ld=48, ld0=4 * 80, nk=2)
            pe.wait_ge(S("dve_set"), 7)
            attention(AC)
            attention(MM)

            pe.sem_inc(S("v_used"), 8)
            pe.wait_ge(S("mm_o"), 2 + 32)
            last = {"est": (8, 8), "acc_cp": (1, 1)}
            slot0 = (NKA + NCM) % 4
            for j in range(4):
                last[f"ring_ld{j}"] = (128, V0[j] + 128)
            T_ = LoopTargets(pe, last)
            with pe.Fori(0, NSAMP):
                for j in range(8):
                    sl = (slot0 + j) % 4
                    T_.wait(f"ring_ld{sl}", V0[sl] + 64 * (j // 4 + 1))
                    T_.wait("est", j + 1)
                    if j == 0:
                        T_.wait("acc_cp", 1)
                    for g in range(4):
                        i = pe.matmul(ps[0:NH, 0, 0:WG], est[:, j % 4, NH * g:NH * g + NH], ring[:, sl, g, :],
                                      start=(j == 0 and g == 0), stop=(j == 7 and g == 3))
                    i.then_inc(S("v_used"), 1)
                T_.end()
            pe.wait_ge(S("acc_cp"), 1 + NSAMP)
            pe.wait_ge(S("e_act"), 3)
            for i, (g, c, b0) in enumerate(cm):
                n_ = NKA + NCM + NKA + i
                sl = n_ % 4
                pe.wait_ge(S(f"ring_ld{sl}"), ring_total(n_))
                nk = CROWS[c] if g == DIL else P
                e_ = sC if g == DIL else sM
                lastc = 2 if g == DIL else 1
                grp = {0: 0, 3: 1, 6: 2, 8: 3}.get(i)
                if grp is not None and grp > 0:
                    pe.wait_ge(S("acc2_cp"), grp)
                for b in range(4):
                    m = pe.matmul(ps[0:NH, b, 0:WG], e_[0:nk, c, b0 + b, :], ring[0:nk, sl, b, :],
                                  start=(c == 0), stop=(c == lastc))
                m.then_inc(S("v_used"), 1)
            pe.wait_ge(S("esum"), 3)
            for g in range(3):
                for h in range(NH):
                    m = pe.matmul(ps[0:NSAMP, 6, 8 * g + h:8 * g + h + 1], small[:, g, 32 + h:64:NH], ones[:, 0:1],
                                  start=True, stop=True)
            pe.wait_ge(S("acc2_cp"), 4)
            sel = cv("sel", 4).rearrange("p (b m) -> p b m", b=8)
            for g in range(3):
                for b in range(NSAMP):
                    m = pe.matmul(ps[0:NSAMP, 4 + (g > 1), WG * (g % 2):WG * (g % 2) + WG], sel[:, b, :], mkd[:, g, b, :],
                                  start=(b == 0), stop=(b == NSAMP - 1))
            m.then_inc(S("samp_pe"), 1)

            for x, tt in enumerate(list(range(NT)) + ["S"]):
                pe.wait_ge(S("o_scaled"), x + 1)
                a = x % 2
                if x >= 2:
                    pe.wait_ge(S("o_lo"), x - 1)
                else:
                    pe.wait_ge(S("acc2_cp"), 4)
                r = NSAMP if tt == "S" else P
                for j in range(KC):
                    src = oS[:, j // 2, (j % 2) * P:(j % 2 + 1) * P] if tt == "S" else oN[:, tt, j * P:(j + 1) * P]
                    dst = SBANK(a)[:, j * r:(j + 1) * r]
                    m = pe.transpose(dst, src, ident[0:r, 0:r])
                m.then_inc(S("ot_pe"), 1)

            def product(par, lhs_hi, lhs_lo, rhs_hi, rhs_lo, nk):
                for kc in range(nk):
                    for ch in range(3):
                        out = ps[:, 3 * par + ch, 0:CH]
                        cs = slice(ch * CH, (ch + 1) * CH)
                        pe.matmul(out, lhs_hi(kc), rhs_hi(kc)[:, cs], start=(kc == 0), stop=False)
                        pe.matmul(out, lhs_hi(kc), rhs_lo(kc)[:, cs], start=False, stop=False)
                        i = pe.matmul(out, lhs_lo(kc), rhs_hi(kc)[:, cs], start=False, stop=(kc == nk - 1))
                return i
            pe.wait_ge(S("o_lo"), 9)
            for d in range(KC):
                pe.wait_ge(S("wo_split"), d + 1)
                if d >= 2:
                    pe.wait_ge(S("x2_add"), d - 1)
                else:
                    pe.wait_ge(S("o_scaled"), 9)
                product(d % 2, lambda kc: wohi[:, d % 2, kc, :], lambda kc: wolo[:, d % 2, kc, :],
                        lambda kc: hhi[:, kc, :], lambda kc: hlo[:, kc, :], KC).then_inc(S("out_pe"), 1)

            def up(k, first=False):
                half, j = k % 2, k // 2
                return product(k % 2, lambda kc: uhi[:, half, kc, j * P:(j + 1) * P],
                               lambda kc: ulo[:, half, kc, j * P:(j + 1) * P],
                               lambda kc: hhi[:, kc, :], lambda kc: hlo[:, kc, :], KC)

            def down(d, gp):
                return product(d % 2, lambda f: dhi[:, f, d * P:(d + 1) * P], lambda f: dlo[:, f, d * P:(d + 1) * P],
                               lambda f: ahi[:, gp, f, :], lambda f: alo[:, gp, f, :], 2)
            pe.wait_ge(S("h2_split"), KC)
            for k in range(4):
                pe.wait_ge(S("f_split"), 4)
                if k == 0:
                    pe.wait_ge(S("x2_add"), 7)
                elif k == 1:
                    pe.wait_ge(S("x2_add"), 8)
                    pe.wait_ge(S("sacc"), KC)
                    for ch in range(3):
                        m = pe.matmul(ps[:, 3 + ch, 0:CH], ones, sacc[:, ch * CH:(ch + 1) * CH], start=True, stop=True)
                    m.then_inc(S("ms_pe"), 1)
                    pe.wait_ge(S("ms_cp"), 1)
                else:
                    pe.wait_ge(S("f_free"), k - 1)
                up(k).then_inc(S("f_pe"), 1)
            T_ = LoopTargets(pe, {"f_split": (12, 16), "f_free": (24, 26), "a_split": (4, 4)})
            with pe.Fori(0, (NGRP - 1) // 2):
                for par in range(2):
                    for k in range(4):
                        if k == 0:
                            T_.wait("f_split", 6 * par + 8)
                        T_.wait("f_free", 12 * par + 3 + k)
                        up(k).then_inc(S("f_pe"), 1)
                    T_.wait("f_split", 6 * par + 10)
                    T_.wait("a_split", 2 * par + 2)
                    for d in range(KC):
                        T_.wait("f_free", 12 * par + 7 + d)
                        down(d, par).then_inc(S("f_pe"), 1)
                T_.end()
            pe.wait_ge(S("f_split"), 6 * NGRP)
            pe.wait_ge(S("a_split"), 2 * NGRP)
            for d in range(KC):
                pe.wait_ge(S("f_free"), 4 + 12 * (NGRP - 1) + d - 1)
                down(d, 0).then_inc(S("f_pe"), 1)

        def ffn_waits(e, last, G, T_, par):
            def w(name, base, per):
                if G == 0:
                    e.wait_ge(S(name), base - min(per, 4))
                elif T_ is None:
                    e.wait_ge(S(name), base + per * (G - 1))
                else:
                    T_.wait(name, base + per * par)
            return w

        @block.scalar
        def _(act):
            def split_hi(q):
                b = q // KC
                act.wait_ge(S(f"w_ld{q % 4}"), 16 * (q // 4 + 1))
                if q >= NW:
                    act.wait_ge(S("w_used"), q - NW + 1)
                elif q == 8:
                    act.wait_ge(S("rdram"), 32)
                    act.wait_ge(S("rtab"), 3)
                act.activation(whi[:, q % NW, 0:WID[b]], wst[:, q % 4, 0:WID[b]], ACT.Copy).then_inc(S("w_hi"), 1)

            def x_hi(i):
                act.wait_ge(xsem(i), xtotal(i))
                if i < 16:
                    c = slice((i // 8) * 516, (i // 8) * 516 + 516)
                    w, kc, s = 516, i % 8, 0
                else:
                    c, w, kc, s = slice(0, NMEM), NMEM, i - 16, 1
                    act.wait_ge(S("z_done"), UI[(4, 1)] + 1)
                act.activation(hhi[:, kc, c], xslot(i)[:, 0:w], ACT.Copy, scale=gain[:, s, kc:kc + 1])\
                    .then_inc(S("x_hi"), 1)

            act.wait_ge(S("const_ld"), 96)
            for i in range(2):
                act.wait_ge(S("lft_pe"), 4 * (i + 1))
                act.activation(lft[:, i].rearrange("p h c -> p (h c)"), ps[:, 4 + i, :], ACT.Copy).then_inc(S("lft_cp"), 1)
            for kc in range(KC):
                x_hi(kc)
                split_hi(kc)
                if kc == 2:
                    for i in range(2):
                        act.wait_ge(S("lft_pe"), 8 + i + 1)
                        for b4 in range(4):
                            v = ps[:, 6 + i, :].rearrange("p (h b g) -> p b g h", h=NH, b=4)[:, b4]
                            m = act.activation(biasA[:, 4 * i + b4], v, ACT.Copy)
                        m.then_inc(S("lft_cp"), 1)
            for i in range(8, 16):
                x_hi(i)
            act.wait_ge(S("dve_set"), 1)
            act.wait_ge(S("lsuf"), 1)
            for x in range(11):
                n = NSAMP if x == 0 else P
                act.wait_ge(S(f"xrow_ld{x % 3}"), 16 * (x // 3 + 1))
                if x >= 1:
                    act.wait_ge(S("x_stat"), x)
                if x == 0:
                    act.wait_ge(S("lft_pe"), 10)
                act.activation(zn[0:n].rearrange("p a c -> p (a c)"), xrow(x, n),
                               ACT.Square, accum_out=ssx[0:n, x:x + 1]).then_inc(S("x_stat"), 1)
            act.wait_ge(S("rs_row"), 1)
            for u, k in enumerate(units):
                b, tt = k
                for bb, kc in CT[u]:
                    split_hi(bb * KC + kc)
                if b == 4 and tt != "S" and tt >= 2 and tt < 6:
                    for i in (2 * (tt - 2), 2 * (tt - 2) + 1):
                        x_hi(16 + i)
                r = rows(k)
                rx = rsx[0:r, xi(k):xi(k) + 1]
                z = zview(k)
                act.wait_ge(S("z_done"), u + 1)
                dst = zdst(k)
                if b in COPY or b == 2:
                    if tt != "S":
                        wait_zo_free(act, k)
                    elif b == 1:
                        act.wait_ge(S("zs_norm"), 1)
                if b in COPY:
                    c0, w = COPY[b]
                    if b == 1 and tt == "S":
                        w = 260
                    m = act.activation(dst[:, c0:c0 + w], z[:, c0:c0 + w], ACT.Copy, scale=rx)
                if b == 2:
                    m = act.activation(dst[:, 0:512], z[:, :], ACT.Gelu_apprx_tanh, scale=rx)
                if b in NORM:
                    c0, nh, _g = NORM[b]
                    if NI[k] >= 2:
                        act.wait_ge(S("ss_dve"), NI[k] - 1)
                    m = act.activation(sq[0:r, NI[k] % 2, 0:nh * HD], z[:, c0:c0 + nh * HD], ACT.Square, scale=rx)
                m.then_inc(S("act_z"), 1)
                if k in kgran and 4 <= kgran[k] + 3 < NKP:
                    n_ = kgran[k] + 3
                    act.wait_ge(S("k_used"), n_ - 3)
                    load_pages(act, kpool, n_ // 8, n_ % 8, n_ % 4, (2, 3))
                if k == (1, NT - 1):
                    act.wait_ge(S("forget"), 1)
                    act.activation(fb[:, :], fb[:, :], ACT.Exp).then_inc(S("fb_act"), 1)
                    act.wait_ge(S("fb_act"), 1)
                    act.activation(fb[:, :], fb[:, :], ACT.Ln, bias=1.0).then_inc(S("fb_act"), 1)
                if k == (2, 2):
                    act.wait_ge(S("csum_pe"), 2)
                    act.activation(crow[:, :], ps[0:32, 7, 64:64 + P], ACT.Copy).then_inc(S("crow"), 1)

            def attention(A):
                n, two = A["n"], A["bias"]
                last = {n + "_prep": (2, 2), n + "_nm": (16, 16), n + "_tpa": (16, 18), n + "_pv": (16, 16)}
                T_ = LoopTargets(act, last)
                act.sem_inc(S(n + "_eva"), 1)
                if not two:
                    act.sem_inc(S(n + "_exp"), 2)
                with act.Fori(0, A["iters"]):
                    for par in range(2):
                        T_.wait(n + "_prep", par + 1)
                        act.activation(qT[0:HD, par, :], SBANK(0)[0:HD, :], ACT.Copy).then_inc(S(n + "_qT"), 1)

                        def ex(s):
                            g, W = 8 * par + s, P * A["blocks"][s]
                            T_.wait(n + "_nm", g + 1)
                            if not two:
                                T_.wait(n + "_tpa", g + 1)
                            src = lg[:, s % 2, 0:W] if two else SBANK(s % 2)[:, 0:W]
                            act.activation(lg[:, s % 2, 0:W], src, ACT.Exp, bias=nm[:, s % 2, 1:2])\
                                .then_inc(S(n + "_exp"), 1)

                        def eva(s):
                            g, nb = 8 * par + s, min(4, A["blocks"][s])
                            T_.wait(n + "_tpa", g + 3)
                            T_.wait(n + "_pv", g + 1)
                            act.activation(pts[:, s % 2, 0:nb, :].rearrange("p b c -> p (b c)"), ps[:, 4, 0:nb * P],
                                           ACT.Copy).then_inc(S(n + "_eva"), 1)
                        ex(0)
                        for s in range(1, NT):
                            ex(s)
                            eva(s - 1)
                        eva(NT - 1)
                    T_.end()
            act.wait_ge(S("zo_dve"), len(norm_units))
            act.wait_ge(S("z_done"), NU)
            attention(AC)
            act.wait_ge(S("sub"), 1)
            act.activation(sA[:, :, :, :].rearrange("p b g h -> p (b g h)"), sA[:, :, :, :].rearrange("p b g h -> p (b g h)"),
                           ACT.Exp).then_inc(S("e_act"), 1)
            attention(MM)
            act.wait_ge(S("e_act"), 1)
            act.wait_ge(S("ob_ld"), 16)
            act.wait_ge(S("mm_o"), 2 + 32)
            act.wait_ge(S("dve_set"), 8)
            act.wait_ge(S("k_used"), NKA + NCM)
            T_ = LoopTargets(act, {"v_used": (8, 12), "o_sq": (4, 4)})
            act.sem_inc(S("o_sq"), 4)
            with act.Fori(0, NSAMP) as b:
                for j in range(8):
                    T_.wait("v_used", 8 + j - 3)
                    act.activation(est[:, j % 4, :], sA[:, bass.ds(b, 1), 4 * j:4 * j + 4, :].rearrange("p o g h -> p (o g h)"),
                                   ACT.Copy).then_inc(S("est"), 1)
                    if j % 2 == 1:
                        load_pages(act, vpool, b, j, (NKA + NCM + j) % 4)
                    if j % 2 == 1:
                        g = j // 2
                        T_.wait("o_sq", g + 1)
                        act.activation(osq[:, 0, g * WG:(g + 1) * WG],
                                       oN[:, bass.ds(b, 1), g * WG:(g + 1) * WG].rearrange("p o c -> p (o c)"),
                                       ACT.Square, accum_out=sso[:, bass.ds(b * 4 + g, 1)]).then_inc(S("o_sq"), 1)
                T_.end()
            for g, s_ in ((1, sC), (2, sM)):
                act.wait_ge(S("sub"), 2 * g + 1)
                v = s_[:, :, :, :].rearrange("p c b h -> p (c b h)")
                act.activation(v, v, ACT.Exp).then_inc(S("e_act"), 1)
            for g in range(2):
                act.wait_ge(S("sub"), 2 * g + 2)
                act.activation(small[0:8, g, 136:140], small[0:8, g, 136:140], ACT.Exp).then_inc(S("e_act"), 1)

            def w_out_hi(d):
                act.wait_ge(S("wo_gain"), d + 1)
                if d >= 2:
                    act.wait_ge(S("out_pe"), d - 1)
                act.activation(wohi[:, d % 2], wost[:, d % 2], ACT.Copy).then_inc(S("wo_hi"), 1)
            for x, tt in enumerate(list(range(NT)) + ["S"]):
                r = NSAMP if tt == "S" else P
                c0 = 0 if tt == "S" else NSAMP + tt * P
                if tt == "S":
                    act.wait_ge(S("oS"), 4)
                    for g in range(4):
                        act.wait_ge(S("o_sq"), 4 + 32 + g)
                        act.activation(osq[0:8, 1, g * WG:(g + 1) * WG], oS[:, g, :], ACT.Square,
                                       accum_out=sso[0:8, 32 + g:33 + g]).then_inc(S("o_sq"), 1)
                act.wait_ge(S("ot_pe"), x + 1)
                act.activation(hhi[:, :, c0:c0 + r], SBANK(x % 2)[:, 0:KC * r].rearrange("p (k c) -> p k c", k=KC),
                               ACT.Copy).then_inc(S("o_hi"), 1)
            for d in range(KC):
                w_out_hi(d)
                if d >= 1:
                    act.wait_ge(S("x2_add"), d)
                    if d >= 2:
                        act.wait_ge(S("sacc"), d - 1)
                    act.activation(sqx[:, :], x2[:, d - 1, :], ACT.Square).then_inc(S("sqx"), 1)
            act.wait_ge(S("x2_add"), KC)
            act.wait_ge(S("sacc"), KC - 1)
            act.activation(sqx[:, :], x2[:, KC - 1, :], ACT.Square).then_inc(S("sqx"), 1)
            act.wait_ge(S("out_pe"), KC)
            for kc in range(KC):
                act.activation(hhi[:, kc, :], x2[:, kc, :], ACT.Copy, scale=gain[:, 3, kc:kc + 1]).then_inc(S("h2_hi"), 1)

            def up_hi(i, w):
                half, q4 = i // 2, i % 2
                return act.activation(uhi[:, half, 4 * q4:4 * q4 + 4, :].rearrange("p k c -> p (k c)"), fst[:, i % 2],
                                      ACT.Copy).then_inc(S("f_hi"), 1)
            act.wait_ge(S("h2_split"), KC)
            act.wait_ge(S("sacc"), KC)
            for p in range(4):
                act.wait_ge(S(f"f_ld{p % 2}"), 16 * (p // 2 + 1))
                up_hi(p, None)
            act.wait_ge(S("ms_pe"), 1)
            act.activation(c3(rstd_bc[:, :]), U3(1), ACT.Sqrt, scale=1.0 / DM, bias=epsc[:, 0:1]).then_inc(S("ms_cp"), 1)

            def chain_affine(w, k, ft):
                cb = convA if k % 2 == 0 else convG
                w("f_free", 4 + k + 1, 12)
                act.activation(cb[:, NSAMP:COLS], uu[:, NSAMP:COLS], ACT.Identity, scale=conv[:, 2, ft],
                               bias=conv[:, 3, ft]).then_inc(S("aff"), 1)

            def chain_silu(w, j):
                w("tap2", 4 + 2 * j + 2, 4)
                act.activation(convG[:, :], convG[:, :], ACT.Silu).then_inc(S("silu"), 1)

            def chain_hi(w, j, gp, first=False):
                w("cmul", 2 + j + 1, 2)
                if not first:
                    w("f_pe", 4, 12)
                act.activation(ahi[:, gp, j, :], convA[:, :], ACT.Copy).then_inc(S("a_hi"), 1)

            def fts(G, half, j):
                if isinstance(G, int):
                    return slice(half * FT + 2 * G + j, half * FT + 2 * G + j + 1)
                return bass.ds(G * 2 + (half * FT + j), 1)

            def group(w, G, gp, downs, ups):
                first = G == 0 if isinstance(G, int) else False
                for k in range(4):
                    if downs and k < 2:
                        w(f"f_ld{k}", 16 * 5, 48)
                        w("f_pe", 4, 12)
                        act.activation(dhi[:, k, :], fst[:, k], ACT.Copy).then_inc(S("f_hi"), 1)
                    if k == 2:
                        chain_silu(w, 0)
                        chain_hi(w, 0, gp, first)
                    chain_affine(w, k, fts(G, k % 2, k // 2))
                chain_silu(w, 1)
                chain_hi(w, 1, gp, first)
                if ups:
                    for i in range(4):
                        w(f"f_ld{i % 2}", 16 * (6 + i // 2), 48)
                        w("f_pe", 7 + i // 2, 12)
                        up_hi(i, w)
            w0 = ffn_waits(act, None, 0, None, 0)
            group(w0, 0, 0, False, False)
            for i in range(4):
                act.wait_ge(S(f"f_ld{i % 2}"), 16 * (3 + i // 2))
                act.wait_ge(S("f_pe"), 3 + i // 2)
                up_hi(i, None)
            T_ = LoopTargets(act, {"f_ld0": (96, 48 + 112), "f_ld1": (96, 48 + 112), "f_pe": (24, 20), "f_free": (24, 20),
                                   "tap2": (8, 12), "cmul": (4, 6)})
            with act.Fori(1, NGRP - 2, 2) as G:
                for par in range(2):
                    group(ffn_waits(act, None, None, T_, par), G + par, 1 - par, True, True)
                T_.end()
            group(ffn_waits(act, None, NGRP - 2, None, 0), NGRP - 2, 1, True, True)
            wl = ffn_waits(act, None, NGRP - 1, None, 0)
            group(wl, NGRP - 1, 0, True, False)
            i = NGRP - 1
            for k in range(2):
                act.wait_ge(S(f"f_ld{k}"), 16 * (5 + 3 * (NGRP - 2) + 1))
                act.wait_ge(S("f_pe"), 4 + 12 * (NGRP - 1))
                act.activation(dhi[:, k, :], fst[:, k], ACT.Copy).then_inc(S("f_hi"), 1)

        @block.vector
        def _(dve):
            chain = [0]

            def link(ins):
                chain[0] += 1
                ins.then_inc(S("dve_chain"), 1)
                dve.wait_ge(S("dve_chain"), chain[0])
            dve.memset(ssx[:, :], 1.0).then_inc(S("dve_set"), 1)
            dve.memset(fa[:, :], 0.0).then_inc(S("dve_set"), 1)
            dve.memset(epsc[:, :], EPS).then_inc(S("dve_set"), 1)
            dve.memset(lmask[:, :], 1.0).then_inc(S("dve_set"), 1)
            dve.wait_ge(S("dve_set"), 4)
            dve.memset(lmask[:, ::PAGES], 0.0).then_inc(S("dve_set"), 1)
            dve.wait_ge(S("const_ld"), 96)
            for s in (0, 2, 4):
                link(dve.tensor_scalar(gq[:, s, :], gq[:, s, :], QSCALE, None, ALU.mult))
            dve.wait_ge(S("tab_ld"), 48)
            for j in range(3):
                w = min(512, NR - 512 * j)
                dve.wait_ge(S("rt_pe"), j + 1)
                dve.tensor_tensor(rtab[:, 512 * j:512 * j + w], ps[0:NH, j, 0:w], clm[:, 512 * j:512 * j + w], ALU.add)\
                    .then_inc(S("rtab"), 1)
            dve.wait_ge(S("rt_pe"), 6)
            for c in range(3):
                n = CROWS[c]
                m = dve.tensor_scalar(bsamp[0:n, c, :], ps[0:n, 3, NH * c:NH * c + NH], cv("lm")[0:n, c:c + 1], None,
                                      ALU.add)
            m.then_inc(S("rtab"), 1)
            dve.wait_ge(S("lft_cp"), 2)
            dve.wait_ge(S("dve_set"), 5)
            flat = lft[:, :, :, :].rearrange("p i h c -> p (i h c)")
            link(dve.tensor_tensor_scan(lscan[:, :], lmask[:, :], flat, 0.0, ALU.mult, ALU.add))
            sc = lscan[:, :].rearrange("p (s g) -> p s g", g=PAGES)
            dve.tensor_tensor(lmask[:, :].rearrange("p (s g) -> p s g", g=PAGES),
                              sc[:, :, PAGES - 1:PAGES].broadcast_to([P, 2 * NH * P // PAGES, PAGES]), sc, ALU.subtract)\
                .then_inc(S("lsuf"), 1)

            def split_lo(q):
                dve.wait_ge(S("w_hi"), q + 1)
                dve.tensor_tensor(wlo[:, q % NW, 0:WID[q // KC]], wst[:, q % 4, 0:WID[q // KC]],
                                  whi[:, q % NW, 0:WID[q // KC]].bitcast(f32), ALU.subtract).then_inc(S("w_split"), 1)

            def x_lo(i):
                dve.wait_ge(S("x_hi"), i + 1)
                if i < 16:
                    c, w, kc, s = slice((i // 8) * 516, (i // 8) * 516 + 516), 516, i % 8, 0
                else:
                    c, w, kc, s = slice(0, NMEM), NMEM, i - 16, 1
                dve.scalar_tensor_tensor(out=hlo[:, kc, c], in0=xslot(i)[:, 0:w], scalar=gain[:, s, kc:kc + 1],
                                         in1=hhi[:, kc, c].bitcast(f32), op0=ALU.mult, op1=ALU.subtract)\
                    .then_inc(S("x_split"), 1)
            for kc in range(KC):
                x_lo(kc)
                split_lo(kc)
            for i in range(8, 16):
                x_lo(i)

            def k_dot(n, b, pg, slot, q, kwait, selfwait):
                kv = ring[:, slot]
                kwait()
                dve.tensor_tensor(kv, kv, q.broadcast_to([P, 4, WG]), ALU.mult).then_inc(S("k_mul"), 1)
                selfwait()
                out = sA[:, b, 4 * pg:4 * pg + 4, :]
                dve.tensor_reduce(out=out, in_=kv.rearrange("p g (h e) -> p (g h) e", e=HD), axis=AX.X, op=ALU.add)\
                    .then_inc(S("k_used"), 1)

            def reduce_sq(k):
                c0, nh, g0 = NORM[k[0]]
                r, i = rows(k), NI[k]
                dve.wait_ge(S("act_z"), UI[k] + 1)
                if i >= 2:
                    dve.wait_ge(S("rs_norm"), i - 1)
                dve.tensor_reduce(out=ssn[0:r, i % 2, 0:nh], in_=sq[0:r, i % 2, 0:nh * HD].rearrange("p (h e) -> p h e", e=HD),
                                  axis=AX.X, op=ALU.add).then_inc(S("ss_dve"), 1)

            def finish_norm(k):
                c0, nh, g0 = NORM[k[0]]
                r, i = rows(k), NI[k]
                dst = zdst(k)[:, c0:c0 + nh * HD]
                dve.wait_ge(S("rs_norm"), i + 1)
                if i >= 1:
                    dve.wait_ge(S("zo_dve"), i)
                z = zview(k)[:, c0:c0 + nh * HD].rearrange("p (h e) -> p h e", e=HD)
                zt = zn[0:r, i % 2, 0:nh * HD].rearrange("p (h e) -> p h e", e=HD)
                dve.scalar_tensor_tensor(out=zt, in0=z, scalar=rsx[0:r, xi(k):xi(k) + 1],
                                         in1=rsn[0:r, i % 2, 0:nh].unsqueeze(2).broadcast_to([r, nh, HD]),
                                         op0=ALU.mult, op1=ALU.mult).then_inc(S("dve_z"), 1)
                if k[1] != "S":
                    wait_zo_free(dve, k)
                dve.wait_ge(S("dve_z"), DI[k] + 1)
                for a in range(nh // NH):
                    w = slice(a * WG, (a + 1) * WG)
                    m = dve.tensor_tensor(dst[:, w].rearrange("p (h e) -> p h e", e=HD),
                                          zn[0:r, i % 2, w].rearrange("p (h e) -> p h e", e=HD),
                                          gq[0:r, g0 + a:g0 + a + 1, :].broadcast_to([r, NH, HD]), ALU.mult)
                m.then_inc(S("zo_dve"), 1)
                if k[1] == "S":
                    dve.wait_ge(S("zo_dve"), i + 1)
                    dve.sem_inc(S("zs_norm"), 1)

            def forget(k):
                r = rows(k)
                dve.wait_ge(S("act_z"), UI[k] + 1)
                if k[1] == "S":
                    out = fa[0:r, 32:36]
                    dve.wait_ge(S("dve_set"), 2)
                else:
                    out = fa[:, 0:32].rearrange("p (h t) -> p t h", t=NT)[:, k[1]]
                dve.scalar_tensor_tensor(out=out, in0=zview(k)[:, WG:WG + NH], scalar=rsx[0:r, xi(k):xi(k) + 1],
                                         in1=pv("bf", r), op0=ALU.mult, op1=ALU.add).then_inc(S("dve_z"), 1)

            def gate(tt):
                k = (2, tt)
                dve.wait_ge(S("sgu_pe"), tt + 1)
                if tt >= 2:
                    dve.wait_ge(S(f"ob_out{tt % 2}"), 16 * (tt // 2))
                for g in range(NH):
                    c = slice(g * HD, (g + 1) * HD)
                    m = dve.scalar_tensor_tensor(out=ob[:, tt % 2, c], in0=ps[:, 7, WG + g * HD:WG + (g + 1) * HD],
                                                 scalar=pv("bs")[:, g:g + 1], in1=zo[:, prompt_no[k] % 4, c],
                                                 op0=ALU.add, op1=ALU.mult)
                m.then_inc(S("ob_ready"), 1)

            dve.wait_ge(S("rs_row"), 1)
            dve.wait_ge(S("x_stat"), 11)
            pending = None
            for u, k in enumerate(units):
                b, tt = k
                for bb, kc in CT[u]:
                    split_lo(bb * KC + kc)
                if b == 4 and tt != "S" and tt >= 2 and tt < 6:
                    for i in (2 * (tt - 2), 2 * (tt - 2) + 1):
                        x_lo(16 + i)
                if b in NORM:
                    reduce_sq(k)
                if b == 1:
                    if pending:
                        finish_norm(pending)
                        pending = None
                    forget(k)
                if pending:
                    finish_norm(pending)
                    pending = None
                if b in NORM:
                    pending = k
                if k == (1, NT - 1):
                    dve.wait_ge(S("dve_z"), DI[k] + 1)
                    dve.scalar_tensor_tensor(out=fb[:, :], in0=fa[:, :], scalar=-1.0, in1=fa[:, :], op0=ALU.mult,
                                             op1=ALU.min).then_inc(S("forget"), 1)
                if k == (2, "S"):
                    dve.wait_ge(S("fb_act"), 2)
                    dve.scalar_tensor_tensor(out=lf[:, :], in0=fa[:, :], scalar=0.0, in1=fb[:, :], op0=ALU.min,
                                             op1=ALU.subtract).then_inc(S("forget"), 1)
                    dve.wait_ge(S("forget"), 2)
                    dve.tensor_tensor_scan(npre[:, :], cv("rs"), lf[:, 0:32], 0.0, ALU.mult, ALU.subtract)\
                        .then_inc(S("forget"), 1)
                if k == (2, 1):
                    dve.wait_ge(S("csum_pe"), 1)
                    dve.tensor_copy(fb[:, 0:32], ps[:, 7, 0:32]).then_inc(S("forget"), 1)
                if k == (3, 0):
                    for t7 in (6,):
                        gate(t7)
                if b == 2 and tt not in ("S", 0, 1, 2):
                    gate(tt - 3)
                if k == (3, "S"):
                    gate(5)
                if k == (3, 1):
                    gate(7)
                if k in kgran:
                    n = kgran[k]

                    def kw(n=n):
                        dve.wait_ge(S("qb_ld"), 16)
                        dve.wait_ge(S(f"ring_ld{n % 4}"), ring_total(n))
                    k_dot(n, n // 8, n % 8, n % 4, qb[:, n // 8:n // 8 + 1, :], kw, lambda: dve.wait_ge(S("k_mul"), n + 1))
            finish_norm(pending)

            for s_ in range(4):
                uses = [k for k in prompt_no if prompt_no[k] % 4 == s_]
                dve.wait_ge(S(f"zo_out{s_}"), 16 * sum(0 if k[0] == 2 else n_out[k[0]] for k in uses))
            dve.wait_ge(S("ob_out0"), 64)
            dve.wait_ge(S("ob_out1"), 64)
            dve.wait_ge(S("z_done"), NU)
            dve.memset(qT[HD:HD + 1, :, :], 1.0).then_inc(S("dve_set"), 1)
            dve.memset(vst[:, :, :, HD:HD + 1], 1.0).then_inc(S("dve_set"), 1)

            def attention(A):
                n, two = A["n"], A["bias"]
                last = {n + "_prep": (2, 2), n + "_qk": (16, 16), n + "_pv": (16, 18), n + "_rc": (16, 16)}
                if two:
                    last.update({n + "_tpa": (16, 16), n + "_tpb": (8, 9), n + "_lg": (16, 18),
                                 "k_mul": (8, NKP + 8), "ring_ld0": (128, RK[0] + 128), "ring_ld1": (128, RK[1] + 128),
                                 "ring_ld2": (128, RK[2] + 128), "ring_ld3": (128, RK[3] + 128)})
                else:
                    last[n + "_exp"] = (16, 16)
                T_ = LoopTargets(dve, last)
                dve.sem_inc(S(n + "_o"), 2)
                if two:
                    dve.sem_inc(S(n + "_lg"), 2)
                    dve.sem_inc(S(n + "_evb"), 1)
                with dve.Fori(0, A["iters"]) as it:
                    for par in range(2):
                        T_.wait(n + "_prep", par + 1)
                        w = P * A["nk"]
                        dve.tensor_copy(kT[0:HD, par, 0:w], SBANK(1)[0:HD, 0:w]).then_inc(S(n + "_kT"), 1)

                        def score(s):
                            g, W = 8 * par + s, P * A["blocks"][s]
                            T_.wait(n + "_qk", g + 1)
                            if two:
                                T_.wait(n + "_tpb", 4 * par + min(max(s - 1, 0), 4) + 1)
                                dve.wait_ge(S("const_ld"), 96)
                                T_.wait(n + "_tpa", g + 1)
                                dve.tensor_tensor_reduce(out=lg[:, s % 2, 0:W], in0=SBANK(s % 2)[:, 0:W],
                                                         in1=toe[:, par, SEQ - W:SEQ], scale=1.0, scalar=-3.0e38,
                                                         op0=ALU.add, op1=ALU.max, accum_out=nm[:, s % 2, 0:1])\
                                    .then_inc(S(n + "_lg"), 1)
                                T_.wait(n + "_lg", g + 3)
                                dve.tensor_scalar(nm[:, s % 2, 1:2], nm[:, s % 2, 0:1], -1.0, None, ALU.mult)\
                                    .then_inc(S(n + "_nm"), 1)
                            else:
                                T_.wait(n + "_exp", g + 1)
                                dve.tensor_reduce(out=nm[:, s % 2, 1:2], in_=SBANK(s % 2)[:, 0:W], axis=AX.X,
                                                  op=ALU.max, negate=True).then_inc(S(n + "_nm"), 1)

                        def evb(s):
                            nb = A["blocks"][s]
                            if nb > 4:
                                T_.wait(n + "_tpb", 4 * par + s + 2)
                                T_.wait(n + "_pv", 8 * par + s + 1)
                                dve.tensor_copy(pts[:, s % 2, 4:nb, :].rearrange("p b c -> p (b c)"),
                                                ps[:, 5, 0:(nb - 4) * P]).then_inc(S(n + "_evb"), 1)

                        def out(s):
                            g = 8 * par + s
                            T_.wait(n + "_pv", g + 3)
                            dve.reciprocal(rc[:, s % 2:s % 2 + 1], ps[:, 6 + s % 2, HD:HD + 1]).then_inc(S(n + "_rc"), 1)
                            T_.wait(n + "_rc", g + 1)
                            col = bass.ds(it * (2 * HD) + (par * HD + (0 if two else 3 * WG)), HD)
                            dve.tensor_scalar(oN[:, A["tile"][s], col], ps[:, 6 + s % 2, 0:HD], rc[:, s % 2:s % 2 + 1],
                                              None, ALU.mult).then_inc(S(n + "_o"), 1)

                        def granule(s):
                            j = par * 4 + s // 2
                            bq = qb[:, bass.ds(it + 4, 1), :]
                            slot = j % 4
                            k_dot(None, bass.ds(it + 4, 1), j, slot, bq,
                                  lambda: T_.wait(f"ring_ld{slot}", RK[slot] + 64 * (j // 4 + 1)),
                                  lambda: T_.wait("k_mul", NKP + j + 1))
                        score(0)
                        score(1)
                        evb(0)
                        for s in range(2, NT):
                            if two and s % 2 == 1:
                                granule(s - 2)
                            score(s)
                            evb(s - 1)
                            out(s - 2)
                        if two:
                            granule(NT - 1)
                        out(NT - 2)
                        out(NT - 1)
                    T_.end()
            RK = [ring_total(NKP - 4 + s4) for s4 in range(4)]
            attention(AC)

            def gview(g):
                if g == 0:
                    return sA[:, :, :, :].rearrange("p b g h -> p b h g")
                return (sC if g == 1 else sM)[:, :, :, :].rearrange("p c b h -> p b h c")

            def maxima(g):
                pm = small[:, g, 0:32].rearrange("p (b h) -> p b h", b=8)
                dve.tensor_reduce(out=pm, in_=gview(g), axis=AX.X, op=ALU.max).then_inc(S("pm"), 1)
                if g < 2:
                    qo, ko = (0, WG) if g == 0 else (BLK[3][0], BLK[3][0] + WG)
                    sn = small[0:8, g, 128:132]
                    dve.wait_ge(S("zs_norm"), 3)
                    link(dve.tensor_tensor(prod8[:, 0, :], zs[:, qo:qo + WG], zs[:, ko:ko + WG], ALU.mult))
                    link(dve.tensor_reduce(out=sn, in_=prod8[:, 0, :].rearrange("p (h e) -> p h e", e=HD), axis=AX.X,
                                           op=ALU.add))
                    if g == 0:
                        link(dve.tensor_tensor(sn, sn, lf[0:8, 32:36], ALU.subtract))
                    else:
                        link(dve.scalar_tensor_tensor(out=sn, in0=pv("rb0", 8), scalar=float(np.float32(math.log(3.0))),
                                                      in1=sn, op0=ALU.add, op1=ALU.add))
                    d = small[0:8, g, 96:128].rearrange("p (b h) -> p b h", b=8)
                    link(dve.tensor_tensor(d, sn.unsqueeze(1).broadcast_to([8, 8, NH]),
                                           cv("dm", 8).rearrange("p (b h) -> p b h", b=8), ALU.add))
                    dve.wait_ge(S("pm"), 2 * g + 1)
                    dve.tensor_tensor(small[0:8, g, 0:32], small[0:8, g, 0:32], small[0:8, g, 96:128], ALU.max)\
                        .then_inc(S("pm"), 1)

            def subtract(g):
                dve.wait_ge(S("gmax"), g + 1)
                m = small[:, g, 64:96]
                if g == 0:
                    mb = m.rearrange("p (b h) -> p b h", b=8)
                    for b in range(8):
                        i = dve.tensor_tensor(sA[:, b], sA[:, b], mb[:, b:b + 1, :].broadcast_to([P, PAGES, NH]), ALU.subtract)
                    i.then_inc(S("sub"), 1)
                else:
                    s_ = sC if g == 1 else sM
                    nc_ = 3 if g == 1 else 2
                    v = s_[:, :, :, :].rearrange("p c b h -> p c (b h)")
                    dve.tensor_tensor(v, v, m.unsqueeze(1).broadcast_to([P, nc_, 32]), ALU.subtract)\
                        .then_inc(S("sub"), 1)
                if g < 2:
                    t3 = small[0:8, g, 96:128]
                    dve.wait_ge(S("pm"), 2 * g + 2)
                    link(dve.tensor_tensor(t3, small[0:8, g, 64:96], cv("e8", 8), ALU.mult))
                    link(dve.tensor_reduce(out=small[0:8, g, 132:136], in_=t3.rearrange("p (b h) -> p h b", b=8), axis=AX.X,
                                           op=ALU.add))
                    dve.tensor_tensor(small[0:8, g, 136:140], small[0:8, g, 128:132], small[0:8, g, 132:136], ALU.subtract)\
                        .then_inc(S("sub"), 1)

            def key_sums(g):
                dve.wait_ge(S("e_act"), g + 1)
                dve.tensor_reduce(out=small[:, g, 32:64].rearrange("p (b h) -> p b h", b=8), in_=gview(g), axis=AX.X,
                                  op=ALU.add).then_inc(S("esum"), 1)

            dve.wait_ge(S("k_used"), NKA)
            dve.wait_ge(S("lft_cp"), 4)
            link(dve.tensor_tensor(sA[:, :, :, :].rearrange("p b g h -> p (b g h)"),
                                   sA[:, :, :, :].rearrange("p b g h -> p (b g h)"),
                                   biasA[:, :, :, :].rearrange("p b g h -> p (b g h)"), ALU.add))
            maxima(0)
            subtract(0)
            attention(MM)
            dve.wait_ge(S("mm_pv"), 2 + 32)
            dve.memset(sso[:, :], 1.0).then_inc(S("dve_set"), 1)
            dve.memset(sC[:, :, :, :], NEG).then_inc(S("dve_set"), 1)
            dve.wait_ge(S("dve_set"), 9)
            for i, (g, c, b0) in enumerate(cm):
                n = NKA + i
                nk = CROWS[c] if g == DIL else P
                kv = ring[0:nk, n % 4]
                dve.wait_ge(S("qb_ld"), 32 if g == DIL else 48)
                dve.wait_ge(S(f"ring_ld{n % 4}"), ring_total(n))
                dve.tensor_tensor(kv, kv, qb[0:nk, b0:b0 + 4, :], ALU.mult).then_inc(S("k_mul"), 1)
                dve.wait_ge(S("k_mul"), n + 1)
                dst = (sC if g == DIL else sM)[0:nk, c, b0:b0 + 4, :]
                dve.tensor_reduce(out=dst, in_=kv.rearrange("p b (h e) -> p (b h) e", e=HD),
                                  axis=AX.X, op=ALU.add).then_inc(S("k_used"), 1)
            dve.wait_ge(S("k_used"), NKA + NCM)
            for c in range(3):
                nk = CROWS[c]
                m = dve.tensor_tensor(sC[0:nk, c], sC[0:nk, c], bsamp[0:nk, c:c + 1, :].broadcast_to([nk, 8, NH]), ALU.add)
            link(m)
            maxima(1)
            maxima(2)
            subtract(1)
            subtract(2)
            key_sums(0)
            m4 = cv("m4", 4)
            dve.sem_inc(S("acc_cp"), 1)
            T_ = LoopTargets(dve, {"v_used": (8, 16)})
            with dve.Fori(0, NSAMP) as b:
                T_.wait("v_used", 16)
                dve.tensor_tensor(mkd[:, 0, bass.ds(b, 1), :].rearrange("p o c -> p (o c)"), ps[0:NH, 0, 0:WG], m4, ALU.mult)\
                    .then_inc(S("acc_cp"), 1)
                T_.end()
            for i, (grp, done) in enumerate(((1, 3), (1, 6), (2, 8), (2, 10))):
                dve.wait_ge(S("v_used"), 8 + NKA + done)
                dve.tensor_tensor(mkd[:, grp, 4 * (i % 2):4 * (i % 2) + 4, :], ps[0:NH, 0:4, 0:WG],
                                  m4.unsqueeze(1).broadcast_to([4, 4, WG]), ALU.mult).then_inc(S("acc2_cp"), 1)
            key_sums(1)
            key_sums(2)
            dve.wait_ge(S("rs_row"), 2)
            for tt in range(NT):
                v = oN[:, tt, :].rearrange("p (g c) -> p g c", g=4)
                dve.tensor_tensor(v, v, rso[:, 4 * tt:4 * tt + 4].unsqueeze(2).broadcast_to([P, 4, WG]), ALU.mult)\
                    .then_inc(S("o_scaled"), 1)
            u_, v_ = zs[:, BLK[2][0]:BLK[2][0] + WG], zs[:, BLK[2][0] + WG:BLK[2][0] + 2 * WG]

            def by_head(ap):
                return ap.rearrange("p (h e) -> p h e", e=HD)

            def bc(ap):
                return ap.unsqueeze(2).broadcast_to([8, NH, HD])
            link(dve.tensor_tensor(by_head(prod8[:, 1, :]), by_head(v_), bc(pv("w00", 8)), ALU.mult))
            link(dve.tensor_tensor(by_head(prod8[:, 1, :]), by_head(prod8[:, 1, :]), bc(pv("b0", 8)), ALU.add))
            dve.tensor_tensor(oS[:, 2, :], prod8[:, 1, :], u_, ALU.mult).then_inc(S("oS"), 1)
            dve.wait_ge(S("oS"), 1)
            dve.wait_ge(S("samp_pe"), 1)
            for g, pos, vo in ((0, 0, 2 * WG + 0), (1, 1, BLK[4][0]), (2, 3, None)):
                acc = ps[0:8, 4 + (g > 1), WG * (g % 2):WG * (g % 2) + WG]
                den = ps[0:8, 6, 8 * g:8 * g + 4]
                dd, rd = small[0:8, g, 140:144], small[0:8, g, 144:148]
                if g < 2:
                    dve.wait_ge(S("e_act"), 3 + g + 1)
                    en = small[0:8, g, 136:140]
                    link(dve.tensor_tensor(dd, den, en, ALU.add))
                    link(dve.reciprocal(rd, dd))
                    vv = zs[:, 512:768] if g == 0 else zs[:, vo:vo + WG]
                    link(dve.tensor_tensor(by_head(prod8[:, 0, :]), by_head(vv), bc(en), ALU.mult))
                    link(dve.tensor_tensor(prod8[:, 0, :], prod8[:, 0, :], acc, ALU.add))
                    dve.tensor_tensor(by_head(oS[:, pos, :]), by_head(prod8[:, 0, :]), bc(rd), ALU.mult)\
                        .then_inc(S("oS"), 1)
                    dve.wait_ge(S("oS"), g + 2)
                else:
                    link(dve.reciprocal(rd, den))
                    dve.tensor_tensor(by_head(oS[:, pos, :]), by_head(acc), bc(rd), ALU.mult).then_inc(S("oS"), 1)

            for x, tt in enumerate(list(range(NT)) + ["S"]):
                r = NSAMP if tt == "S" else P
                c0 = 0 if tt == "S" else NSAMP + tt * P
                if tt == "S":
                    dve.wait_ge(S("rs_row"), 3)
                    dve.wait_ge(S("oS"), 4)
                    dve.tensor_tensor(oS[:, :, :], oS[:, :, :], rso[0:8, 32:36].unsqueeze(2).broadcast_to([8, 4, WG]), ALU.mult)\
                        .then_inc(S("o_scaled"), 1)
                    dve.wait_ge(S("o_scaled"), 9)
                dve.wait_ge(S("o_hi"), x + 1)
                dve.tensor_tensor(hlo[:, :, c0:c0 + r], SBANK(x % 2)[:, 0:KC * r].rearrange("p (k c) -> p k c", k=KC),
                                  hhi[:, :, c0:c0 + r].bitcast(f32), ALU.subtract).then_inc(S("o_lo"), 1)

            def w_out(d):
                dve.wait_ge(S(f"wo_ld{d % 2}"), 16 * (d // 2 + 1))
                g = gain[:, 2, :].unsqueeze(2).broadcast_to([P, KC, P])
                dve.tensor_tensor(wost[:, d % 2], wost[:, d % 2], g, ALU.mult).then_inc(S("wo_gain"), 1)

            def w_out_lo(d):
                dve.wait_ge(S("wo_hi"), d + 1)
                dve.tensor_tensor(wolo[:, d % 2], wost[:, d % 2], wohi[:, d % 2].bitcast(f32), ALU.subtract)\
                    .then_inc(S("wo_split"), 1)

            def add_x(d):
                dve.wait_ge(S("out_pe"), d + 1)
                dve.wait_ge(S("x2_ld"), 16 * (KC + 1))
                dve.tensor_tensor(c3(x2[:, d, :]), U3(d % 2), c3(x2[:, d, :]), ALU.add).then_inc(S("x2_add"), 1)

            def add_sq(d):
                dve.wait_ge(S("sqx"), d + 1)
                if d == 0:
                    dve.tensor_copy(sacc[:, :], sqx[:, :]).then_inc(S("sacc"), 1)
                else:
                    dve.wait_ge(S("sacc"), d)
                    dve.tensor_tensor(sacc[:, :], sacc[:, :], sqx[:, :], ALU.add).then_inc(S("sacc"), 1)
            w_out(0)
            w_out(1)
            w_out_lo(0)
            w_out_lo(1)
            for d in range(KC):
                add_x(d)
                if d >= 1:
                    add_sq(d - 1)
                if d + 2 < KC:
                    w_out(d + 2)
                    w_out_lo(d + 2)
            for kc in range(KC):
                dve.wait_ge(S("h2_hi"), kc + 1)
                dve.scalar_tensor_tensor(out=hlo[:, kc, :], in0=x2[:, kc, :], scalar=gain[:, 3, kc:kc + 1],
                                         in1=hhi[:, kc, :].bitcast(f32), op0=ALU.mult, op1=ALU.subtract)\
                    .then_inc(S("h2_split"), 1)
                if kc == 0:
                    add_sq(KC - 1)

            def bt(a):
                return a.unsqueeze(2).broadcast_to([P, 2 * FT, NSAMP])
            tmp = u10[:, :, 10:18]
            dve.wait_ge(S("x2_ld"), 16 * (KC + 1))
            link(dve.tensor_tensor(sbase[:, :, :], stT[:, :, 0, :], bt(conv[:, 0, :]), ALU.mult))
            link(dve.tensor_tensor(tmp, stT[:, :, 1, :], bt(conv[:, 1, :]), ALU.mult))
            link(dve.tensor_tensor(sbase[:, :, :], sbase[:, :, :], tmp, ALU.add))
            link(dve.tensor_tensor(sbase[:, :, :], sbase[:, :, :], bt(conv[:, 3, :]), ALU.add))
            link(dve.tensor_copy(u10[:, :, 10:18], stT[:, :, 1, :]))

            def up_lo(i):
                half, q4 = i // 2, i % 2
                v = (slice(None), half, slice(4 * q4, 4 * q4 + 4))
                dve.tensor_tensor(ulo[v].rearrange("p k c -> p (k c)"), fst[:, i % 2],
                                  uhi[v].rearrange("p k c -> p (k c)").bitcast(f32), ALU.subtract).then_inc(S("f_split"), 1)
            for p in range(4):
                dve.wait_ge(S("f_hi"), p + 1)
                up_lo(p)
            dve.wait_ge(S("ms_cp"), 1)
            link(dve.reciprocal(rstd_bc[:, :], rstd_bc[:, :]))

            def fts(G, half, j):
                if isinstance(G, int):
                    return slice(half * FT + 2 * G + j, half * FT + 2 * G + j + 1)
                return bass.ds(G * 2 + (half * FT + j), 1)

            def unit(w, G, k, ft, between=None):
                cb = convA if k % 2 == 0 else convG
                if k > 0 or not isinstance(G, int) or G > 0:
                    w("tap2", 4 + k, 4)
                w("f_pe", 4 + k + 1, 12)
                dve.tensor_tensor(c3(uu[:, :]), U3(k % 2), c3(rstd_bc[:, :]), ALU.mult).then_inc(S("f_free"), 1)
                w("f_free", 4 + k + 1, 12)
                dve.tensor_copy(u10[:, ft, 0:2], uu[:, COLS - 2:COLS].unsqueeze(1))
                dve.tensor_copy(u10[:, ft, 2:10], uu[:, 0:NSAMP].unsqueeze(1))
                dve.scalar_tensor_tensor(out=cb[:, 0:NSAMP], in0=uu[:, 0:NSAMP], scalar=conv[:, 2, ft],
                                         in1=sbase[:, ft, :].rearrange("p o b -> p (o b)"), op0=ALU.mult, op1=ALU.add)\
                    .then_inc(S("c_samp"), 1)
                w("c_samp", 4 + k + 1, 4)
                dve.memset(uu[:, NSAMP - 2:NSAMP], 0.0).then_inc(S("c_pad"), 1)
                w("c_pad", 4 + k + 1, 4)
                w("aff", 4 + k + 1, 4)
                pc = cb[:, NSAMP:COLS]
                dve.scalar_tensor_tensor(out=pc, in0=uu[:, NSAMP - 1:COLS - 1], scalar=conv[:, 1, ft], in1=pc,
                                         op0=ALU.mult, op1=ALU.add).then_inc(S("tap1"), 1)
                if between:
                    between()
                w("tap1", 4 + k + 1, 4)
                dve.scalar_tensor_tensor(out=pc, in0=uu[:, NSAMP - 2:COLS - 2], scalar=conv[:, 0, ft], in1=pc,
                                         op0=ALU.mult, op1=ALU.add).then_inc(S("tap2"), 1)

            def gated(w, j, gp, between=None):
                w("silu", 2 + j + 1, 2)
                w("tap2", 4 + 2 * j + 2, 4)
                dve.tensor_tensor(convA[:, :], convA[:, :], convG[:, :], ALU.mult).then_inc(S("cmul"), 1)
                if between:
                    between()
                w("a_hi", 2 + j + 1, 2)
                dve.tensor_tensor(alo[:, gp, j, :], convA[:, :], ahi[:, gp, j, :].bitcast(f32), ALU.subtract)\
                    .then_inc(S("a_split"), 1)
                w("a_split", 2 + j + 1, 2)

            def add_down(w, d, G=None):
                w("f_pe", 8 + d + 1, 12)
                dve.tensor_tensor(c3(x2[:, d, :]), U3(d % 2), c3(x2[:, d, :]), ALU.add).then_inc(S("f_free"), 1)

            def group(w, G, gp, downs, ups):
                for k in range(4):
                    if downs and k < 2:
                        w("f_hi", 8 + k + 1, 6)
                        dve.tensor_tensor(dlo[:, k, :], fst[:, k], dhi[:, k, :].bitcast(f32), ALU.subtract)\
                            .then_inc(S("f_split"), 1)
                    if k == 2:
                        gated(w, 0, gp)
                    unit(w, G, k, fts(G, k % 2, k // 2), (lambda: add_down(w, 0)) if downs and k == 3 else None)
                if downs:
                    add_down(w, 1)
                gated(w, 1, gp, (lambda: add_down(w, 2)) if downs else None)
                if downs:
                    for d in range(3, KC):
                        add_down(w, d)
                        if ups and d < KC - 1:
                            w("f_hi", 10 + d - 2, 6)
                            up_lo(d - 3)
            w0 = ffn_waits(dve, None, 0, None, 0)
            group(w0, 0, 0, False, False)
            for i in range(4):
                dve.wait_ge(S("f_hi"), 4 + i + 1)
                up_lo(i)
            T_ = LoopTargets(dve, {"f_pe": (24, 28), "f_free": (24, 20), "c_samp": (8, 12), "c_pad": (8, 12), "aff": (8, 12),
                                   "tap1": (8, 12), "tap2": (8, 12), "silu": (4, 6), "a_hi": (4, 6), "a_split": (4, 6),
                                   "f_hi": (12, 20)})
            with dve.Fori(1, NGRP - 2, 2) as G:
                for par in range(2):
                    group(ffn_waits(dve, None, None, T_, par), G + par, 1 - par, True, True)
                T_.end()
            group(ffn_waits(dve, None, NGRP - 2, None, 0), NGRP - 2, 1, True, True)
            group(ffn_waits(dve, None, NGRP - 1, None, 0), NGRP - 1, 0, True, False)
            for k in range(2):
                dve.wait_ge(S("f_hi"), 8 + 6 * (NGRP - 2) + 2 + k + 1)
                dve.tensor_tensor(dlo[:, k, :], fst[:, k], dhi[:, k, :].bitcast(f32), ALU.subtract).then_inc(S("f_split"), 1)
            for d in range(KC):
                dve.wait_ge(S("f_pe"), 4 + 12 * (NGRP - 1) + d + 1)
                dve.tensor_tensor(c3(x2[:, d, :]), U3(d % 2), c3(x2[:, d, :]), ALU.add).then_inc(S("f_free"), 1)

        @block.gpsimd
        def _(pool):
            pool.memset(nhalf[:, :], -0.5).then_inc(S("pool_chain"), 1)
            pool.wait_ge(S("const_ld"), 96)
            for i in range(2):
                pool.indirect_dma_start(out=lfp[:, i, :], out_offset=None, in_=lfpool,
                                        in_offset=bass.IndirectOffsetOnAxis(ap=pidx[:, i:i + 1], axis=0))\
                    .then_inc(S("lfp_ld"), 16)
            pool.wait_ge(S("const_ld"), 96)
            pool.affine_select(out=wsT[:, :, :], in_=wsT[:, :, :], compare_op=ALU.is_ge, fill=0.0, base=0,
                               pattern=[[0, NH], [1, P]], channel_multiplier=-1).then_inc(S("ws_mask"), 2)
            chain = [1]

            def inverse_rms(out, src, width, done, value):
                r = src.shape[0]
                n = src.shape[1]
                pool.tensor_scalar(out, src, 1.0 / width, EPS, ALU.mult, ALU.add).then_inc(S("pool_chain"), 1)
                chain[0] += 1
                pool.wait_ge(S("pool_chain"), chain[0])
                pool.tensor_tensor(out, out, nhalf[0:r, 0:n], ALU.pow).then_inc(S(done), 1)
            pool.wait_ge(S("x_stat"), 11)
            inverse_rms(rsx[:, :], ssx[:, :], DM, "rs_row", 1)
            for k in norm_units:
                i, r, nh = NI[k], rows(k), NORM[k[0]][1]
                pool.wait_ge(S("ss_dve"), i + 1)
                if i >= 2:
                    pool.wait_ge(S("zo_dve"), i - 1)
                inverse_rms(rsn[0:r, i % 2, 0:nh], ssn[0:r, i % 2, 0:nh], HD, "rs_norm", i + 1)
            for g in range(3):
                pool.wait_ge(S("pm"), (2, 4, 5)[g])
                pool.partition_all_reduce(small[:, g, 64:96], small[:, g, 0:32], P, RMAX).then_inc(S("gmax"), 1)
            pool.wait_ge(S("o_sq"), 4 + 32)
            inverse_rms(rso[:, 0:32], sso[:, 0:32], WG, "rs_row", 2)
            pool.wait_ge(S("o_sq"), 4 + 36)
            inverse_rms(rso[0:8, 32:36], sso[0:8, 32:36], WG, "rs_row", 3)


def kernel(x_prompt, x_sample, mem_prompt, cache_a_k, cache_a_v, cache_a_logf, cache_c_k, cache_c_v,
           cache_mem_k, cache_mem_v, state_ffn_conv, page_table, norm_mix, w_in, b_forget, qk_gain,
           w_spatial, b_spatial, rel_bias, norm_mem, w_mem_kv, norm_out, w_out, norm_ffn, w_up,
           conv_w, conv_b, w_down):
    import concourse.bacc as bacc
    from concourse.bass_utils import run_bass_kernel_spmd as run

    a = lambda x: np.asarray(x)
    xp, xs, mem = a(x_prompt)[0], a(x_sample)[:, 0], a(mem_prompt)[0]
    fmaj = lambda x: x.T.reshape(KC, P, -1).transpose(1, 0, 2)
    vec = lambda v: a(v).reshape(-1, P).T
    order = [0, 1, 4, 5, 2, 3, 6, 7]
    state = a(state_ffn_conv)[0].reshape(NSAMP, 2, 2 * FT, P).transpose(3, 2, 1, 0)
    wide = lambda v: np.broadcast_to(a(v).reshape(1, -1), (P, a(v).size))
    cw, cb = a(conv_w)[0], a(conv_b)[0]
    prm = np.concatenate([
        vec(cw[0]), vec(cw[1]), vec(cw[2]), vec(cb),
        vec(norm_mix), vec(norm_mem), vec(norm_out)[:, order], vec(norm_ffn),
        wide(a(qk_gain)[0]), a(b_spatial)[0].T, wide(b_forget),
        wide(a(w_spatial)[0, :, 0, 0]), wide(a(b_spatial)[0, :, 0]), wide(a(rel_bias)[0])], 1)
    wu = a(w_up)[0].reshape(2, 4, P, 2, NGRP, 256)
    arrays = {
        "xT": fmaj(np.concatenate([xs, xp], 0)), "memT": fmaj(mem), "x_prompt": xp, "x_sample": xs, "mem": mem,
        "cache_a_k": a(cache_a_k), "cache_a_v": a(cache_a_v), "cache_a_logf": a(cache_a_logf),
        "cache_c_k": a(cache_c_k), "cache_c_v": a(cache_c_v), "cache_mem_k": a(cache_mem_k), "cache_mem_v": a(cache_mem_v),
        "ptab": a(page_table).reshape(1, -1), "pidx": a(page_table).reshape(2, P).T,
        "prm": prm, "stT": state, "w_in": a(w_in), "w_mem": a(w_mem_kv), "wsT": a(w_spatial)[0].transpose(2, 0, 1),
        "rel_bias": a(rel_bias),
        "w_outL": a(w_out)[0].reshape(KC, P, KC, P)[order].transpose(2, 1, 0, 3),
        "w_upL": wu.transpose(4, 3, 0, 2, 1, 5).reshape(NGRP, 2, 2, P, 4 * 256),
        "w_down": a(w_down)[0].reshape(FT, P, DM),
    }
    arrays.update(host_constants())
    outs = {"o_yT": (P, KC, COLS), "o_ka": (SEQ, WG), "o_va": (SEQ, WG), "o_lf": (P, 36), "o_kc": (SEQ, WG),
            "o_vc": (SEQ, WG), "o_mk": (NMEM, WG), "o_mv": (NMEM, WG), "o_zs": (NSAMP, 2308), "o_u10": (P, 2 * FT, 18)}
    nc = bacc.Bacc("TRN2", target_bir_lowering=False, num_devices=1)
    feed, t = {}, {}
    for name, x in arrays.items():
        x = np.ascontiguousarray(x)
        feed[f"in_{name}"] = x
        t[name] = nc.dram_tensor(f"in_{name}", x.shape, mybir.dt.from_np(x.dtype), kind="ExternalInput").ap()
    for name, shape in outs.items():
        t[name] = nc.dram_tensor(name, shape, mybir.dt.float32, kind="ExternalOutput").ap()
    build(nc, t)
    r = run(nc, [feed], core_ids=[0]).results[0]

    y = r["o_yT"].transpose(2, 1, 0).reshape(COLS, DM)
    zs, lf, u = r["o_zs"], r["o_lf"], r["o_u10"].transpose(2, 1, 0).reshape(18, 2 * DFF)
    heads = lambda x, lead: x.reshape((1,) + lead + (NH, HD))
    return (y[NSAMP:].reshape(1, SEQ, DM), y[:NSAMP].reshape(NSAMP, 1, DM),
            heads(r["o_ka"], (1, SEQ)), heads(r["o_va"], (1, SEQ)),
            lf[:, 0:32].reshape(P, NH, NT).transpose(2, 0, 1).reshape(1, 1, SEQ, NH),
            heads(r["o_kc"], (1, SEQ)), heads(r["o_vc"], (1, SEQ)),
            heads(r["o_mk"], (1, NMEM)), heads(r["o_mv"], (1, NMEM)), u[0:2].reshape(1, 1, 2, 2 * DFF),
            heads(zs[:, 256:512], (NSAMP, 1)), heads(zs[:, 512:768], (NSAMP, 1)), lf[0:8, 32:36].reshape(1, NSAMP, 1, NH),
            heads(zs[:, 1540:1796], (NSAMP, 1)), heads(zs[:, 1796:2052], (NSAMP, 1)),
            zs[:, 1028:1284].reshape(1, NSAMP, 1, WG),
            np.stack([u[10:18], u[2:10]], 1).reshape(1, NSAMP, 2, 2 * DFF))
```

```python
import math
import numpy as np
import concourse.bass as bass
from concourse import mybir
from concourse.alu_op_type import AluOpType as ALU
from contextlib import ExitStack

P = 128
DM, SEQ, NSAMP, NMEM = 1024, 1024, 8, 256
COLS = NSAMP + SEQ
KC = DM // P
NT = SEQ // P
WG, HD, NH = 256, 64, 4
DFF = 2816
FT = DFF // P
NGRP = FT // 2
PAGES, PSZ, NPOOL = 32, 128, 320
EPS, NEG = 1e-6, -1e30
QSCALE = 1.0 / math.sqrt(HD)
BR = ((128, 1), (512, 4), (2048, 16))
CH = 344
NR = 2 * SEQ - 1 + P - SEQ
BLK = [(0, 512), (512, 260), (772, 512), (1284, 512), (1796, 512)]
ATT, DIL, MEMG = 0, 1, 2


def bucket(d):
    d = np.asarray(d)
    df = np.maximum(d, 1).astype(np.float32)
    large = 16 + (np.log(df / np.float32(16)) / np.float32(math.log(128.0)) * np.float32(16)).astype(np.int32)
    return np.where(d < 16, d, np.minimum(large, 31))


def branches_at(d):
    return sum(((d % dil) == 0) & (d <= win) for win, dil in BR)


def samp_dist():
    return [np.arange(128, 0, -1), 4 * np.arange(128, 32, -1), 16 * np.arange(128, 32, -1)]


def host_constants():
    c = {}
    r = np.arange(P)
    parts = [np.eye(P), np.ones((P, P)), (r[:, None] > r[None, :])]
    lm = np.full((P, 3), 0.0)
    for j, d in enumerate(samp_dist()):
        lm[:len(d), j] = np.log(branches_at(d))
    dm = np.full((P, 8, 4), NEG); e8 = np.zeros((P, 8, 4))
    for b in range(8):
        dm[b, b] = 0.0; e8[b, b] = 1.0
    rs = np.ones((P, 4, NT)); rs[:, :, 0] = 0.0
    parts += [lm, dm.reshape(P, 32), e8.reshape(P, 32), rs.reshape(P, 32)]
    c["ca"] = np.concatenate([np.asarray(p, np.float32) for p in parts], 1)
    d = SEQ - 1 - np.arange(NR)
    oh = np.zeros((32, NR + 320), np.float32)
    ok = d >= 0
    oh[bucket(d[ok]), np.nonzero(ok)[0]] = 1.0
    sd = np.concatenate(samp_dist())
    oh[bucket(sd), NR + np.arange(320)] = 1.0
    n = np.where(ok, branches_at(np.maximum(d, 0)), 0)
    row = np.where(n > 0, np.log(np.maximum(n, 1)), NEG).astype(np.float32)
    c["coh"] = oh
    c["clm"] = np.tile(row[None], (4, 1)).astype(np.float32)
    c["cmask"] = np.tile(np.where(ok, 0.0, NEG).astype(np.float32)[None], (4, 1))
    return c


CA = {}
_o = 0
for _n, _w in (("id", P), ("one", P), ("u", P), ("lm", 3), ("dm", 32), ("e8", 32), ("rs", 32)):
    CA[_n] = (_o, _o + _w)
    _o += _w
CA_W = _o
PR = {}
_o = 0
for _n, _w in (("conv", 4 * 2 * FT), ("gain", 4 * KC), ("g", 6 * HD), ("bs", 4), ("bf", 4),
               ("w00", 4), ("b0", 4), ("rb0", 4)):
    PR[_n] = (_o, _o + _w)
    _o += _w
PR_W = _o


def build(nc, t):
    f32, f32r, i32 = mybir.dt.float32, mybir.dt.float32r, mybir.dt.int32
    ACT = mybir.ActivationFunctionType
    AX = mybir.AxisListType
    RMAX = bass.bass_isa.ReduceOp.max
    ctx = ExitStack()
    with ctx:
        base = (nc.sbuf_base + 31) // 32 * 32
        end = 229344
        cur = [base]

        def at(name, shape, dt=f32, off=None):
            size = int(np.prod(shape[1:])) * 4
            size = (size + 31) // 32 * 32
            o = cur[0] if off is None else off
            if off is None:
                cur[0] += size
            assert o + size <= end, (name, o + size - end)
            return nc.alloc_sbuf_tensor_at(name, list(shape), dt, offset=o), o + size

        def keep(name, shape, dt=f32):
            return at(name, shape, dt)[0]

        prm_a = keep("prm_a", [P, PR["gain"][1]])
        u10 = keep("u10", [P, 2 * FT, 18])
        rstd_bc = keep("rstd_bc", [P, COLS])
        epsc = keep("epsc", [P, 1])
        cfree = cur[0]
        ca = keep("ca", [P, CA_W])
        prm_b = keep("prm_b", [P, PR_W - PR["gain"][1]])
        ssx = keep("ssx", [P, 11]); rsx = keep("rsx", [P, 11])
        ssn = keep("ssn", [P, 2, 8]); rsn = keep("rsn", [P, 2, 8])
        nhalf = keep("nhalf", [P, 32])
        fa = keep("fa", [P, 36]); fb = keep("fb", [P, 36]); lf = keep("lf", [P, 36]); npre = keep("npre", [P, 32])
        ptab = keep("ptab", [1, NSAMP * PAGES], i32)
        bsamp = keep("bsamp", [P, 3, NH])
        cend = cur[0]
        convA = at("convA", [P, COLS], off=cfree)[0]
        sbase, o = at("sbase", [P, 2 * FT, NSAMP], f32, cfree + 4128)
        assert o <= cend, (o, cend)
        hhi = keep("hhi", [P, KC, COLS], f32r)
        hoff = cur[0] - KC * COLS * 4
        hlo = keep("hlo", [P, KC, COLS], f32r)
        mkd, o = at("mkd", [4, 3, 8, WG], f32, hoff)
        cmk, o = at("cmk", [P, 10, 4, WG], f32, o)
        assert o <= cur[0]
        qst, o = at("qst", [P, 2, NT, 2, HD], f32, hoff); kst, o = at("kst", [P, 2, NT, 2, HD], f32, o)
        qhl, o = at("qhl", [P, 2, SEQ], f32r, o); khh, o = at("khh", [P, 2, SEQ], f32r, o)
        q1c, o = at("q1c", [HD + 2, 2, SEQ], f32r, o); klc, o = at("klc", [HD + 2, 2, SEQ], f32r, o)
        assert o <= cur[0]
        R = cur[0]
        o = R
        NW = 12
        whi, o = at("whi", [P, NW, 512], f32r, o); wlo, o = at("wlo", [P, NW, 512], f32r, o)
        wst, o = at("wst", [P, 4, 512], f32, o)
        zo, o = at("zo", [P, 4, 512], f32, o)
        zn, o = at("zn", [P, 2, 512], f32, o)
        sq, o = at("sq", [P, 2, 512], f32, o)
        xst, o = at("xst", [P, 2, NMEM], f32, o)
        ob, o = at("ob", [P, 2, WG], f32, o)
        wsT, o = at("wsT", [P, NH, P], f32, o)
        crow, o = at("crow", [4 * NT, 3, P], f32r, o)
        pidx, o = at("pidx", [P, 2], i32, o)
        prep = R + 2 * NW * 2048 + 4 * 2048
        lfp = at("lfp", [P, 2, PSZ * NH], f32, prep)[0]
        lft = at("lft", [P, 2, NH, P], f32, prep + 4096)[0]
        lmask = at("lmask", [P, 2 * NH * P], f32, prep + 8192)[0]
        lscan = at("lscan", [P, 2 * NH * P], f32, prep + 12288)[0]
        clm = at("clm", [4, NR], f32, R + 8 * 2048)[0]
        rtab = at("rtab", [4, NR], f32, R + (NW + 8) * 2048)[0]
        relb = at("relb", [32, NH], f32, R + (NW + 8) * 2048 + 4608)[0]
        o2 = R
        oN, o2 = at("oN", [P, NT, DM], f32, o2)
        att0 = o2
        o2 += 8192
        vst, o2 = at("vst", [P, 2, NT, HD + 1], f32, o2)
        crs, o2 = at("crs", [HD + 2, 2, SEQ], f32, o2)
        o2 += 8192
        toe0 = o2
        toe, o2 = at("toe", [P, 2, SEQ], f32, o2)
        lg0 = o2
        lg, o2 = at("lg", [P, 2, SEQ], f32, o2)
        pts, o2 = at("pts", [P, 2, NT, P], f32, o2)
        nm, o2 = at("nm", [P, 2, 2], f32, o2)
        rc, o2 = at("rc", [P, 2], f32, o2)
        o = max(o, o2)
        zs, o = at("zs", [NSAMP, 2308], f32, o)
        sA, o = at("sA", [P, 8, PAGES, NH], f32, o); biasA, o = at("biasA", [P, 8, PAGES, NH], f32, o)
        qb, o = at("qb", [P, 8, WG], f32, o)
        ring, o = at("ring", [P, 4, 4, WG], f32, o)
        x7 = at("x7", [P, 7, 516], f32, o - 16384)[0]
        acc8 = at("acc8", [NSAMP, 3, NH, HD], f32, o - 16384 - 8192 - 4096)[0]
        coh = at("coh", [32, NR + 320], f32, o - 16384 - 8192)[0]
        o3 = att0
        oS, o3 = at("oS", [NSAMP, 4, WG], f32, att0 + 24576)
        assert o3 <= toe0
        o3 = toe0
        sC, o3 = at("sC", [P, 3, 8, NH], f32, o3); sM, o3 = at("sM", [P, 2, 8, NH], f32, o3)
        est, o3 = at("est", [P, 8, 16], f32, o3)
        small, o3 = at("small", [P, 3, 32 * 5], f32, o3)
        sso, o3 = at("sso", [P, 36], f32, o3); rso, o3 = at("rso", [P, 36], f32, o3)
        prod8, o3 = at("prod8", [NSAMP, 2, WG], f32, o3)
        assert o3 <= lg0
        osq, o3 = at("osq", [P, 2, DM], f32, lg0)
        ring2 = at("ring2", [P, 4, 4, WG], f32, att0)[0]
        qb2, o3 = at("qb2", [P, 8, WG], f32, o3)
        assert o3 <= o2
        x2off = R + 49152 + 8192 + 33024
        x2, o4 = at("x2", [P, KC, COLS], f32, x2off)
        stT = at("stT", [P, 2 * FT, 2, NSAMP], f32, o4)[0]
        uu, o4 = at("uu", [P, COLS], f32, o4)
        convG, o4 = at("convG", [P, COLS], f32, o4)
        o5 = att0
        wohi, o5 = at("wohi", [P, 2, KC, P], f32r, o5); wolo, o5 = at("wolo", [P, 2, KC, P], f32r, o5)
        wost, o5 = at("wost", [P, 2, KC, P], f32, o5)
        sqx, o5 = at("sqx", [P, COLS], f32, o5); sacc, o5 = at("sacc", [P, COLS], f32, o5)
        assert o5 <= x2off
        fst0 = at("fst0", [P, 4, DM], f32, x2off - 16512)[0]
        o6 = R
        uhi, o6 = at("uhi", [P, 2, KC, 256], f32r, o6); ulo, o6 = at("ulo", [P, 2, KC, 256], f32r, o6)
        dhi, o6 = at("dhi", [P, 2, DM], f32r, o6); dlo, o6 = at("dlo", [P, 2, DM], f32r, o6)
        fst, o6 = at("fst", [P, 2, DM], f32, o6)
        ahi, o6 = at("ahi", [P, 2, 2, COLS], f32r, o6); alo, o6 = at("alo", [P, 2, 2, COLS], f32r, o6)
        assert o6 <= x2off, (o6, x2off)
        ps = ctx.enter_context(nc.psum_tensor("ps", [P, 8, 512], f32))

        def cv(name, rows=P):
            a, b = CA[name]
            return ca[0:rows, a:b]

        def pv(name, rows=P):
            a, b = PR[name]
            if b <= PR["gain"][1]:
                return prm_a[0:rows, a:b]
            return prm_b[0:rows, a - PR["gain"][1]:b - PR["gain"][1]]

        ident, ones, ustr = cv("id"), cv("one"), cv("u")
        gain = pv("gain").rearrange("p (s k) -> p s k", s=4)
        conv = pv("conv").rearrange("p (s f) -> p s f", s=4)
        gq = pv("g").rearrange("p (s e) -> p s e", s=6)

        def dram(name, shape):
            return nc.dram_tensor(name, shape, f32, kind="Internal").ap()
        scr_q = dram("scr_q", (3, SEQ, WG))
        scr_b = dram("scr_b", (SEQ, WG))
        scr_qs = dram("scr_qs", (3, NSAMP, WG))
        scr_r = dram("scr_r", (8, NR))
        scr_t = dram("scr_t", (8, P, NR))
        scr_o = dram("scr_o", (NH, 3, NSAMP, WG))
        scr_c = dram("scr_c", (8, 2, SEQ))

        sems = {}

        def S(name):
            if name not in sems:
                sems[name] = ctx.enter_context(nc.semaphore(name))
            return sems[name]

        units = [(b, tt) for b in range(5) for tt in ["S"] + list(range(NT))] + [(5, 0), (5, 1)]
        UI = {k: i for i, k in enumerate(units)}
        NU = len(units)
        prompt_no = {}
        for k in units:
            if k[1] != "S":
                prompt_no[k] = len(prompt_no)
        bank = {k: (6 if k[1] == "S" else prompt_no[k] % 4) for k in units}
        WID = [w for _, w in BLK] + [512]
        NORM = {0: (0, 8, 0), 3: (0, 8, 2), 4: (256, 4, 4), 5: (0, 4, 5)}
        COPY = {1: (0, 256), 4: (0, 256), 5: (256, 256)}
        norm_units = [k for k in units if k[0] in NORM]
        NI = {k: i for i, k in enumerate(norm_units)}
        dve_units = [k for k in units if k[0] in NORM or k[0] == 1]
        DI = {k: i for i, k in enumerate(dve_units)}
        first_kg = UI[(1, 0)]

        def xi(k):
            return 9 + k[1] if k[0] == 5 else (0 if k[1] == "S" else 1 + k[1])

        def rows(k):
            return NSAMP if k[1] == "S" else P

        def xslot(i):
            return x7[:, i % 7, :] if i < 16 else xst[:, i % 2, :]

        def xsem(i):
            return S(f"x_ld{i % 7}") if i < 16 else S(f"x_ld{i % 2}")

        def xtotal(i):
            return 16 * (i // 7 + 1) if i < 16 else 48 + 16 * (i // 2 - 7)

        def xrow(x, n):
            if x % 3 == 0:
                return sA[0:n].rearrange("p b g h -> p (b g h)")
            return qb[0:n, 4 * (x % 3) - 4:4 * (x % 3), :].rearrange("p b c -> p (b c)")

        def prev_in_bank(k):
            same = [m for m in units[:UI[k]] if bank[m] == bank[k]]
            return same[-1] if same else None

        def dve_last(k):
            return max([DI[m] + 1 for m in dve_units if UI[m] <= UI[k]], default=0)

        def zdst(k):
            if k[1] == "S":
                a, w = BLK[k[0]]
                return zs[:, a:a + min(w, 512)]
            return zo[:, prompt_no[k] % 4, :]

        def chunk_turns():
            turns = {u: [] for u in range(-1, NU)}
            for b in range(6):
                for kc in range(KC):
                    if b == 0:
                        turns[-1].append((b, kc))
                    else:
                        u = UI[(b - 1, kc if kc < 4 else 7)]
                        turns[u if kc < 6 else UI[(b, "S")] if b < 5 else UI[(5, 0)]].append((b, kc))
            return turns
        CT = chunk_turns()
        CT_load = {u: [b * KC + kc for b, kc in CT.get(u + 2, []) if b > 0] for u in range(-1, NU)}
        CT_load[0] = sorted([b * KC + kc for v in (0, 1, 2) for b, kc in CT.get(v, []) if b > 0])
        n_out = {0: 2, 1: 1, 2: 1, 3: 2, 4: 2, 5: 2}
        kgran = {}
        for b in range(1, 5):
            for tt in range(NT):
                kgran[(b, tt)] = len(kgran)
        NKP = len(kgran)
        NKA = NSAMP * PAGES // 4

        kpool = t["cache_a_k"].rearrange("o n p h e -> (o n) p (h e)")
        vpool = t["cache_a_v"].rearrange("o n p h e -> (o n) p (h e)")
        lfpool = t["cache_a_logf"].rearrange("o n p h -> (o n) (p h)")
        o_ka = t["o_ka"]; o_va = t["o_va"]; o_kc = t["o_kc"]; o_vc = t["o_vc"]; o_mk = t["o_mk"]; o_mv = t["o_mv"]

        def vslot(j):
            return ring[:, j] if j < 4 else ring2[:, j - 4]

        def load_pages(sp, pool, seq, group, slot, pages=range(4), sem="ring_ld"):
            for j in pages:
                page = sp.value_load(ptab[0:1, bass.ds(seq * PAGES + (group * 4 + j), 1)], min_val=0, max_val=NPOOL - 1)
                sp.dma_start(vslot(slot)[:, j, :], pool[bass.ds(page, 1)].rearrange("o p c -> p (o c)"))\
                    .then_inc(S(f"{sem}{slot}"), 16)

        def ck_rows(cache, c, b0):
            if c == 0:
                v = cache[0, b0:b0 + 4, 1920:2048]
            elif c == 1:
                v = cache[0, b0:b0 + 4, 1536:1917:4]
            else:
                v = cache[0, b0:b0 + 4, 0:1521:16]
            return v.rearrange("b r h e -> r b (h e)")
        CROWS = [128, 96, 96]
        cm = [(DIL, c, b0) for b0 in (0, 4) for c in range(3)] + [(MEMG, c, b0) for b0 in (0, 4) for c in range(2)]
        NCM = len(cm)

        def ring_total(n):
            keys = sum(64 if m < NKA else 0 if m < 2 * NKA else 16 for m in range(n % 4, n + 1, 4))
            return keys + (48 * NSAMP if n >= 2 * NKA else 0)
        V0 = 16 * NKA
        SHARE = {"sp": ((0, 1), (0,)), "act": ((2,), (1, 2)), "pool": ((3,), (3,))}


        def v_pages(e, who, b, j):
            load_pages(e, vpool, b, j, j, SHARE[who][j % 2], "pool_ld" if who == "pool" else "ring_ld")

        def cm_load(sp, dst, i, sem, key):
            g, c, b0 = cm[i]
            if g == DIL:
                src = ck_rows(t["cache_c_" + key], c, b0)
                n = CROWS[c]
            else:
                src = t["cache_mem_" + key][0, b0:b0 + 4, c * P:(c + 1) * P].rearrange("b r h e -> r b (h e)")
                n = P
            sp.dma_start(dst[0:n], src).then_inc(sem, 16)

        STEPS = NH * NT
        AC = dict(n="ac", blocks=[NT - s for s in range(NT)], tile=[NT - 1 - s for s in range(NT)], bias=True, halves=2,
                  vld=48, qk0=0, v0=0)
        MM = dict(n="mm", blocks=[2] * NT, tile=list(range(NT)), bias=False, halves=1, vld=16, qk0=4 * 64, v0=4 * 48)
        PREP_AT = {4: "q0", 5: "k0", 6: "q1", 7: "k1"}

        def prep_no(A, h, piece):
            pieces = ["q0", "k0", "q1", "k1"][:2 + A["halves"]]
            return len(pieces) * h + pieces.index(piece) + 1

        block = ctx.enter_context(nc.Block())

        @block.sync
        def _(sp):
            sp.dma_start(ca[:, :], t["ca"]).then_inc(S("const_ld"), 16)
            sp.dma_start(prm_a[:, :], t["prm"][:, 0:PR["gain"][1]]).then_inc(S("const_ld"), 16)
            sp.dma_start(prm_b[:, :], t["prm"][:, PR["gain"][1]:PR_W]).then_inc(S("const_ld"), 16)
            sp.dma_start(ptab[:, :], t["ptab"]).then_inc(S("const_ld"), 16)
            sp.dma_start(pidx[:, :], t["pidx"]).then_inc(S("const_ld"), 16)
            sp.dma_start(coh[:, :], t["coh"]).then_inc(S("tab_ld"), 16)
            sp.dma_start(clm[:, :], t["clm"]).then_inc(S("tab_ld"), 16)
            sp.dma_start(relb[:, :], t["rel_bias"]).then_inc(S("tab_ld"), 16)
            sp.dma_start(wsT[:, :, :], t["wsT"]).then_inc(S("const_ld"), 16)
            def stat_load(x):
                src, n = (t["x_sample"], NSAMP) if x == 0 else \
                    ((t["x_prompt"][(x - 1) * P:x * P], P) if x < 9 else (t["mem"][(x - 9) * P:(x - 8) * P], P))
                if x >= 3:
                    sp.wait_ge(S("x_stat"), x - 2)
                elif x == 1:
                    sp.wait_ge(S("rt_pe"), 6)
                sp.dma_start(xrow(x, n), src).then_inc(S(f"xrow_ld{x % 3}"), 16)
            def w_load(q):
                b, kc = divmod(q, KC)
                src = t["w_in"][0, kc * P:(kc + 1) * P, BLK[b][0]:BLK[b][0] + WID[b]] if b < 5 else \
                    t["w_mem"][0, kc * P:(kc + 1) * P, :]
                if q >= 4:
                    sp.wait_ge(S("w_split"), q - 3)
                sp.dma_start(wst[:, q % 4, 0:WID[b]], src).then_inc(S(f"w_ld{q % 4}"), 16)

            def x_load(i):
                if i < 16:
                    src, w = t["xT"][:, i % 8, (i // 8) * 516:(i // 8) * 516 + 516], 516
                else:
                    src, w = t["memT"][:, i - 16, :], NMEM
                if 7 <= i < 16:
                    sp.wait_ge(S("x_split"), i - 6)
                elif i >= 18:
                    sp.wait_ge(S("x_split"), i - 1)
                sp.dma_start(xslot(i)[:, 0:w], src).then_inc(xsem(i), 16)

            for kc in range(KC):
                x_load(kc)
                w_load(kc)
            sp.wait_ge(S("rtab"), 3)
            sp.dma_start(scr_r[4:8, :], rtab[:, :]).then_inc(S("rdram"), 16)
            sp.dma_start(scr_r[0:4, :], t["cmask"]).then_inc(S("rdram"), 16)
            for i in range(8, 16):
                x_load(i)
            for x in range(11):
                stat_load(x)
                if x >= 7:
                    w_load(KC + x - 7)

            def outputs(k):
                b, tt = k
                n = prompt_no[k]
                z = zo[:, n % 4, :]
                r = slice(tt * P, (tt + 1) * P)
                so = S(f"zo_out{n % 4}")
                if b == 2:
                    sp.wait_ge(S("ob_ready"), tt + 1)
                    sp.dma_start(scr_b[r, :], ob[:, tt % 2, :]).then_inc(S(f"ob_out{tt % 2}"), 16)
                    return
                if b in NORM:
                    sp.wait_ge(S("zo_dve"), NI[k] + 1)
                if b in COPY:
                    sp.wait_ge(S("act_z"), UI[k] + 1)
                dst = {0: (scr_q[0], o_ka), 1: (o_va,), 3: (scr_q[1], o_kc), 4: (o_vc, scr_q[2]), 5: (o_mk, o_mv)}[b]
                for i, d in enumerate(dst):
                    sp.dma_start(d[r, :], z[:, i * WG:(i + 1) * WG]).then_inc(so, 16)

            def cols(x, hh):
                return x[:, hh * HD:(hh + 1) * HD].rearrange("(t p) e -> p t e", p=P)

            def qk_load(par, group, hh):
                nk = 2 if group == MEMG else NT
                for i in range(2):
                    sp.dma_start(qst[:, par, :, i, :], cols(scr_q[group], hh)).then_inc(S(f"qk_ld{par}"), 16)
                    sp.dma_start(kst[:, par, 0:nk, i, :], cols((o_ka, o_kc, o_mk)[group], hh)).then_inc(S(f"qk_ld{par}"), 16)

            for u, k in enumerate(units):
                b, tt = k
                for q in CT_load[u]:
                    if q >= KC + 4:
                        w_load(q)
                if k == (0, 4):
                    sp.wait_ge(S("const_ld"), 96)
                    sp.wait_ge(S("x_split"), 16)
                    for s4 in range(4):
                        load_pages(sp, kpool, 0, s4, s4)
                if k == (1, 0):
                    sp.wait_ge(S("rdram"), 32)
                if b == 1 and tt != "S":
                    src = scr_r[tt:tt + 1, :]
                    sp.dma_start(scr_t[tt], bass.AP(src.tensor, src.offset, [[0, P], [1, NR]])).then_inc(S("toe_dram"), 16)
                if b == 4 and tt != "S" and tt >= 2 and tt < 6:
                    for i in (2 * (tt - 2), 2 * (tt - 2) + 1):
                        x_load(16 + i)
                if k in kgran:
                    n = kgran[k] + 3
                    if 4 <= n < NKP:
                        sp.wait_ge(S("k_used"), n - 3)
                        load_pages(sp, kpool, n // 8, n % 8, n % 4, (0, 1))
                if u >= 2 and units[u - 2][1] != "S":
                    outputs(units[u - 2])
                if k == (0, 2):
                    sp.wait_ge(S("zs_norm"), 1)
                    sp.dma_start(scr_qs[0], zs[:, 0:WG]).then_inc(S("qs_dram"), 16)
                    sp.wait_ge(S("qs_dram"), 16)
                    sp.dma_start(qb[:, :, :], bass.AP(scr_qs.tensor, scr_qs[0].offset, [[0, P], [1, 8 * WG]]))\
                        .then_inc(S("qb_ld"), 16)
                if k == (3, 0):
                    sp.wait_ge(S("crow"), 3)
                    for half, parts in ((0, (0, 1)), (1, (2, 2))):
                        for i, part in enumerate(parts):
                            sp.dma_start(scr_c[4 * half:4 * half + 4, i].rearrange("h (t p) -> h t p", p=P), crow[:, part, :].bitcast(f32))\
                                .then_inc(S("crow_dram"), 16)
                    sp.dma_start(t["o_lf"], lf[:, :]).then_inc(S("out"), 16)
            outputs(units[NU - 2])
            sp.wait_ge(S("z_done"), NU)
            for s4 in range(4):
                uses = [k for k in prompt_no if prompt_no[k] % 4 == s4 and k[0] <= 3]
                sp.wait_ge(S(f"zo_out{s4}"), 16 * sum(0 if k[0] == 2 else n_out[k[0]] for k in uses))
            for h in range(2):
                qk_load(h, ATT, h)
            outputs(units[NU - 1])
            for s4 in range(4):
                uses = [k for k in prompt_no if prompt_no[k] % 4 == s4]
                sp.wait_ge(S(f"zo_out{s4}"), 16 * sum(0 if k[0] == 2 else n_out[k[0]] for k in uses))
            for s2 in range(2):
                sp.wait_ge(S(f"ob_out{s2}"), 64)
            sp.wait_ge(S("crow_dram"), 64)
            sp.wait_ge(S("toe_dram"), 128)
            sp.wait_ge(S("zo_dve"), len(norm_units))
            sp.wait_ge(S("z_done"), NU)

            def v_load(par, group, hh):
                nk, h, ld = 2 if group == MEMG else NT, group * NH + hh, S(f"v_ld{par}")
                sp.dma_start(vst[:, par, 0:nk, 0:HD], cols((o_va, o_vc, o_mv)[group], hh)).then_inc(ld, 16)
                if group != MEMG:
                    off = scr_t.rearrange("h p r -> h (p r)")[h:h + 1, P - 1:P - 1 + P * (NR - 1)]
                    sp.dma_start(toe[:, par, :], off.rearrange("o (p r) -> (o p) r", r=NR - 1)[:, 0:SEQ]).then_inc(ld, 16)
                    sp.dma_start(crs[HD:HD + 2, par, :], scr_c[h]).then_inc(ld, 16)

            def k_granules(h):
                for n in range(NKP + 4 * h, NKP + 4 * h + 4):
                    sp.wait_ge(S("k_used"), n - 3)
                    load_pages(sp, kpool, n // 8, n % 8, n % 4)
            for h in range(2):
                v_load(h, ATT, h)
            sp.dma_start(oN[:, :, 2 * WG:3 * WG], scr_b.rearrange("(t p) c -> p t c", p=P)).then_inc(S("ob_ld"), 16)
            k_granules(0)
            for h in range(8):
                group, hh = divmod(h + 2, NH)
                sp.wait_ge(S("ac_prep"), 4 * (h + 1))
                qk_load(h % 2, group, hh)
                if h + 1 < 8:
                    k_granules(h + 1)
                sp.wait_ge(S("ac_pv"), 2 + 8 * (h + 1))
                sp.wait_ge(S("ac_lg"), 2 + 8 * (h + 1))
                v_load(h % 2, group, hh)
            sp.wait_ge(S("k_used"), NKA)
            sp.wait_ge(S("zs_norm"), 3)
            sp.dma_start(scr_qs[1], zs[:, BLK[3][0]:BLK[3][0] + WG]).then_inc(S("qs_dram"), 16)
            sp.dma_start(scr_qs[2], zs[:, BLK[4][0] + WG:BLK[4][0] + 2 * WG]).then_inc(S("qs_dram"), 16)
            sp.wait_ge(S("qs_dram"), 48)
            sp.dma_start(qb[:, :, :], bass.AP(scr_qs.tensor, scr_qs[1].offset, [[0, P], [1, 8 * WG]])).then_inc(S("qb_ld"), 16)
            for j in range(4):
                load_pages(sp, vpool, 0, j, j, (0, 1, 2))
            for h in (2, 3):
                sp.wait_ge(S("mm_prep"), 3 * (h - 1))
                qk_load(h % 2, MEMG, h)
                sp.wait_ge(S("mm_pv"), 2 + 8 * (h - 1))
                v_load(h % 2, MEMG, h)
            sp.wait_ge(S("mm_pv"), 2 + 32)
            sp.dma_start(qb2[:, :, :], bass.AP(scr_qs.tensor, scr_qs[2].offset, [[0, P], [1, 8 * WG]])).then_inc(S("qb2_ld"), 16)
            for j in range(4, 8):
                v_pages(sp, "sp", 0, j)
                for i in range(3 * (j - 4), min(3 * (j - 3), NCM)):
                    cm_load(sp, cmk[:, i], i, S("cmk_ld"), "k")
            for d in range(2):
                sp.dma_start(wost[:, d], t["w_outL"][d]).then_inc(S(f"wo_ld{d}"), 16)
            with sp.Fori(1, 8) as b:
                for j in range(8):
                    sp.wait_ge(S("v_used"), b * 8 + (j + 1))
                    v_pages(sp, "sp", b, j)
            for i in range(NCM):
                sp.wait_ge(S("v_used"), NKA + min(i, 4) + 1 if i < 4 else 8 + NKA + i - 3)
                cm_load(sp, ring[:, i % 4], i, S(f"ring_ld{i % 4}"), "v")
            sp.wait_ge(S("acc_cp"), 1 + NSAMP)
            sp.wait_ge(S("acc2_cp"), 4)
            sp.dma_start(scr_o, mkd[:, :, :, :]).then_inc(S("acc_ld"), 16)
            sp.wait_ge(S("acc_ld"), 16)
            for h in range(NH):
                sp.dma_start(acc8[:, :, h, :], scr_o[h, :, :, h * HD:(h + 1) * HD].rearrange("g b e -> b g e"))\
                    .then_inc(S("acc_ld"), 16)
            sp.wait_ge(S("zs_norm"), 3)
            sp.dma_start(t["o_zs"], zs[:, :]).then_inc(S("out"), 16)
            sp.wait_ge(S("o_scaled"), 9)
            sp.wait_ge(S("ot_pe"), 9)
            sp.wait_ge(S("out"), 32)
            for kc in range(KC):
                sp.dma_start(x2[:, kc, :], t["xT"][:, kc, :]).then_inc(S("x2_ld"), 16)
            sp.dma_start(stT[:, :, :, :], t["stT"]).then_inc(S("x2_ld"), 16)
            upL, dnL = t["w_upL"], t["w_down"]
            for d in range(2, KC):
                sp.wait_ge(S("wo_split"), d - 1)
                sp.dma_start(wost[:, d % 2], t["w_outL"][d]).then_inc(S(f"wo_ld{d % 2}"), 16)
                if d < 6:
                    sp.dma_start(fst0[:, d - 2], upL[0, (d - 2) // 2, d % 2]).then_inc(S("f0_ld"), 16)
            sp.wait_ge(S("wo_split"), KC)

            def f_piece(i, src):
                sp.dma_start(fst[:, i % 2], src).then_inc(S(f"f_ld{i % 2}"), 16)
            for p in range(4, 8):
                if p >= 6:
                    sp.wait_ge(S("f_split"), p - 1)
                f_piece(p, upL[p // 4, (p % 4) // 2, p % 2])
            with sp.Fori(1, NGRP - 1) as G:
                for i in range(6):
                    sp.wait_ge(S("f_split"), G * 6 + (i + 1))
                    if i < 2:
                        f_piece(i, dnL[bass.ds(G * 2 + (i - 2), 1)].rearrange("o p c -> (o p) c"))
                    else:
                        f_piece(i, upL[bass.ds(G + 1, 1), (i - 2) // 2, i % 2].rearrange("o p c -> (o p) c"))
            for i in range(4):
                p = 8 + 6 * (NGRP - 2) + i
                sp.wait_ge(S("f_split"), p - 1)
                f_piece(p, dnL[2 * (NGRP - 2) + i])
            for d in range(KC):
                sp.wait_ge(S("f_free"), 4 + 12 * (NGRP - 1) + d + 1)
                sp.dma_start(t["o_yT"][:, d, :], x2[:, d, :]).then_inc(S("out"), 16)
            sp.dma_start(t["o_u10"], u10[:, :, :]).then_inc(S("out"), 16)
            sp.wait_ge(S("out"), 16 * (1 + 1 + KC + 1))

        targets = []

        class LoopTargets:

            def __init__(self, eng, last):
                self.eng, self.reg, self.cur, self.base = eng, {}, {}, {}
                self.last = {name: (per, max(per, c)) for name, (per, c) in last.items()}
                for name, (per, c) in self.last.items():
                    self.reg[name] = eng.alloc_register(f"{name}_{len(targets)}")
                    targets.append(name)
                    eng.reg_mov(self.reg[name], c - per)
                    self.cur[name] = c - per

            def wait(self, name, c):
                c += self.base.get(name, 0)
                if c <= self.cur[name]:
                    return
                self.eng.reg_add(self.reg[name], self.reg[name], c - self.cur[name])
                self.cur[name] = c
                self.eng.wait_ge(S("const_ld"), 96)
                self.eng.wait_ge(S(name), self.reg[name])

            def end(self):
                for name, (per, c) in self.last.items():
                    assert self.cur[name] <= c, (name, self.cur[name], c)
                    if self.cur[name] < c:
                        self.eng.reg_add(self.reg[name], self.reg[name], c - self.cur[name])
                    self.cur[name] = c - per

        class PassTargets:

            def __init__(self, eng):
                self.eng, self.cur = eng, {}

            def wait(self, name, c):
                if c > self.cur.get(name, 0):
                    self.cur[name] = c
                    self.eng.wait_ge(S(name), c)

        def zview(k):
            return ps[0:rows(k), bank[k], :]

        def wait_zo_free(e, k):
            n = prompt_no[k]
            if n >= 4:
                m = [x for x in prompt_no if prompt_no[x] == n - 4][0]
                if m[0] == 2:
                    e.wait_ge(S("ob_ready"), m[1] + 1)
                done = sum(n_out[x[0]] for x in prompt_no if prompt_no[x] % 4 == n % 4 and prompt_no[x] < n and x[0] != 2)
                if done:
                    e.wait_ge(S(f"zo_out{n % 4}"), 16 * done)

        SBANK = lambda a: ps[:, 2 * a:2 * a + 2, :].rearrange("p b c -> p (b c)")

        def U3(par):
            return ps[:, 3 * par:3 * par + 3, 0:CH]

        def c3(ap):
            return ap.rearrange("p (b c) -> p b c", b=3)

        @block.tensor
        def _(pe):
            pe.wait_ge(S("const_ld"), 96)
            pe.wait_ge(S("tab_ld"), 48)
            for j in range(3):
                w = min(512, NR - 512 * j)
                pe.matmul(ps[0:NH, j, 0:w], relb[:, :], coh[:, 512 * j:512 * j + w], start=True, stop=True)\
                    .then_inc(S("rt_pe"), 1)
            for c in range(3):
                n = CROWS[c]
                o_ = NR + sum(CROWS[:c])
                pe.matmul(ps[0:n, 3, NH * c:NH * c + NH], coh[:, o_:o_ + n], relb[:, :], start=True, stop=True)\
                    .then_inc(S("rt_pe"), 1)
            pe.wait_ge(S("lfp_ld"), 32)
            for i in range(2):
                for h in range(NH):
                    pe.transpose(ps[:, 4 + i, h * P:(h + 1) * P], lfp[:, i, h::NH], ident).then_inc(S("lft_pe"), 1)
            def sgu(tt):
                k = (2, tt)
                if tt == 0:
                    pe.wait_ge(S("crow"), 3)
                    pe.wait_ge(S("ws_mask"), 2)
                pe.wait_ge(S("act_z"), UI[k] + 1)
                if tt >= 1:
                    pe.wait_ge(S("ob_ready"), tt)
                v = zo[:, prompt_no[k] % 4, WG:2 * WG]
                for g in range(NH):
                    i = pe.matmul(ps[:, 7, WG + g * HD:WG + (g + 1) * HD], wsT[:, g, :], v[:, g * HD:(g + 1) * HD],
                                  start=True, stop=True)
                i.then_inc(S("sgu_pe"), 1)

            for u, k in enumerate(units):
                b, tt = k
                pk = prev_in_bank(k)
                if pk is not None:
                    pe.wait_ge(S("act_z"), UI[pk] + 1)
                    if dve_last(pk):
                        pe.wait_ge(S("dve_z"), dve_last(pk))
                elif bank[k] != 6:
                    pe.wait_ge(S("rtab"), 4)
                c0 = 0 if tt == "S" else (tt * P if b == 5 else NSAMP + tt * P)
                for kc in range(KC):
                    if tt == "S" or (b == 5 and tt == 0):
                        pe.wait_ge(S("w_split"), b * KC + kc + 1)
                    if b == 0:
                        pe.wait_ge(S("x_split"), (kc + 1) if tt in ("S", 0, 1, 2) else 9 + kc)
                    if b == 5:
                        pe.wait_ge(S("x_split"), 17 + kc)
                    sl = (b * KC + kc) % NW
                    w = WID[b]
                    lh, ll = hhi[:, kc, c0:c0 + P], hlo[:, kc, c0:c0 + P]
                    out = ps[:, bank[k], 0:w]
                    pe.matmul(out, lh, whi[:, sl, 0:w], start=(kc == 0), stop=False)
                    pe.matmul(out, lh, wlo[:, sl, 0:w], start=False, stop=False)
                    i = pe.matmul(out, ll, whi[:, sl, 0:w], start=False, stop=(kc == KC - 1))
                    if tt == NT - 1 or (b == 5 and tt == 1):
                        i.then_inc(S("w_used"), 1)
                    elif kc == KC - 1:
                        i.then_inc(S("z_done"), 1)
                if tt == NT - 1 or (b == 5 and tt == 1):
                    pe.wait_ge(S("w_used"), (b + 1) * KC)
                    pe.sem_inc(S("z_done"), 1)
                if k == (0, "S"):
                    pe.wait_ge(S("lsuf"), 1)
                    pe.wait_ge(S("lft_cp"), 2)
                    for i in range(2):
                        v = slice(i * 512, (i + 1) * 512)
                        pe.matmul(ps[:, 4 + i, :], ustr, lft[:, i].rearrange("p h c -> p (h c)"), start=True, stop=False)
                        pe.matmul(ps[:, 4 + i, :], ones, lmask[:, v], start=False, stop=True).then_inc(S("lft_pe"), 1)
                if k == (2, 0):
                    pe.wait_ge(S("forget"), 3)
                    pe.wait_ge(S("lft_cp"), 4)
                    pe.matmul(ps[:, 7, 0:32], ustr, lf[:, 0:32], start=True, stop=False)
                    pe.matmul(ps[:, 7, 0:32], ones, npre[:, :], start=False, stop=True).then_inc(S("csum_pe"), 1)
                if k == (2, 1):
                    pe.wait_ge(S("forget"), 4)
                    pe.transpose(ps[0:32, 7, 64:64 + P], fb[:, 0:32], ident).then_inc(S("csum_pe"), 1)
                if b == 2 and tt not in ("S", 0, 1):
                    sgu(tt - 2)
                if k == (3, "S"):
                    sgu(6)
                if k == (3, 0):
                    sgu(7)

            def heads_pass(A, T_):
                n, two = A["n"], A["bias"]
                K2 = HD + 2 if two else HD
                free = "_lg" if two else "_exp"
                exp_seed = 0 if two else 2

                def prep(h, piece):
                    par, i = h % 2, int(piece[1])
                    src, bank_ = (qst, 1) if piece[0] == "q" else (kst, 3)
                    T_.wait(f"qk_ld{par}", A["qk0"] + 64 * (h // 2 + 1))
                    if i == 1:
                        T_.wait(n + "_lo", prep_no(A, h, piece[0] + "0"))
                    nb = 2 if piece == "k0" and not two else 4
                    for j in range(nb):
                        m = pe.transpose(ps[:, bank_, j * P:(j + 1) * P],
                                         src[:, par, 4 * i + j].rearrange("p a e -> p (a e)"), ident)
                    m.then_inc(S(n + "_prep"), 1)

                def qk(g):
                    h, s = divmod(g, NT)
                    W = P * A["blocks"][s]
                    if s == 0:
                        T_.wait(n + "_lo", (2 + A["halves"]) * (h + 1))
                    T_.wait(n + free, g + 1)
                    q0 = A["tile"][s] * P
                    for c in range(0, W, 512):
                        w = min(512, W - c)
                        out = ps[:, 2 * (g % 2) + c // 512, 0:w]
                        pe.matmul(out, qhl[:, h % 2, q0:q0 + P], khh[:, h % 2, c:c + w], start=True, stop=False)
                        i = pe.matmul(out, (q1c if two else qhl)[0:K2, h % 2, q0:q0 + P], klc[0:K2, h % 2, c:c + w],
                                      start=False, stop=True)
                    i.then_inc(S(n + "_qk"), 1)

                def tp(g):
                    h, s = divmod(g, NT)
                    nb = A["blocks"][s]
                    T_.wait(n + "_exp", g + 1 + exp_seed)
                    T_.wait(n + "_eva", g + 1)
                    for j in range(min(nb, 4)):
                        i = pe.transpose(ps[:, 4, j * P:(j + 1) * P], lg[:, g % 2, j * P:(j + 1) * P], ident)
                    i.then_inc(S(n + "_tpa"), 1)
                    if nb > 4:
                        T_.wait(n + "_evb", 4 * h + s + 1)
                        for j in range(4, nb):
                            i = pe.transpose(ps[:, 5, (j - 4) * P:(j - 3) * P], lg[:, g % 2, j * P:(j + 1) * P], ident)
                        i.then_inc(S(n + "_tpb"), 1)

                def pv_(g):
                    h, s = divmod(g, NT)
                    nb = A["blocks"][s]
                    T_.wait(n + "_eva", g + 2)
                    if nb > 4:
                        T_.wait(n + "_evb", 4 * h + s + 2)
                    T_.wait(n + "_o", g + 1)
                    for j in range(nb):
                        i = pe.matmul(ps[:, 6 + g % 2, 0:HD + 1], pts[:, g % 2, j, :], vst[:, h % 2, j, :],
                                      start=(j == 0), stop=(j == nb - 1))
                    i.then_inc(S(n + "_pv"), 1)

                for s in (4, 5, 6, 7):
                    if PREP_AT[s] != "k1" or two:
                        prep(0, PREP_AT[s])
                for g in range(STEPS + 3):
                    if 0 <= g - 2 < STEPS:
                        tp(g - 2)
                    h, s = divmod(g, NT)
                    piece = PREP_AT.get(s) if h + 1 < NH else None
                    if piece and (piece != "k1" or two):
                        T_.wait(n + free, g + 1)
                        prep(h + 1, piece)
                    if g < STEPS:
                        qk(g)
                    if 0 <= g - 3 < STEPS:
                        pv_(g - 3)

            def seed(A):
                pe.sem_inc(S(A["n"] + "_tpa"), 2)
                pe.sem_inc(S(A["n"] + "_pv"), 2)
                if A["bias"]:
                    pe.sem_inc(S(A["n"] + "_tpb"), 1)
            pe.wait_ge(S("q_ones"), 1)
            pe.wait_ge(S("dve_set"), 6)
            seed(AC)
            T_ = LoopTargets(pe, {"qk_ld0": (128, 128), "qk_ld1": (128, 128), "ac_lg": (32, 32), "ac_lo": (16, 16),
                                  "ac_eva": (32, 33), "ac_o": (32, 32), "ac_exp": (32, 32),
                                  "ac_evb": (16, 17)})
            with pe.Fori(0, 2):
                heads_pass(AC, T_)
                T_.end()
            seed(MM)
            heads_pass(MM, PassTargets(pe))

            pe.sem_inc(S("v_used"), 8)
            pe.wait_ge(S("mm_o"), 2 + 32)
            last = {"est": (8, 8), "acc_cp": (1, 1)}
            for j in range(8):
                last[f"ring_ld{j}"] = (48, (V0 if j < 4 else 0) + 48)
                last[f"pool_ld{j}"] = (16, 16)
            T_ = LoopTargets(pe, last)
            with pe.Fori(0, NSAMP):
                for j in range(8):
                    T_.wait(f"ring_ld{j}", (V0 if j < 4 else 0) + 48)
                    T_.wait(f"pool_ld{j}", 16)
                    T_.wait("est", j + 1)
                    if j == 0:
                        T_.wait("acc_cp", 1)
                    for g in range(4):
                        i = pe.matmul(ps[0:NH, 0, 0:WG], est[:, j, NH * g:NH * g + NH], vslot(j)[:, g, :],
                                      start=(j == 0 and g == 0), stop=(j == 7 and g == 3))
                    i.then_inc(S("v_used"), 1)
                T_.end()
            pe.wait_ge(S("acc_cp"), 1 + NSAMP)
            pe.wait_ge(S("e_act"), 3)
            for i, (g, c, b0) in enumerate(cm):
                n_ = 2 * NKA + i
                sl = n_ % 4
                pe.wait_ge(S(f"ring_ld{sl}"), ring_total(n_))
                nk = CROWS[c] if g == DIL else P
                e_ = sC if g == DIL else sM
                lastc = 2 if g == DIL else 1
                bank0 = 4 if i in (3, 4, 5, 8, 9) else 0
                if i in (6, 8):
                    pe.wait_ge(S("acc2_cp"), 1 if i == 6 else 2)
                for b in range(4):
                    m = pe.matmul(ps[0:NH, bank0 + b, 0:WG], e_[0:nk, c, b0 + b, :], ring[0:nk, sl, b, :],
                                  start=(c == 0), stop=(c == lastc))
                m.then_inc(S("v_used"), 1)
            pe.wait_ge(S("esum"), 3)
            pe.wait_ge(S("acc2_cp"), 4)
            for g in range(3):
                for h in range(NH):
                    m = pe.matmul(ps[0:NSAMP, 6, 8 * g + h:8 * g + h + 1], small[:, g, 32 + h:64:NH], ones[:, 0:1],
                                  start=True, stop=True)
            m.then_inc(S("samp_pe"), 1)

            for x, tt in enumerate(list(range(NT)) + ["S"]):
                pe.wait_ge(S("o_scaled"), x + 1)
                a = x % 2
                if x >= 2:
                    pe.wait_ge(S("o_lo"), x - 1)
                else:
                    pe.wait_ge(S("acc2_cp"), 4)
                r = NSAMP if tt == "S" else P
                for j in range(KC):
                    src = oS[:, j // 2, (j % 2) * P:(j % 2 + 1) * P] if tt == "S" else oN[:, tt, j * P:(j + 1) * P]
                    dst = SBANK(a)[:, j * r:(j + 1) * r]
                    m = pe.transpose(dst, src, ident[0:r, 0:r])
                m.then_inc(S("ot_pe"), 1)

            def product(par, lhs_hi, lhs_lo, rhs_hi, rhs_lo, nk, before=None):
                for kc in range(nk):
                    if before:
                        before(kc)
                    for ch in range(3):
                        out = ps[:, 3 * par + ch, 0:CH]
                        cs = slice(ch * CH, (ch + 1) * CH)
                        pe.matmul(out, lhs_hi(kc), rhs_hi(kc)[:, cs], start=(kc == 0), stop=False)
                        pe.matmul(out, lhs_hi(kc), rhs_lo(kc)[:, cs], start=False, stop=False)
                        i = pe.matmul(out, lhs_lo(kc), rhs_hi(kc)[:, cs], start=False, stop=(kc == nk - 1))
                return i
            pe.wait_ge(S("o_lo"), 9)
            for d in range(KC):
                pe.wait_ge(S("wo_split"), d + 1)
                if d >= 2:
                    pe.wait_ge(S("x2_add"), d - 1)
                else:
                    pe.wait_ge(S("o_scaled"), 9)
                product(d % 2, lambda kc: wohi[:, d % 2, kc, :], lambda kc: wolo[:, d % 2, kc, :],
                        lambda kc: hhi[:, kc, :], lambda kc: hlo[:, kc, :], KC).then_inc(S("out_pe"), 1)

            def up(k, before=None):
                half, j = k % 2, k // 2
                return product(k % 2, lambda kc: uhi[:, half, kc, j * P:(j + 1) * P],
                               lambda kc: ulo[:, half, kc, j * P:(j + 1) * P],
                               lambda kc: hhi[:, kc, :], lambda kc: hlo[:, kc, :], KC, before)

            def down(d, gp):
                return product(d % 2, lambda f: dhi[:, f, d * P:(d + 1) * P], lambda f: dlo[:, f, d * P:(d + 1) * P],
                               lambda f: ahi[:, gp, f, :], lambda f: alo[:, gp, f, :], 2)
            for k in range(4):
                pe.wait_ge(S("f_split"), 4)
                if k == 0:
                    pe.wait_ge(S("x2_add"), 7)
                elif k == 1:
                    pe.wait_ge(S("x2_add"), 8)
                    pe.wait_ge(S("sacc"), KC)
                    for ch in range(3):
                        m = pe.matmul(ps[:, 3 + ch, 0:CH], ones, sacc[:, ch * CH:(ch + 1) * CH], start=True, stop=True)
                    m.then_inc(S("ms_pe"), 1)
                    pe.wait_ge(S("ms_cp"), 1)
                else:
                    pe.wait_ge(S("f_free"), k - 1)
                up(k, (lambda kc: pe.wait_ge(S("h2_split"), kc + 1)) if k == 0 else None).then_inc(S("f_pe"), 1)
            T_ = LoopTargets(pe, {"f_split": (12, 16), "f_free": (24, 26), "a_split": (4, 4)})
            with pe.Fori(0, (NGRP - 1) // 2):
                for par in range(2):
                    for k in range(4):
                        if k < 2:
                            T_.wait("f_split", 6 * par + 6 + 2 * k)
                        T_.wait("f_free", 12 * par + 3 + k)
                        up(k).then_inc(S("f_pe"), 1)
                    T_.wait("f_split", 6 * par + 10)
                    T_.wait("a_split", 2 * par + 2)
                    for d in range(KC):
                        T_.wait("f_free", 12 * par + 7 + d)
                        down(d, par).then_inc(S("f_pe"), 1)
                T_.end()
            pe.wait_ge(S("f_split"), 6 * NGRP)
            pe.wait_ge(S("a_split"), 2 * NGRP)
            for d in range(KC):
                pe.wait_ge(S("f_free"), 4 + 12 * (NGRP - 1) + d - 1)
                down(d, 0).then_inc(S("f_pe"), 1)

        def ffn_waits(e, last, G, T_, par):
            def w(name, base, per):
                if G == 0:
                    e.wait_ge(S(name), base - min(per, 4))
                elif T_ is None:
                    e.wait_ge(S(name), base + per * (G - 1))
                else:
                    T_.wait(name, base + per * par)
            return w

        @block.scalar
        def _(act):
            def split_hi(q):
                b = q // KC
                act.wait_ge(S(f"w_ld{q % 4}"), 16 * (q // 4 + 1))
                if q >= NW:
                    act.wait_ge(S("w_used"), q - NW + 1)
                elif q == 8:
                    act.wait_ge(S("rdram"), 32)
                    act.wait_ge(S("rtab"), 3)
                act.activation(whi[:, q % NW, 0:WID[b]], wst[:, q % 4, 0:WID[b]], ACT.Copy).then_inc(S("w_hi"), 1)

            def x_hi(i):
                act.wait_ge(xsem(i), xtotal(i))
                if i < 16:
                    c = slice((i // 8) * 516, (i // 8) * 516 + 516)
                    w, kc, s = 516, i % 8, 0
                else:
                    c, w, kc, s = slice(0, NMEM), NMEM, i - 16, 1
                    act.wait_ge(S("z_done"), UI[(4, 1)] + 1)
                act.activation(hhi[:, kc, c], xslot(i)[:, 0:w], ACT.Copy, scale=gain[:, s, kc:kc + 1])\
                    .then_inc(S("x_hi"), 1)

            act.wait_ge(S("const_ld"), 96)
            for kc in range(KC):
                x_hi(kc)
                split_hi(kc)
                if kc == 3:
                    for i in range(2):
                        act.wait_ge(S("lft_pe"), 4 * (i + 1))
                        act.activation(lft[:, i].rearrange("p h c -> p (h c)"), ps[:, 4 + i, :], ACT.Copy)\
                            .then_inc(S("lft_cp"), 1)
            for i in range(8, 16):
                x_hi(i)
            act.wait_ge(S("dve_set"), 1)
            for x in range(11):
                n = NSAMP if x == 0 else P
                act.wait_ge(S(f"xrow_ld{x % 3}"), 16 * (x // 3 + 1))
                if x >= 1:
                    act.wait_ge(S("x_stat"), x)
                act.activation(biasA[0:n].rearrange("p b g h -> p (b g h)"), xrow(x, n),
                               ACT.Square, accum_out=ssx[0:n, x:x + 1]).then_inc(S("x_stat"), 1)
            act.wait_ge(S("x_stat"), 11)
            for i in range(2):
                act.wait_ge(S("lft_pe"), 8 + i + 1)
                for b4 in range(4):
                    v = ps[:, 4 + i, :].rearrange("p (h b g) -> p b g h", h=NH, b=4)[:, b4]
                    m = act.activation(biasA[:, 4 * i + b4], v, ACT.Copy)
                m.then_inc(S("lft_cp"), 1)
            act.wait_ge(S("lsuf"), 1)
            act.wait_ge(S("rs_row"), 1)
            for u, k in enumerate(units):
                b, tt = k
                for bb, kc in CT[u]:
                    split_hi(bb * KC + kc)
                if b == 4 and tt != "S" and tt >= 2 and tt < 6:
                    for i in (2 * (tt - 2), 2 * (tt - 2) + 1):
                        x_hi(16 + i)
                r = rows(k)
                rx = rsx[0:r, xi(k):xi(k) + 1]
                z = zview(k)
                act.wait_ge(S("z_done"), u + 1)
                dst = zdst(k)
                if b in COPY or b == 2:
                    if tt != "S":
                        wait_zo_free(act, k)
                    elif b == 1:
                        act.wait_ge(S("zs_norm"), 1)
                if b in COPY:
                    c0, w = COPY[b]
                    if b == 1 and tt == "S":
                        w = 260
                    m = act.activation(dst[:, c0:c0 + w], z[:, c0:c0 + w], ACT.Copy, scale=rx)
                if b == 2:
                    m = act.activation(dst[:, 0:512], z[:, :], ACT.Gelu_apprx_tanh, scale=rx)
                if b in NORM:
                    c0, nh, _g = NORM[b]
                    if NI[k] >= 2:
                        act.wait_ge(S("ss_dve"), NI[k] - 1)
                    m = act.activation(sq[0:r, NI[k] % 2, 0:nh * HD], z[:, c0:c0 + nh * HD], ACT.Square, scale=rx)
                m.then_inc(S("act_z"), 1)
                if k in kgran and 4 <= kgran[k] + 3 < NKP:
                    n_ = kgran[k] + 3
                    act.wait_ge(S("k_used"), n_ - 3)
                    load_pages(act, kpool, n_ // 8, n_ % 8, n_ % 4, (2, 3))
                if k == (1, NT - 1):
                    act.wait_ge(S("forget"), 1)
                    act.activation(fb[:, :], fb[:, :], ACT.Exp).then_inc(S("fb_act"), 1)
                    act.wait_ge(S("fb_act"), 1)
                    act.activation(fb[:, :], fb[:, :], ACT.Ln, bias=1.0).then_inc(S("fb_act"), 1)
                if k == (2, 2):
                    act.wait_ge(S("csum_pe"), 2)
                    act.activation(crow[:, 0, :], ps[0:32, 7, 64:64 + P], ACT.Copy).then_inc(S("crow"), 1)
                    act.activation(crow[:, 2, :], ones[0:32, :], ACT.Copy, scale=0.0).then_inc(S("crow"), 1)

            def heads_pass(A, T_):
                n, two = A["n"], A["bias"]

                def hi(h, piece):
                    T_.wait(n + "_prep", prep_no(A, h, piece))
                    i, w = int(piece[1]), 512 if two or piece[0] == "q" else NMEM
                    last = "k1" if two else "q1"
                    if piece == last:
                        T_.wait(f"v_ld{h % 2}", A["v0"] + A["vld"] * (h // 2 + 1))
                    if two and piece == last:
                        act.activation(klc[HD:HD + 2, h % 2, :], crs[HD:HD + 2, h % 2, :], ACT.Copy)
                    c = slice(i * 512, i * 512 + w)
                    if piece[0] == "q":
                        m = act.activation(qhl[:, h % 2, c], ps[:, 1, 0:w], ACT.Copy)
                        if two:
                            m = act.activation(q1c[0:HD, h % 2, c], ps[0:HD, 1, 0:w], ACT.Copy)
                    else:
                        m = act.activation(khh[:, h % 2, c], ps[:, 3, 0:w], ACT.Copy)
                    m.then_inc(S(n + "_hi"), 1)

                def ex(g):
                    W = P * A["blocks"][g % NT]
                    T_.wait(n + "_nm", g + 1)
                    if not two:
                        T_.wait(n + "_tpa", g + 1)
                    src = lg[:, g % 2, 0:W] if two else SBANK(g % 2)[:, 0:W]
                    act.activation(lg[:, g % 2, 0:W], src, ACT.Exp, bias=nm[:, g % 2, 1:2]).then_inc(S(n + "_exp"), 1)

                def eva(g):
                    nb = min(4, A["blocks"][g % NT])
                    T_.wait(n + "_tpa", g + 3)
                    T_.wait(n + "_pv", g + 1)
                    act.activation(pts[:, g % 2, 0:nb, :].rearrange("p b c -> p (b c)"), ps[:, 4, 0:nb * P],
                                   ACT.Copy).then_inc(S(n + "_eva"), 1)
                for s in PREP_AT:
                    if PREP_AT[s] != "k1" or two:
                        hi(0, PREP_AT[s])
                for g in range(STEPS + 2):
                    if g >= 2:
                        eva(g - 2)
                    h, s = divmod(g, NT)
                    piece = PREP_AT.get(s) if h + 1 < NH else None
                    if piece and (piece != "k1" or two):
                        hi(h + 1, piece)
                    if g < STEPS:
                        ex(g)

            def seed(A):
                act.sem_inc(S(A["n"] + "_eva"), 1)
                if not A["bias"]:
                    act.sem_inc(S(A["n"] + "_exp"), 2)
            act.wait_ge(S("zo_dve"), len(norm_units))
            act.wait_ge(S("z_done"), NU)
            act.activation(q1c[HD:HD + 2, :, :], ones[HD:HD + 2, 0:1].unsqueeze(2).broadcast_to([2, 2, SEQ]), ACT.Copy)\
                .then_inc(S("q_ones"), 1)
            seed(AC)
            T_ = LoopTargets(act, {"v_ld0": (96, 96), "v_ld1": (96, 96), "ac_prep": (16, 16), "ac_nm": (32, 32), "ac_tpa": (32, 34), "ac_pv": (32, 32)})
            with act.Fori(0, 2):
                heads_pass(AC, T_)
                T_.end()
            seed(MM)
            heads_pass(MM, PassTargets(act))
            act.wait_ge(S("sub"), 1)
            act.activation(sA[:, :, :, :].rearrange("p b g h -> p (b g h)"), sA[:, :, :, :].rearrange("p b g h -> p (b g h)"),
                           ACT.Exp).then_inc(S("e_act"), 1)
            act.wait_ge(S("e_act"), 1)
            act.wait_ge(S("ob_ld"), 16)
            act.wait_ge(S("mm_o"), 2 + 32)
            act.wait_ge(S("dve_set"), 7)
            act.sem_inc(S("o_sq"), 4)

            def v_step(b, j, T_):
                T_.wait("v_used", j + 1)
                bs_ = bass.ds(b, 1) if not isinstance(b, int) else slice(b, b + 1)
                act.activation(est[:, j, :], sA[:, bs_, 4 * j:4 * j + 4, :].rearrange("p o g h -> p (o g h)"),
                               ACT.Copy).then_inc(S("est"), 1)
                if not (isinstance(b, int) and j < 4):
                    v_pages(act, "act", b, j)
                if j % 2 == 1:
                    g = j // 2
                    T_.wait("o_sq", g + 1)
                    col = bass.ds(b * 4 + g, 1) if not isinstance(b, int) else slice(4 * b + g, 4 * b + g + 1)
                    act.activation(osq[:, 0, g * WG:(g + 1) * WG],
                                   oN[:, bs_, g * WG:(g + 1) * WG].rearrange("p o c -> p (o c)"),
                                   ACT.Square, accum_out=sso[:, col]).then_inc(S("o_sq"), 1)
            T_ = PassTargets(act)
            for j in range(8):
                v_step(0, j, T_)
            T_ = LoopTargets(act, {"v_used": (8, 16), "o_sq": (4, 8)})
            for name in ("v_used", "o_sq"):
                T_.base[name] = 8 if name == "v_used" else 4
            with act.Fori(1, NSAMP) as b:
                for j in range(8):
                    v_step(b, j, T_)
                T_.end()
            for g, s_ in ((1, sC), (2, sM)):
                act.wait_ge(S("sub"), 2 * g + 1)
                v = s_[:, :, :, :].rearrange("p c b h -> p (c b h)")
                act.activation(v, v, ACT.Exp).then_inc(S("e_act"), 1)
            for g in range(2):
                act.wait_ge(S("sub"), 2 * g + 2)
                act.activation(small[0:8, g, 136:140], small[0:8, g, 136:140], ACT.Exp).then_inc(S("e_act"), 1)

            def w_out_hi(d):
                act.wait_ge(S("wo_gain"), d + 1)
                if d >= 2:
                    act.wait_ge(S("out_pe"), d - 1)
                act.activation(wohi[:, d % 2], wost[:, d % 2], ACT.Copy).then_inc(S("wo_hi"), 1)
            act.wait_ge(S("v_used"), 8 + NKA)
            w_out_hi(0)
            w_out_hi(1)
            for x, tt in enumerate(list(range(NT)) + ["S"]):
                r = NSAMP if tt == "S" else P
                c0 = 0 if tt == "S" else NSAMP + tt * P
                if tt == "S":
                    act.wait_ge(S("oS"), 4)
                    for g in range(4):
                        act.wait_ge(S("o_sq"), 4 + 32 + g)
                        act.activation(osq[0:8, 1, g * WG:(g + 1) * WG], oS[:, g, :], ACT.Square,
                                       accum_out=sso[0:8, 32 + g:33 + g]).then_inc(S("o_sq"), 1)
                if x == 0:
                    act.wait_ge(S("acc_ld"), 16)
                act.wait_ge(S("ot_pe"), x + 1)
                act.activation(hhi[:, :, c0:c0 + r], SBANK(x % 2)[:, 0:KC * r].rearrange("p (k c) -> p k c", k=KC),
                               ACT.Copy).then_inc(S("o_hi"), 1)
            def up_hi(i, src):
                half, q4 = i // 2, i % 2
                act.activation(uhi[:, half, 4 * q4:4 * q4 + 4, :].rearrange("p k c -> p (k c)"), src, ACT.Copy)\
                    .then_inc(S("f_hi"), 1)

            def square_x2(d):
                act.wait_ge(S("x2_add"), d + 1)
                if d >= 1:
                    act.wait_ge(S("sacc"), d)
                act.activation(sqx[:, :], x2[:, d, :], ACT.Square).then_inc(S("sqx"), 1)
            for d in range(1, KC):
                if d >= 2:
                    w_out_hi(d)
                square_x2(d - 1)
                if d >= 4:
                    act.wait_ge(S("f0_ld"), 64)
                    up_hi(d - 4, fst0[:, d - 4])
            act.wait_ge(S("out_pe"), KC)
            for kc in range(KC):
                if kc == KC - 1:
                    act.wait_ge(S("x2_add"), KC)
                act.activation(hhi[:, kc, :], x2[:, kc, :], ACT.Copy, scale=gain[:, 3, kc:kc + 1]).then_inc(S("h2_hi"), 1)
            square_x2(KC - 1)
            act.wait_ge(S("h2_split"), KC)
            act.wait_ge(S("sacc"), KC)
            act.wait_ge(S("ms_pe"), 1)
            act.activation(c3(rstd_bc[:, :]), U3(1), ACT.Sqrt, scale=1.0 / DM, bias=epsc[:, 0:1]).then_inc(S("ms_cp"), 1)

            def chain_affine(w, k, ft):
                cb = convA if k % 2 == 0 else convG
                w("f_free", 4 + k + 1, 12)
                act.activation(cb[:, NSAMP:COLS], uu[:, NSAMP:COLS], ACT.Identity, scale=conv[:, 2, ft],
                               bias=conv[:, 3, ft]).then_inc(S("aff"), 1)

            def chain_silu(w, j):
                w("tap2", 4 + 2 * j + 2, 4)
                act.activation(convG[:, :], convG[:, :], ACT.Silu).then_inc(S("silu"), 1)

            def chain_hi(w, j, gp, first=False):
                w("cmul", 2 + j + 1, 2)
                if not first:
                    w("f_pe", 4, 12)
                act.activation(ahi[:, gp, j, :], convA[:, :], ACT.Copy).then_inc(S("a_hi"), 1)

            def fts(G, half, j):
                if isinstance(G, int):
                    return slice(half * FT + 2 * G + j, half * FT + 2 * G + j + 1)
                return bass.ds(G * 2 + (half * FT + j), 1)

            def group(w, G, gp, downs, ups):
                first = G == 0 if isinstance(G, int) else False
                for k in range(4):
                    if downs and k < 2:
                        w(f"f_ld{k}", 16 * 3, 48)
                        w("f_pe", 4, 12)
                        act.activation(dhi[:, k, :], fst[:, k], ACT.Copy).then_inc(S("f_hi"), 1)
                    if k == 2:
                        chain_silu(w, 0)
                        chain_hi(w, 0, gp, first)
                    chain_affine(w, k, fts(G, k % 2, k // 2))
                    if first and k >= 2:
                        for i in (2 * k - 4, 2 * k - 3):
                            act.wait_ge(S(f"f_ld{i % 2}"), 16 * (1 + i // 2))
                            act.wait_ge(S("f_pe"), k + 1)
                            up_hi(i, fst[:, i % 2])
                chain_silu(w, 1)
                chain_hi(w, 1, gp, first)
                if ups:
                    for i in range(4):
                        w(f"f_ld{i % 2}", 16 * (4 + i // 2), 48)
                        w("f_pe", 7 + i // 2, 12)
                        up_hi(i, fst[:, i % 2])
            w0 = ffn_waits(act, None, 0, None, 0)
            group(w0, 0, 0, False, False)
            T_ = LoopTargets(act, {"f_ld0": (96, 48 + 80), "f_ld1": (96, 48 + 80), "f_pe": (24, 20), "f_free": (24, 20),
                                   "tap2": (8, 12), "cmul": (4, 6)})
            with act.Fori(1, NGRP - 2, 2) as G:
                for par in range(2):
                    group(ffn_waits(act, None, None, T_, par), G + par, 1 - par, True, True)
                T_.end()
            group(ffn_waits(act, None, NGRP - 2, None, 0), NGRP - 2, 1, True, True)
            wl = ffn_waits(act, None, NGRP - 1, None, 0)
            group(wl, NGRP - 1, 0, True, False)
            i = NGRP - 1
            for k in range(2):
                act.wait_ge(S(f"f_ld{k}"), 16 * (3 + 3 * (NGRP - 2) + 1))
                act.wait_ge(S("f_pe"), 4 + 12 * (NGRP - 1))
                act.activation(dhi[:, k, :], fst[:, k], ACT.Copy).then_inc(S("f_hi"), 1)

        @block.vector
        def _(dve):
            chain = [0]

            def link(ins):
                chain[0] += 1
                ins.then_inc(S("dve_chain"), 1)
                dve.wait_ge(S("dve_chain"), chain[0])
            dve.memset(ssx[:, :], 1.0).then_inc(S("dve_set"), 1)
            dve.memset(fa[:, :], 0.0).then_inc(S("dve_set"), 1)
            dve.memset(epsc[:, :], EPS).then_inc(S("dve_set"), 1)
            dve.memset(lmask[:, :], 1.0).then_inc(S("dve_set"), 1)
            dve.wait_ge(S("dve_set"), 4)
            dve.memset(lmask[:, ::PAGES], 0.0).then_inc(S("dve_set"), 1)
            dve.wait_ge(S("const_ld"), 96)
            for s in (0, 2, 4):
                link(dve.tensor_scalar(gq[:, s, :], gq[:, s, :], QSCALE, None, ALU.mult))
            dve.wait_ge(S("tab_ld"), 48)
            for j in range(3):
                w = min(512, NR - 512 * j)
                dve.wait_ge(S("rt_pe"), j + 1)
                dve.tensor_tensor(rtab[:, 512 * j:512 * j + w], ps[0:NH, j, 0:w], clm[:, 512 * j:512 * j + w], ALU.add)\
                    .then_inc(S("rtab"), 1)
            dve.wait_ge(S("rt_pe"), 6)
            for c in range(3):
                n = CROWS[c]
                m = dve.tensor_scalar(bsamp[0:n, c, :], ps[0:n, 3, NH * c:NH * c + NH], cv("lm")[0:n, c:c + 1], None,
                                      ALU.add)
            m.then_inc(S("rtab"), 1)
            def split_lo(q):
                dve.wait_ge(S("w_hi"), q + 1)
                dve.tensor_tensor(wlo[:, q % NW, 0:WID[q // KC]], wst[:, q % 4, 0:WID[q // KC]],
                                  whi[:, q % NW, 0:WID[q // KC]].bitcast(f32), ALU.subtract).then_inc(S("w_split"), 1)

            def x_lo(i):
                dve.wait_ge(S("x_hi"), i + 1)
                if i < 16:
                    c, w, kc, s = slice((i // 8) * 516, (i // 8) * 516 + 516), 516, i % 8, 0
                else:
                    c, w, kc, s = slice(0, NMEM), NMEM, i - 16, 1
                dve.scalar_tensor_tensor(out=hlo[:, kc, c], in0=xslot(i)[:, 0:w], scalar=gain[:, s, kc:kc + 1],
                                         in1=hhi[:, kc, c].bitcast(f32), op0=ALU.mult, op1=ALU.subtract)\
                    .then_inc(S("x_split"), 1)
            for kc in range(KC):
                x_lo(kc)
                split_lo(kc)
            dve.wait_ge(S("lft_cp"), 2)
            dve.wait_ge(S("dve_set"), 5)
            flat = lft[:, :, :, :].rearrange("p i h c -> p (i h c)")
            link(dve.tensor_tensor_scan(lscan[:, :], lmask[:, :], flat, 0.0, ALU.mult, ALU.add))
            sc = lscan[:, :].rearrange("p (s g) -> p s g", g=PAGES)
            dve.tensor_tensor(lmask[:, :].rearrange("p (s g) -> p s g", g=PAGES),
                              sc[:, :, PAGES - 1:PAGES].broadcast_to([P, 2 * NH * P // PAGES, PAGES]), sc, ALU.subtract)\
                .then_inc(S("lsuf"), 1)
            for i in range(8, 16):
                x_lo(i)
            dve.wait_ge(S("lft_pe"), 10)

            def k_dot(n, b, pg, slot, q, kwait, selfwait):
                kv = ring[:, slot]
                kwait()
                dve.tensor_tensor(kv, kv, q.broadcast_to([P, 4, WG]), ALU.mult).then_inc(S("k_mul"), 1)
                selfwait()
                out = sA[:, b, 4 * pg:4 * pg + 4, :]
                dve.tensor_reduce(out=out, in_=kv.rearrange("p g (h e) -> p (g h) e", e=HD), axis=AX.X, op=ALU.add)\
                    .then_inc(S("k_used"), 1)

            def reduce_sq(k):
                c0, nh, g0 = NORM[k[0]]
                r, i = rows(k), NI[k]
                dve.wait_ge(S("act_z"), UI[k] + 1)
                if i >= 2:
                    dve.wait_ge(S("rs_norm"), i - 1)
                dve.tensor_reduce(out=ssn[0:r, i % 2, 0:nh], in_=sq[0:r, i % 2, 0:nh * HD].rearrange("p (h e) -> p h e", e=HD),
                                  axis=AX.X, op=ALU.add).then_inc(S("ss_dve"), 1)

            def finish_norm(k):
                c0, nh, g0 = NORM[k[0]]
                r, i = rows(k), NI[k]
                dst = zdst(k)[:, c0:c0 + nh * HD]
                dve.wait_ge(S("rs_norm"), i + 1)
                if i >= 1:
                    dve.wait_ge(S("zo_dve"), i)
                z = zview(k)[:, c0:c0 + nh * HD].rearrange("p (h e) -> p h e", e=HD)
                zt = zn[0:r, i % 2, 0:nh * HD].rearrange("p (h e) -> p h e", e=HD)
                dve.scalar_tensor_tensor(out=zt, in0=z, scalar=rsx[0:r, xi(k):xi(k) + 1],
                                         in1=rsn[0:r, i % 2, 0:nh].unsqueeze(2).broadcast_to([r, nh, HD]),
                                         op0=ALU.mult, op1=ALU.mult).then_inc(S("dve_z"), 1)
                if k[1] != "S":
                    wait_zo_free(dve, k)
                dve.wait_ge(S("dve_z"), DI[k] + 1)
                for a in range(nh // NH):
                    w = slice(a * WG, (a + 1) * WG)
                    m = dve.tensor_tensor(dst[:, w].rearrange("p (h e) -> p h e", e=HD),
                                          zn[0:r, i % 2, w].rearrange("p (h e) -> p h e", e=HD),
                                          gq[0:r, g0 + a:g0 + a + 1, :].broadcast_to([r, NH, HD]), ALU.mult)
                m.then_inc(S("zo_dve"), 1)
                if k[1] == "S":
                    dve.wait_ge(S("zo_dve"), i + 1)
                    dve.sem_inc(S("zs_norm"), 1)

            def forget(k):
                r = rows(k)
                dve.wait_ge(S("act_z"), UI[k] + 1)
                if k[1] == "S":
                    out = fa[0:r, 32:36]
                    dve.wait_ge(S("dve_set"), 2)
                else:
                    out = fa[:, 0:32].rearrange("p (h t) -> p t h", t=NT)[:, k[1]]
                dve.scalar_tensor_tensor(out=out, in0=zview(k)[:, WG:WG + NH], scalar=rsx[0:r, xi(k):xi(k) + 1],
                                         in1=pv("bf", r), op0=ALU.mult, op1=ALU.add).then_inc(S("dve_z"), 1)

            def gate(tt):
                k = (2, tt)
                dve.wait_ge(S("sgu_pe"), tt + 1)
                if tt >= 2:
                    dve.wait_ge(S(f"ob_out{tt % 2}"), 16 * (tt // 2))
                for g in range(NH):
                    c = slice(g * HD, (g + 1) * HD)
                    m = dve.scalar_tensor_tensor(out=ob[:, tt % 2, c], in0=ps[:, 7, WG + g * HD:WG + (g + 1) * HD],
                                                 scalar=pv("bs")[:, g:g + 1], in1=zo[:, prompt_no[k] % 4, c],
                                                 op0=ALU.add, op1=ALU.mult)
                m.then_inc(S("ob_ready"), 1)

            dve.wait_ge(S("rs_row"), 1)
            dve.wait_ge(S("x_stat"), 11)
            pending = None
            for u, k in enumerate(units):
                b, tt = k
                for bb, kc in CT[u]:
                    split_lo(bb * KC + kc)
                if b == 4 and tt != "S" and tt >= 2 and tt < 6:
                    for i in (2 * (tt - 2), 2 * (tt - 2) + 1):
                        x_lo(16 + i)
                if b in NORM:
                    reduce_sq(k)
                if b == 1:
                    if pending:
                        finish_norm(pending)
                        pending = None
                    forget(k)
                if pending:
                    finish_norm(pending)
                    pending = None
                if b in NORM:
                    pending = k
                if k == (1, NT - 1):
                    dve.wait_ge(S("dve_z"), DI[k] + 1)
                    dve.scalar_tensor_tensor(out=fb[:, :], in0=fa[:, :], scalar=-1.0, in1=fa[:, :], op0=ALU.mult,
                                             op1=ALU.min).then_inc(S("forget"), 1)
                if k == (2, "S"):
                    dve.wait_ge(S("fb_act"), 2)
                    dve.scalar_tensor_tensor(out=lf[:, :], in0=fa[:, :], scalar=0.0, in1=fb[:, :], op0=ALU.min,
                                             op1=ALU.subtract).then_inc(S("forget"), 1)
                    dve.wait_ge(S("forget"), 2)
                    dve.tensor_tensor_scan(npre[:, :], cv("rs"), lf[:, 0:32], 0.0, ALU.mult, ALU.subtract)\
                        .then_inc(S("forget"), 1)
                if k == (2, 1):
                    dve.wait_ge(S("csum_pe"), 1)
                    dve.tensor_copy(fb[:, 0:32], ps[:, 7, 0:32]).then_inc(S("forget"), 1)
                if k == (2, 3):
                    dve.wait_ge(S("crow"), 2)
                    dve.tensor_tensor(crow[:, 1, :], ps[0:32, 7, 64:64 + P], crow[:, 0, :].bitcast(f32), ALU.subtract)\
                        .then_inc(S("crow"), 1)
                if k == (3, 0):
                    for t7 in (6,):
                        gate(t7)
                if b == 2 and tt not in ("S", 0, 1, 2):
                    gate(tt - 3)
                if k == (3, "S"):
                    gate(5)
                if k == (3, 1):
                    gate(7)
                if k in kgran:
                    n = kgran[k]

                    def kw(n=n):
                        dve.wait_ge(S("qb_ld"), 16)
                        dve.wait_ge(S(f"ring_ld{n % 4}"), ring_total(n))
                    k_dot(n, n // 8, n % 8, n % 4, qb[:, n // 8:n // 8 + 1, :], kw, lambda: dve.wait_ge(S("k_mul"), n + 1))
            finish_norm(pending)

            for s_ in range(4):
                uses = [k for k in prompt_no if prompt_no[k] % 4 == s_]
                dve.wait_ge(S(f"zo_out{s_}"), 16 * sum(0 if k[0] == 2 else n_out[k[0]] for k in uses))
            dve.wait_ge(S("ob_out0"), 64)
            dve.wait_ge(S("ob_out1"), 64)
            dve.wait_ge(S("z_done"), NU)
            dve.memset(vst[:, :, :, HD:HD + 1], 1.0).then_inc(S("dve_set"), 1)

            def heads_pass(A, T_, it, between={}):
                n, two = A["n"], A["bias"]

                def lo(h, piece):
                    T_.wait(n + "_hi", prep_no(A, h, piece))
                    i, w = int(piece[1]), 512 if two or piece[0] == "q" else NMEM
                    c = slice(i * 512, i * 512 + w)
                    if piece[0] == "q":
                        v = qhl[HD:P, h % 2, c]
                        m = dve.tensor_tensor(v, ps[HD:P, 1, 0:w], v.bitcast(f32), ALU.subtract)
                    else:
                        m = dve.tensor_tensor(klc[0:HD, h % 2, c], ps[0:HD, 3, 0:w], khh[0:HD, h % 2, c].bitcast(f32),
                                              ALU.subtract)
                    m.then_inc(S(n + "_lo"), 1)

                def score(g):
                    h, s = divmod(g, NT)
                    W = P * A["blocks"][s]
                    T_.wait(n + "_qk", g + 1)
                    if two:
                        if g >= 2:
                            T_.wait(n + "_tpb", 4 * ((g - 2) // NT) + min((g - 2) % NT + 1, 4) + 1)
                        T_.wait(n + "_tpa", g + 1)
                        dve.tensor_tensor_reduce(out=lg[:, g % 2, 0:W], in0=SBANK(g % 2)[:, 0:W],
                                                 in1=toe[:, h % 2, SEQ - W:SEQ], scale=1.0, scalar=-3.0e38,
                                                 op0=ALU.add, op1=ALU.max, accum_out=nm[:, g % 2, 0:1])\
                            .then_inc(S(n + "_lg"), 1)
                        T_.wait(n + "_lg", g + 3)
                        dve.tensor_scalar(nm[:, g % 2, 1:2], nm[:, g % 2, 0:1], -1.0, None, ALU.mult)\
                            .then_inc(S(n + "_nm"), 1)
                    else:
                        T_.wait(n + "_exp", g + 1)
                        dve.tensor_reduce(out=nm[:, g % 2, 1:2], in_=SBANK(g % 2)[:, 0:W], axis=AX.X,
                                          op=ALU.max, negate=True).then_inc(S(n + "_nm"), 1)

                def evb(g):
                    h, s = divmod(g, NT)
                    nb = A["blocks"][s]
                    if nb > 4:
                        T_.wait(n + "_tpb", 4 * h + s + 2)
                        T_.wait(n + "_pv", g + 1)
                        dve.tensor_copy(pts[:, g % 2, 4:nb, :].rearrange("p b c -> p (b c)"),
                                        ps[:, 5, 0:(nb - 4) * P]).then_inc(S(n + "_evb"), 1)

                def out(g):
                    h, s = divmod(g, NT)
                    T_.wait(n + "_pv", g + 3)
                    dve.reciprocal(rc[:, g % 2:g % 2 + 1], ps[:, 6 + g % 2, HD:HD + 1]).then_inc(S(n + "_rc"), 1)
                    T_.wait(n + "_rc", g + 1)
                    col = bass.ds(it * WG + h * HD, HD) if two else slice(3 * WG + h * HD, 3 * WG + (h + 1) * HD)
                    dve.tensor_scalar(oN[:, A["tile"][s], col], ps[:, 6 + g % 2, 0:HD], rc[:, g % 2:g % 2 + 1],
                                      None, ALU.mult).then_inc(S(n + "_o"), 1)

                def granule(h, i):
                    j = 4 * h + i
                    seq = bass.ds(it * 2 + (4 + h // 2), 1)
                    k_dot(None, seq, j % 8, j % 4, qb[:, seq, :],
                          lambda: T_.wait(f"ring_ld{j % 4}", RK[j % 4] + 64 * (j // 4 + 1)),
                          lambda: T_.wait("k_mul", NKP + j + 1))
                for s in PREP_AT:
                    if PREP_AT[s] != "k1" or two:
                        lo(0, PREP_AT[s])
                for g in range(STEPS + 3):
                    h, s = divmod(g, NT)
                    if 0 <= g - 2 < STEPS:
                        evb(g - 2)
                    if g < STEPS:
                        score(g)
                    piece = PREP_AT.get(s) if h + 1 < NH else None
                    if piece and (piece != "k1" or two):
                        lo(h + 1, piece)
                    if g >= 3:
                        out(g - 3)
                    if g in between:
                        between[g]()
                    if two and g < STEPS and s % 2 == 1:
                        granule(h, s // 2)

            def seed(A):
                dve.sem_inc(S(A["n"] + "_o"), 2)
                if A["bias"]:
                    dve.sem_inc(S(A["n"] + "_lg"), 2)
                    dve.sem_inc(S(A["n"] + "_evb"), 1)
            RK = [ring_total(NKP - 4 + s4) for s4 in range(4)]
            seed(AC)
            T_ = LoopTargets(dve, {"ac_hi": (16, 16), "ac_qk": (32, 32), "ac_pv": (32, 34), "ac_rc": (32, 32),
                                   "ac_tpa": (32, 32), "ac_tpb": (16, 17), "ac_lg": (32, 34), "k_mul": (16, NKP + 16),
                                   **{f"ring_ld{s4}": (256, RK[s4] + 256) for s4 in range(4)}})
            with dve.Fori(0, 2) as it:
                heads_pass(AC, T_, it)
                T_.end()

            def gview(g):
                if g == 0:
                    return sA[:, :, :, :].rearrange("p b g h -> p b h g")
                return (sC if g == 1 else sM)[:, :, :, :].rearrange("p c b h -> p b h c")

            def maxima(g):
                pm = small[:, g, 0:32].rearrange("p (b h) -> p b h", b=8)
                dve.tensor_reduce(out=pm, in_=gview(g), axis=AX.X, op=ALU.max).then_inc(S("pm"), 1)
                if g < 2:
                    qo, ko = (0, WG) if g == 0 else (BLK[3][0], BLK[3][0] + WG)
                    sn = small[0:8, g, 128:132]
                    dve.wait_ge(S("zs_norm"), 3)
                    link(dve.tensor_tensor(prod8[:, 0, :], zs[:, qo:qo + WG], zs[:, ko:ko + WG], ALU.mult))
                    link(dve.tensor_reduce(out=sn, in_=prod8[:, 0, :].rearrange("p (h e) -> p h e", e=HD), axis=AX.X,
                                           op=ALU.add))
                    if g == 0:
                        link(dve.tensor_tensor(sn, sn, lf[0:8, 32:36], ALU.subtract))
                    else:
                        link(dve.scalar_tensor_tensor(out=sn, in0=pv("rb0", 8), scalar=float(np.float32(math.log(3.0))),
                                                      in1=sn, op0=ALU.add, op1=ALU.add))
                    d = small[0:8, g, 96:128].rearrange("p (b h) -> p b h", b=8)
                    link(dve.tensor_tensor(d, sn.unsqueeze(1).broadcast_to([8, 8, NH]),
                                           cv("dm", 8).rearrange("p (b h) -> p b h", b=8), ALU.add))
                    dve.wait_ge(S("pm"), 2 * g + 1)
                    dve.tensor_tensor(small[0:8, g, 0:32], small[0:8, g, 0:32], small[0:8, g, 96:128], ALU.max)\
                        .then_inc(S("pm"), 1)

            def subtract(g):
                dve.wait_ge(S("gmax"), g + 1)
                m = small[:, g, 64:96]
                if g == 0:
                    mb = m.rearrange("p (b h) -> p b h", b=8)
                    for b in range(8):
                        i = dve.tensor_tensor(sA[:, b], sA[:, b], mb[:, b:b + 1, :].broadcast_to([P, PAGES, NH]), ALU.subtract)
                    i.then_inc(S("sub"), 1)
                else:
                    s_ = sC if g == 1 else sM
                    nc_ = 3 if g == 1 else 2
                    v = s_[:, :, :, :].rearrange("p c b h -> p c (b h)")
                    dve.tensor_tensor(v, v, m.unsqueeze(1).broadcast_to([P, nc_, 32]), ALU.subtract)\
                        .then_inc(S("sub"), 1)
                if g < 2:
                    t3 = small[0:8, g, 96:128]
                    dve.wait_ge(S("pm"), 2 * g + 2)
                    link(dve.tensor_tensor(t3, small[0:8, g, 64:96], cv("e8", 8), ALU.mult))
                    link(dve.tensor_reduce(out=small[0:8, g, 132:136], in_=t3.rearrange("p (b h) -> p h b", b=8), axis=AX.X,
                                           op=ALU.add))
                    dve.tensor_tensor(small[0:8, g, 136:140], small[0:8, g, 128:132], small[0:8, g, 132:136], ALU.subtract)\
                        .then_inc(S("sub"), 1)

            def key_sums(g):
                dve.wait_ge(S("e_act"), g + 1)
                dve.tensor_reduce(out=small[:, g, 32:64].rearrange("p (b h) -> p b h", b=8), in_=gview(g), axis=AX.X,
                                  op=ALU.add).then_inc(S("esum"), 1)

            def forget_bias():
                flat_ = "p b g h -> p (b g h)"
                dve.wait_ge(S("k_used"), NKA)
                dve.wait_ge(S("lft_cp"), 4)
                link(dve.tensor_tensor(sA[:, :, :, :].rearrange(flat_), sA[:, :, :, :].rearrange(flat_),
                                       biasA[:, :, :, :].rearrange(flat_), ALU.add))
            seed(MM)
            heads_pass(MM, PassTargets(dve), None, {4: forget_bias, 10: lambda: maxima(0), 18: lambda: subtract(0)})
            def cm_dot(i):
                g, c, b0 = cm[i]
                nk = CROWS[c] if g == DIL else P
                kv, q = cmk[0:nk, i], qb if g == DIL else qb2
                dve.wait_ge(S("qb_ld") if g == DIL else S("qb2_ld"), 32 if g == DIL else 16)
                dve.wait_ge(S("cmk_ld"), 16 * NCM)
                link(dve.tensor_tensor(kv, kv, q[0:nk, b0:b0 + 4, :], ALU.mult))
                dst = (sC if g == DIL else sM)[0:nk, c, b0:b0 + 4, :]
                link(dve.tensor_reduce(out=dst, in_=kv.rearrange("p b (h e) -> p (b h) e", e=HD), axis=AX.X, op=ALU.add))

            def w_out(d):
                dve.wait_ge(S(f"wo_ld{d % 2}"), 16 * (d // 2 + 1))
                g = gain[:, 2, :].unsqueeze(2).broadcast_to([P, KC, P])
                dve.tensor_tensor(wost[:, d % 2], wost[:, d % 2], g, ALU.mult).then_inc(S("wo_gain"), 1)

            def w_out_lo(d):
                dve.wait_ge(S("wo_hi"), d + 1)
                dve.tensor_tensor(wolo[:, d % 2], wost[:, d % 2], wohi[:, d % 2].bitcast(f32), ALU.subtract)\
                    .then_inc(S("wo_split"), 1)

            def scale_out(tt):
                dve.wait_ge(S("rs_row"), 2)
                v = oN[:, tt, :].rearrange("p (g c) -> p g c", g=4)
                dve.tensor_tensor(v, v, rso[:, 4 * tt:4 * tt + 4].unsqueeze(2).broadcast_to([P, 4, WG]), ALU.mult)\
                    .then_inc(S("o_scaled"), 1)
            dve.wait_ge(S("mm_pv"), 2 + 32)
            dve.memset(sso[:, :], 1.0).then_inc(S("dve_set"), 1)
            dve.memset(sC[:, :, :, :], NEG).then_inc(S("dve_set"), 1)
            dve.wait_ge(S("dve_set"), 8)
            dve.sem_inc(S("acc_cp"), 1)
            for b in range(NSAMP):
                if b < 5:
                    cm_dot(2 * b)
                    cm_dot(2 * b + 1)
                elif b == 5:
                    for c in range(3):
                        nk = CROWS[c]
                        m = dve.tensor_tensor(sC[0:nk, c], sC[0:nk, c], bsamp[0:nk, c:c + 1, :].broadcast_to([nk, 8, NH]),
                                              ALU.add)
                    link(m)
                    maxima(1)
                    maxima(2)
                elif b == 6:
                    subtract(1)
                    subtract(2)
                    key_sums(0)
                else:
                    w_out(0)
                    w_out(1)
                dve.wait_ge(S("v_used"), 8 + 8 * (b + 1))
                dve.tensor_copy(mkd[:, 0, b, :], ps[0:NH, 0, 0:WG]).then_inc(S("acc_cp"), 1)
            for i, (grp, done) in enumerate(((1, 3), (1, 6), (2, 8), (2, 10))):
                dve.wait_ge(S("v_used"), 8 + NKA + done)
                dve.tensor_copy(mkd[:, grp, 4 * (i % 2):4 * (i % 2) + 4, :],
                                ps[0:NH, 4 * (i % 2):4 * (i % 2) + 4, 0:WG]).then_inc(S("acc2_cp"), 1)
                if i == 0:
                    key_sums(1)
                    key_sums(2)
                else:
                    if i < 3:
                        w_out_lo(i - 1)
                    scale_out(i - 1)
            for tt in range(3, NT):
                scale_out(tt)
            u_, v_ = zs[:, BLK[2][0]:BLK[2][0] + WG], zs[:, BLK[2][0] + WG:BLK[2][0] + 2 * WG]

            def by_head(ap):
                return ap.rearrange("p (h e) -> p h e", e=HD)

            def bc(ap):
                return ap.unsqueeze(2).broadcast_to([8, NH, HD])
            def sample_out():
                link(dve.tensor_tensor(by_head(prod8[:, 1, :]), by_head(v_), bc(pv("w00", 8)), ALU.mult))
                link(dve.tensor_tensor(by_head(prod8[:, 1, :]), by_head(prod8[:, 1, :]), bc(pv("b0", 8)), ALU.add))
                dve.tensor_tensor(oS[:, 2, :], prod8[:, 1, :], u_, ALU.mult).then_inc(S("oS"), 1)
                dve.wait_ge(S("oS"), 1)
                dve.wait_ge(S("samp_pe"), 1)
                dve.wait_ge(S("acc_ld"), 80)
                for g, pos, vo in ((0, 0, 2 * WG + 0), (1, 1, BLK[4][0]), (2, 3, None)):
                    acc = acc8[:, g].rearrange("p h e -> p (h e)")
                    den = ps[0:8, 6, 8 * g:8 * g + 4]
                    dd, rd = small[0:8, g, 140:144], small[0:8, g, 144:148]
                    if g < 2:
                        dve.wait_ge(S("e_act"), 3 + g + 1)
                        en = small[0:8, g, 136:140]
                        link(dve.tensor_tensor(dd, den, en, ALU.add))
                        link(dve.reciprocal(rd, dd))
                        vv = zs[:, 512:768] if g == 0 else zs[:, vo:vo + WG]
                        link(dve.tensor_tensor(by_head(prod8[:, 0, :]), by_head(vv), bc(en), ALU.mult))
                        link(dve.tensor_tensor(prod8[:, 0, :], prod8[:, 0, :], acc, ALU.add))
                        dve.tensor_tensor(by_head(oS[:, pos, :]), by_head(prod8[:, 0, :]), bc(rd), ALU.mult)\
                            .then_inc(S("oS"), 1)
                        dve.wait_ge(S("oS"), g + 2)
                    else:
                        link(dve.reciprocal(rd, den))
                        dve.tensor_tensor(by_head(oS[:, pos, :]), by_head(acc), bc(rd), ALU.mult).then_inc(S("oS"), 1)

            for x, tt in enumerate(list(range(NT)) + ["S"]):
                r = NSAMP if tt == "S" else P
                c0 = 0 if tt == "S" else NSAMP + tt * P
                if tt == "S":
                    dve.wait_ge(S("rs_row"), 3)
                    dve.wait_ge(S("oS"), 4)
                    dve.tensor_tensor(oS[:, :, :], oS[:, :, :], rso[0:8, 32:36].unsqueeze(2).broadcast_to([8, 4, WG]), ALU.mult)\
                        .then_inc(S("o_scaled"), 1)
                    dve.wait_ge(S("o_scaled"), 9)
                if x == 3:
                    sample_out()
                dve.wait_ge(S("o_hi"), x + 1)
                dve.tensor_tensor(hlo[:, :, c0:c0 + r], SBANK(x % 2)[:, 0:KC * r].rearrange("p (k c) -> p k c", k=KC),
                                  hhi[:, :, c0:c0 + r].bitcast(f32), ALU.subtract).then_inc(S("o_lo"), 1)

            def add_x(d):
                dve.wait_ge(S("out_pe"), d + 1)
                dve.wait_ge(S("x2_ld"), 16 * (KC + 1))
                dve.tensor_tensor(c3(x2[:, d, :]), U3(d % 2), c3(x2[:, d, :]), ALU.add).then_inc(S("x2_add"), 1)

            def up_lo(i, src):
                half, q4 = i // 2, i % 2
                v = (slice(None), half, slice(4 * q4, 4 * q4 + 4))
                dve.tensor_tensor(ulo[v].rearrange("p k c -> p (k c)"), src,
                                  uhi[v].rearrange("p k c -> p (k c)").bitcast(f32), ALU.subtract).then_inc(S("f_split"), 1)

            def add_sq(d):
                dve.wait_ge(S("sqx"), d + 1)
                if d == 0:
                    dve.tensor_copy(sacc[:, :], sqx[:, :]).then_inc(S("sacc"), 1)
                else:
                    dve.wait_ge(S("sacc"), d)
                    dve.tensor_tensor(sacc[:, :], sacc[:, :], sqx[:, :], ALU.add).then_inc(S("sacc"), 1)
            for d in range(KC):
                add_x(d)
                if d >= 1:
                    add_sq(d - 1)
                if d + 2 < KC:
                    w_out(d + 2)
                    w_out_lo(d + 2)
                if d >= 4:
                    dve.wait_ge(S("f_hi"), d - 3)
                    up_lo(d - 4, fst0[:, d - 4])
            for kc in range(KC):
                dve.wait_ge(S("h2_hi"), kc + 1)
                dve.scalar_tensor_tensor(out=hlo[:, kc, :], in0=x2[:, kc, :], scalar=gain[:, 3, kc:kc + 1],
                                         in1=hhi[:, kc, :].bitcast(f32), op0=ALU.mult, op1=ALU.subtract)\
                    .then_inc(S("h2_split"), 1)

            add_sq(KC - 1)

            def bt(a):
                return a.unsqueeze(2).broadcast_to([P, 2 * FT, NSAMP])
            tmp = u10[:, :, 10:18]
            dve.wait_ge(S("x2_ld"), 16 * (KC + 1))
            link(dve.tensor_tensor(sbase[:, :, :], stT[:, :, 0, :], bt(conv[:, 0, :]), ALU.mult))
            link(dve.tensor_tensor(tmp, stT[:, :, 1, :], bt(conv[:, 1, :]), ALU.mult))
            link(dve.tensor_tensor(sbase[:, :, :], sbase[:, :, :], tmp, ALU.add))
            link(dve.tensor_tensor(sbase[:, :, :], sbase[:, :, :], bt(conv[:, 3, :]), ALU.add))
            link(dve.tensor_copy(u10[:, :, 10:18], stT[:, :, 1, :]))

            dve.wait_ge(S("ms_cp"), 1)
            link(dve.reciprocal(rstd_bc[:, :], rstd_bc[:, :]))

            def fts(G, half, j):
                if isinstance(G, int):
                    return slice(half * FT + 2 * G + j, half * FT + 2 * G + j + 1)
                return bass.ds(G * 2 + (half * FT + j), 1)

            def unit(w, G, k, ft, between=None):
                cb = convA if k % 2 == 0 else convG
                if k > 0 or not isinstance(G, int) or G > 0:
                    w("tap2", 4 + k, 4)
                w("f_pe", 4 + k + 1, 12)
                dve.tensor_tensor(c3(uu[:, :]), U3(k % 2), c3(rstd_bc[:, :]), ALU.mult).then_inc(S("f_free"), 1)
                w("f_free", 4 + k + 1, 12)
                dve.tensor_copy(u10[:, ft, 0:2], uu[:, COLS - 2:COLS].unsqueeze(1))
                dve.tensor_copy(u10[:, ft, 2:10], uu[:, 0:NSAMP].unsqueeze(1))
                dve.scalar_tensor_tensor(out=cb[:, 0:NSAMP], in0=uu[:, 0:NSAMP], scalar=conv[:, 2, ft],
                                         in1=sbase[:, ft, :].rearrange("p o b -> p (o b)"), op0=ALU.mult, op1=ALU.add)\
                    .then_inc(S("c_samp"), 1)
                w("c_samp", 4 + k + 1, 4)
                dve.memset(uu[:, NSAMP - 2:NSAMP], 0.0).then_inc(S("c_pad"), 1)
                w("c_pad", 4 + k + 1, 4)
                w("aff", 4 + k + 1, 4)
                pc = cb[:, NSAMP:COLS]
                dve.scalar_tensor_tensor(out=pc, in0=uu[:, NSAMP - 1:COLS - 1], scalar=conv[:, 1, ft], in1=pc,
                                         op0=ALU.mult, op1=ALU.add).then_inc(S("tap1"), 1)
                if between:
                    between()
                w("tap1", 4 + k + 1, 4)
                dve.scalar_tensor_tensor(out=pc, in0=uu[:, NSAMP - 2:COLS - 2], scalar=conv[:, 0, ft], in1=pc,
                                         op0=ALU.mult, op1=ALU.add).then_inc(S("tap2"), 1)

            def gated(w, j, gp, between=None):
                w("silu", 2 + j + 1, 2)
                w("tap2", 4 + 2 * j + 2, 4)
                dve.tensor_tensor(convA[:, :], convA[:, :], convG[:, :], ALU.mult).then_inc(S("cmul"), 1)
                if between:
                    between()
                w("a_hi", 2 + j + 1, 2)
                dve.tensor_tensor(alo[:, gp, j, :], convA[:, :], ahi[:, gp, j, :].bitcast(f32), ALU.subtract)\
                    .then_inc(S("a_split"), 1)
                w("a_split", 2 + j + 1, 2)

            def add_down(w, d, G=None):
                w("f_pe", 8 + d + 1, 12)
                dve.tensor_tensor(c3(x2[:, d, :]), U3(d % 2), c3(x2[:, d, :]), ALU.add).then_inc(S("f_free"), 1)

            def group(w, G, gp, downs, ups):
                G0 = isinstance(G, int) and G == 0
                for k in range(4):
                    if downs and k < 2:
                        w("f_hi", 8 + k + 1, 6)
                        dve.tensor_tensor(dlo[:, k, :], fst[:, k], dhi[:, k, :].bitcast(f32), ALU.subtract)\
                            .then_inc(S("f_split"), 1)
                    if k == 2:
                        gated(w, 0, gp)
                    unit(w, G, k, fts(G, k % 2, k // 2), (lambda: add_down(w, 0)) if downs and k == 3 else None)
                    if G0 and k >= 2:
                        for i in (2 * k - 4, 2 * k - 3):
                            dve.wait_ge(S("f_hi"), 4 + i + 1)
                            up_lo(i, fst[:, i % 2])
                if downs:
                    add_down(w, 1)
                gated(w, 1, gp, (lambda: add_down(w, 2)) if downs else None)
                if downs:
                    for d in range(3, KC):
                        add_down(w, d)
                        if ups and d < KC - 1:
                            w("f_hi", 10 + d - 2, 6)
                            up_lo(d - 3, fst[:, (d - 3) % 2])
            w0 = ffn_waits(dve, None, 0, None, 0)
            group(w0, 0, 0, False, False)
            T_ = LoopTargets(dve, {"f_pe": (24, 28), "f_free": (24, 20), "c_samp": (8, 12), "c_pad": (8, 12), "aff": (8, 12),
                                   "tap1": (8, 12), "tap2": (8, 12), "silu": (4, 6), "a_hi": (4, 6), "a_split": (4, 6),
                                   "f_hi": (12, 20)})
            with dve.Fori(1, NGRP - 2, 2) as G:
                for par in range(2):
                    group(ffn_waits(dve, None, None, T_, par), G + par, 1 - par, True, True)
                T_.end()
            group(ffn_waits(dve, None, NGRP - 2, None, 0), NGRP - 2, 1, True, True)
            group(ffn_waits(dve, None, NGRP - 1, None, 0), NGRP - 1, 0, True, False)
            for k in range(2):
                dve.wait_ge(S("f_hi"), 8 + 6 * (NGRP - 2) + 2 + k + 1)
                dve.tensor_tensor(dlo[:, k, :], fst[:, k], dhi[:, k, :].bitcast(f32), ALU.subtract).then_inc(S("f_split"), 1)
            for d in range(KC):
                dve.wait_ge(S("f_pe"), 4 + 12 * (NGRP - 1) + d + 1)
                dve.tensor_tensor(c3(x2[:, d, :]), U3(d % 2), c3(x2[:, d, :]), ALU.add).then_inc(S("f_free"), 1)

        @block.gpsimd
        def _(pool):
            pool.memset(nhalf[:, :], -0.5).then_inc(S("pool_chain"), 1)
            pool.wait_ge(S("const_ld"), 96)
            for i in range(2):
                pool.indirect_dma_start(out=lfp[:, i, :], out_offset=None, in_=lfpool,
                                        in_offset=bass.IndirectOffsetOnAxis(ap=pidx[:, i:i + 1], axis=0))\
                    .then_inc(S("lfp_ld"), 16)
            pool.wait_ge(S("const_ld"), 96)
            pool.affine_select(out=wsT[:, :, :], in_=wsT[:, :, :], compare_op=ALU.is_ge, fill=0.0, base=0,
                               pattern=[[0, NH], [1, P]], channel_multiplier=-1).then_inc(S("ws_mask"), 2)
            chain = [1]

            def inverse_rms(out, src, width, done, value):
                r = src.shape[0]
                n = src.shape[1]
                pool.tensor_scalar(out, src, 1.0 / width, EPS, ALU.mult, ALU.add).then_inc(S("pool_chain"), 1)
                chain[0] += 1
                pool.wait_ge(S("pool_chain"), chain[0])
                pool.tensor_tensor(out, out, nhalf[0:r, 0:n], ALU.pow).then_inc(S(done), 1)
            pool.wait_ge(S("x_stat"), 11)
            inverse_rms(rsx[:, :], ssx[:, :], DM, "rs_row", 1)
            for k in norm_units:
                i, r, nh = NI[k], rows(k), NORM[k[0]][1]
                pool.wait_ge(S("ss_dve"), i + 1)
                if i >= 2:
                    pool.wait_ge(S("zo_dve"), i - 1)
                inverse_rms(rsn[0:r, i % 2, 0:nh], ssn[0:r, i % 2, 0:nh], HD, "rs_norm", i + 1)
            def max_all(g):
                pool.wait_ge(S("pm"), (2, 4, 5)[g])
                pool.partition_all_reduce(small[:, g, 64:96], small[:, g, 0:32], P, RMAX).then_inc(S("gmax"), 1)
            max_all(0)
            pool.wait_ge(S("k_used"), NKA)
            for j in range(8):
                if j == 4:
                    pool.wait_ge(S("mm_pv"), 2 + 32)
                v_pages(pool, "pool", 0, j)
            for first, end_ in ((1, 6), (6, NSAMP)):
                with pool.Fori(first, end_) as b:
                    for j in range(8):
                        pool.wait_ge(S("v_used"), b * 8 + (j + 1))
                        v_pages(pool, "pool", b, j)
                if end_ < NSAMP:
                    max_all(1)
                    max_all(2)
            pool.wait_ge(S("o_sq"), 4 + 32)
            inverse_rms(rso[:, 0:32], sso[:, 0:32], WG, "rs_row", 2)
            pool.wait_ge(S("o_sq"), 4 + 36)
            inverse_rms(rso[0:8, 32:36], sso[0:8, 32:36], WG, "rs_row", 3)


def kernel(x_prompt, x_sample, mem_prompt, cache_a_k, cache_a_v, cache_a_logf, cache_c_k, cache_c_v,
           cache_mem_k, cache_mem_v, state_ffn_conv, page_table, norm_mix, w_in, b_forget, qk_gain,
           w_spatial, b_spatial, rel_bias, norm_mem, w_mem_kv, norm_out, w_out, norm_ffn, w_up,
           conv_w, conv_b, w_down):
    import concourse.bacc as bacc
    from concourse.bass_utils import run_bass_kernel_spmd as run

    a = lambda x: np.asarray(x)
    xp, xs, mem = a(x_prompt)[0], a(x_sample)[:, 0], a(mem_prompt)[0]
    fmaj = lambda x: x.T.reshape(KC, P, -1).transpose(1, 0, 2)
    vec = lambda v: a(v).reshape(-1, P).T
    order = [0, 1, 4, 5, 2, 3, 6, 7]
    state = a(state_ffn_conv)[0].reshape(NSAMP, 2, 2 * FT, P).transpose(3, 2, 1, 0)
    wide = lambda v: np.broadcast_to(a(v).reshape(1, -1), (P, a(v).size))
    cw, cb = a(conv_w)[0], a(conv_b)[0]
    prm = np.concatenate([
        vec(cw[0]), vec(cw[1]), vec(cw[2]), vec(cb),
        vec(norm_mix), vec(norm_mem), vec(norm_out)[:, order], vec(norm_ffn),
        wide(a(qk_gain)[0]), a(b_spatial)[0].T, wide(b_forget),
        wide(a(w_spatial)[0, :, 0, 0]), wide(a(b_spatial)[0, :, 0]), wide(a(rel_bias)[0])], 1)
    wu = a(w_up)[0].reshape(2, 4, P, 2, NGRP, 256)
    arrays = {
        "xT": fmaj(np.concatenate([xs, xp], 0)), "memT": fmaj(mem), "x_prompt": xp, "x_sample": xs, "mem": mem,
        "cache_a_k": a(cache_a_k), "cache_a_v": a(cache_a_v), "cache_a_logf": a(cache_a_logf),
        "cache_c_k": a(cache_c_k), "cache_c_v": a(cache_c_v), "cache_mem_k": a(cache_mem_k), "cache_mem_v": a(cache_mem_v),
        "ptab": a(page_table).reshape(1, -1), "pidx": a(page_table).reshape(2, P).T,
        "prm": prm, "stT": state, "w_in": a(w_in), "w_mem": a(w_mem_kv), "wsT": a(w_spatial)[0].transpose(2, 0, 1),
        "rel_bias": a(rel_bias),
        "w_outL": a(w_out)[0].reshape(KC, P, KC, P)[order].transpose(2, 1, 0, 3),
        "w_upL": wu.transpose(4, 3, 0, 2, 1, 5).reshape(NGRP, 2, 2, P, 4 * 256),
        "w_down": a(w_down)[0].reshape(FT, P, DM),
    }
    arrays.update(host_constants())
    outs = {"o_yT": (P, KC, COLS), "o_ka": (SEQ, WG), "o_va": (SEQ, WG), "o_lf": (P, 36), "o_kc": (SEQ, WG),
            "o_vc": (SEQ, WG), "o_mk": (NMEM, WG), "o_mv": (NMEM, WG), "o_zs": (NSAMP, 2308), "o_u10": (P, 2 * FT, 18)}
    nc = bacc.Bacc("TRN2", target_bir_lowering=False, num_devices=1)
    feed, t = {}, {}
    for name, x in arrays.items():
        x = np.ascontiguousarray(x)
        feed[f"in_{name}"] = x
        t[name] = nc.dram_tensor(f"in_{name}", x.shape, mybir.dt.from_np(x.dtype), kind="ExternalInput").ap()
    for name, shape in outs.items():
        t[name] = nc.dram_tensor(name, shape, mybir.dt.float32, kind="ExternalOutput").ap()
    build(nc, t)
    r = run(nc, [feed], core_ids=[0]).results[0]

    y = r["o_yT"].transpose(2, 1, 0).reshape(COLS, DM)
    zs, lf, u = r["o_zs"], r["o_lf"], r["o_u10"].transpose(2, 1, 0).reshape(18, 2 * DFF)
    heads = lambda x, lead: x.reshape((1,) + lead + (NH, HD))
    return (y[NSAMP:].reshape(1, SEQ, DM), y[:NSAMP].reshape(NSAMP, 1, DM),
            heads(r["o_ka"], (1, SEQ)), heads(r["o_va"], (1, SEQ)),
            lf[:, 0:32].reshape(P, NH, NT).transpose(2, 0, 1).reshape(1, 1, SEQ, NH),
            heads(r["o_kc"], (1, SEQ)), heads(r["o_vc"], (1, SEQ)),
            heads(r["o_mk"], (1, NMEM)), heads(r["o_mv"], (1, NMEM)), u[0:2].reshape(1, 1, 2, 2 * DFF),
            heads(zs[:, 256:512], (NSAMP, 1)), heads(zs[:, 512:768], (NSAMP, 1)), lf[0:8, 32:36].reshape(1, NSAMP, 1, NH),
            heads(zs[:, 1540:1796], (NSAMP, 1)), heads(zs[:, 1796:2052], (NSAMP, 1)),
            zs[:, 1028:1284].reshape(1, NSAMP, 1, WG),
            np.stack([u[10:18], u[2:10]], 1).reshape(1, NSAMP, 2, 2 * DFF))
```
